# Optimizing a Trainium2 kernel written in Bass

```python
import math
import numpy as np
import jax, jax.numpy as jnp
from jax import lax

D_MODEL = 1024
BATCH = 1
SEQ = 512
DEPTH = 2

CHUNK = 64
N_MEM = 256
RMS_EPS = 1e-6
S5_WIDTH = D_MODEL // 2
S5_GROUP = 16
S5_GROUPS = S5_WIDTH // S5_GROUP
S5_STATE = 64
S5_DT_MIN = 0.001
S5_DT_MAX = 0.1
GDN_HEAD_DIM = 128
GDN_WIDTH = D_MODEL // 2
GDN_HEADS = GDN_WIDTH // GDN_HEAD_DIM
GDN_CONV = 4
GDN_DT_MIN = 0.001
GDN_DT_MAX = 0.1
AB_IN = S5_WIDTH + 4 * GDN_WIDTH + 2 * GDN_HEADS
CA_HEADS = 16
CA_HEAD_DIM = D_MODEL // CA_HEADS
CA_LEFT_CHUNKS = 8
CA_BAND = (CA_LEFT_CHUNKS + 1) * CHUNK
MAX_REL_DIST = 128
XA_HEADS = 4
XA_HEAD_DIM = D_MODEL // XA_HEADS
FFN_HIDDEN = -(-8 * D_MODEL // (3 * 256)) * 256
N_EVEN = (DEPTH + 1) // 2
N_ODD = DEPTH // 2

kernel_name = "hybrid_s5_deltanet_chunkattn_encoder"

F32 = jnp.float32

def rms_norm(x, g):
    x32 = x.astype(F32)
    y = x32 * lax.rsqrt(jnp.mean(x32 * x32, axis=-1, keepdims=True) + RMS_EPS)
    return (y * g.astype(F32)).astype(x.dtype)

def l2_norm(t):
    return t * lax.rsqrt(jnp.sum(t * t, axis=-1, keepdims=True) + RMS_EPS)

def s5_mixer(u, a_re, a_im, log_dt, b_re, b_im, c_re, c_im, d, w_glu, b_glu):
    bsz, seq, _ = u.shape
    u32 = u.astype(F32).reshape(bsz, seq, S5_GROUPS, S5_GROUP)
    lam = lax.complex(a_re.astype(F32), a_im.astype(F32))
    dt = jnp.exp(log_dt.astype(F32))[:, None]
    lam_bar = jnp.exp(lam * dt)
    b_bar = ((lam_bar - 1.0) / lam)[:, :, None] * lax.complex(b_re.astype(F32), b_im.astype(F32))
    c = lax.complex(c_re.astype(F32), c_im.astype(F32))
    bu = jnp.einsum('bsgc,gpc->bsgp', u32.astype(jnp.complex64), b_bar)
    lam_seq = jnp.broadcast_to(lam_bar, bu.shape)

    def combine(e_prev, e_next):
        a_p, s_p = e_prev
        a_n, s_n = e_next
        return a_n * a_p, a_n * s_p + s_n

    _, states = lax.associative_scan(combine, (lam_seq, bu), axis=1)
    y = jnp.real(jnp.einsum('bsgp,gcp->bsgc', states, c)) + d.astype(F32) * u32
    h = jax.nn.gelu(y.reshape(bsz, seq, S5_WIDTH))
    out = h * jax.nn.sigmoid(h @ w_glu.astype(F32) + b_glu.astype(F32))
    return out.astype(u.dtype)

def gated_deltanet(q, k, v, gate, a_logit, b_logit, conv_w, a_log, dt_bias, out_g):
    bsz, seq, _ = q.shape
    n = seq // CHUNK
    qkv = jnp.concatenate([q, k, v], axis=-1).astype(F32)
    qkv = lax.conv_general_dilated(
        qkv, conv_w.astype(F32)[:, None, :], window_strides=(1,),
        padding=[(GDN_CONV - 1, 0)], dimension_numbers=('NWC', 'WIO', 'NWC'),
        feature_group_count=3 * GDN_WIDTH)
    qkv = jax.nn.silu(qkv)
    q, k, v = jnp.split(qkv, 3, axis=-1)

    def heads(t):
        return t.reshape(bsz, n, CHUNK, GDN_HEADS, GDN_HEAD_DIM).transpose(0, 3, 1, 2, 4)

    def per_head(t):
        return t.reshape(bsz, n, CHUNK, GDN_HEADS).transpose(0, 3, 1, 2)

    q = l2_norm(heads(q)) * (GDN_HEAD_DIM ** -0.5)
    k = l2_norm(heads(k))
    v = heads(v)
    beta = per_head(jax.nn.sigmoid(b_logit.astype(F32)))
    g = -jnp.exp(a_log.astype(F32)) * jax.nn.softplus(a_logit.astype(F32) + dt_bias.astype(F32))
    gcum = jnp.cumsum(per_head(g), axis=-1)
    gamma = jnp.exp(gcum)
    diff = gcum[..., :, None] - gcum[..., None, :]
    idx = jnp.arange(CHUNK)
    strict = idx[:, None] > idx[None, :]
    causal = idx[:, None] >= idx[None, :]
    decay_strict = jnp.where(strict, jnp.exp(jnp.where(strict, diff, 0.0)), 0.0)
    decay_causal = jnp.where(causal, jnp.exp(jnp.where(causal, diff, 0.0)), 0.0)
    kk = jnp.einsum('bhntd,bhnjd->bhntj', k, k)
    lower = jnp.eye(CHUNK, dtype=F32) + beta[..., :, None] * kk * decay_strict
    rhs = jnp.concatenate([beta[..., None] * v, (beta * gamma)[..., None] * k], axis=-1)
    sol = lax.linalg.triangular_solve(lower, rhs, left_side=True, lower=True, unit_diagonal=True)
    u_new, w_k = jnp.split(sol, [GDN_HEAD_DIM], axis=-1)
    qk = jnp.einsum('bhntd,bhnjd->bhntj', q, k) * decay_causal
    q_g = q * gamma[..., None]
    k_tail = k * jnp.exp(gcum[..., -1:] - gcum)[..., None]
    chunk_decay = jnp.exp(gcum[..., -1])

    def step(state, inp):
        u_c, wk_c, qk_c, qg_c, kt_c, dec_c = inp
        w = u_c - jnp.einsum('bhtd,bhde->bhte', wk_c, state)
        o = jnp.einsum('bhtd,bhde->bhte', qg_c, state) + jnp.einsum('bhtj,bhje->bhte', qk_c, w)
        state = dec_c[..., None, None] * state + jnp.einsum('bhtd,bhte->bhde', kt_c, w)
        return state, o

    state0 = jnp.zeros((bsz, GDN_HEADS, GDN_HEAD_DIM, GDN_HEAD_DIM), F32)
    xs = (jnp.moveaxis(u_new, 2, 0), jnp.moveaxis(w_k, 2, 0), jnp.moveaxis(qk, 2, 0),
          jnp.moveaxis(q_g, 2, 0), jnp.moveaxis(k_tail, 2, 0), jnp.moveaxis(chunk_decay, 2, 0))
    _, o = lax.scan(step, state0, xs)
    o = o.transpose(1, 0, 3, 2, 4).reshape(bsz, seq, GDN_HEADS, GDN_HEAD_DIM)
    o = rms_norm(o, out_g) * jax.nn.silu(gate.astype(F32).reshape(bsz, seq, GDN_HEADS, GDN_HEAD_DIM))
    return o.reshape(bsz, seq, GDN_WIDTH).astype(gate.dtype)

def chunk_attention(h, w_qkv, w_out, q_g, k_g, rel_bias):
    bsz, seq, _ = h.shape
    n = seq // CHUNK
    qkv = (h @ w_qkv).reshape(bsz, seq, 3, CA_HEADS, CA_HEAD_DIM)
    q = rms_norm(qkv[:, :, 0], q_g).astype(F32)
    k = rms_norm(qkv[:, :, 1], k_g).astype(F32)
    v = qkv[:, :, 2].astype(F32)
    pad = CA_LEFT_CHUNKS * CHUNK
    k_pad = jnp.pad(k, ((0, 0), (pad, 0), (0, 0), (0, 0)))
    v_pad = jnp.pad(v, ((0, 0), (pad, 0), (0, 0), (0, 0)))
    rel = np.arange(CHUNK)[:, None] - np.arange(CA_BAND)[None, :] + pad
    rel_idx = np.clip(rel, -MAX_REL_DIST, MAX_REL_DIST) + MAX_REL_DIST
    bias = rel_bias.astype(F32)[:, rel_idx]
    band_pos = jnp.arange(CA_BAND) - pad
    scale = CA_HEAD_DIM ** -0.5

    def one_chunk(c):
        start = c * CHUNK
        q_c = lax.dynamic_slice_in_dim(q, start, CHUNK, axis=1)
        k_c = lax.dynamic_slice_in_dim(k_pad, start, CA_BAND, axis=1)
        v_c = lax.dynamic_slice_in_dim(v_pad, start, CA_BAND, axis=1)
        s = jnp.einsum('bqhd,bkhd->bhqk', q_c, k_c) * scale + bias
        s = jnp.where((band_pos + start) >= 0, s, -1e30)
        p = jax.nn.softmax(s, axis=-1)
        return jnp.einsum('bhqk,bkhd->bqhd', p, v_c)

    o = lax.map(one_chunk, jnp.arange(n))
    o = o.transpose(1, 0, 2, 3, 4).reshape(bsz, seq, D_MODEL).astype(h.dtype)
    return o @ w_out

def memory_cross_attention(h, mem_n, w_q, w_kv, w_out, q_g, k_g):
    bsz, seq, _ = h.shape
    n_mem = mem_n.shape[1]
    q = rms_norm((h @ w_q).reshape(bsz, seq, XA_HEADS, XA_HEAD_DIM), q_g).astype(F32)
    kv = (mem_n @ w_kv).reshape(bsz, n_mem, 2, XA_HEADS, XA_HEAD_DIM)
    k = rms_norm(kv[:, :, 0], k_g).astype(F32)
    v = kv[:, :, 1].astype(F32)
    s = jnp.einsum('bqhd,bkhd->bhqk', q, k) * (XA_HEAD_DIM ** -0.5)
    p = jax.nn.softmax(s, axis=-1)
    o = jnp.einsum('bhqk,bkhd->bqhd', p, v).reshape(bsz, seq, D_MODEL).astype(h.dtype)
    return o @ w_out

def swiglu(h, w_gate, w_up, w_down):
    return (jax.nn.silu(h @ w_gate) * (h @ w_up)) @ w_down

def setup_inputs(seed: int = 0) -> dict:
    key = jax.random.key(seed)
    keys = jax.random.split(key, 64)
    counter = iter(range(64))

    def nk():
        return keys[next(counter)]

    def nrm(shape, scale):
        return scale * jax.random.normal(nk(), shape, F32)

    def gain(shape):
        return 1.0 + nrm(shape, 0.02)

    D, NE, NO = D_MODEL, N_EVEN, N_ODD
    G, P, CG = S5_GROUPS, S5_STATE, S5_GROUP
    x = nrm((BATCH, SEQ, D), 1.0)
    mem = nrm((BATCH, N_MEM, D), 1.0)
    ab_norm_g = gain((NE, D))
    ab_w_in = nrm((NE, D, AB_IN), D ** -0.5)
    ab_w_out = nrm((NE, S5_WIDTH + GDN_WIDTH, D), (S5_WIDTH + GDN_WIDTH) ** -0.5)
    s5_a_re = -0.5 + nrm((NE, G, P), 0.01)
    s5_a_im = math.pi * jnp.arange(P, dtype=F32) + nrm((NE, G, P), 0.01)
    s5_log_dt = jax.random.uniform(nk(), (NE, G), F32, math.log(S5_DT_MIN), math.log(S5_DT_MAX))
    s5_b_re = nrm((NE, G, P, CG), (2 * CG) ** -0.5)
    s5_b_im = nrm((NE, G, P, CG), (2 * CG) ** -0.5)
    s5_c_re = nrm((NE, G, CG, P), (2 * P) ** -0.5)
    s5_c_im = nrm((NE, G, CG, P), (2 * P) ** -0.5)
    s5_d = nrm((NE, G, CG), 1.0)
    s5_w_glu = nrm((NE, S5_WIDTH, S5_WIDTH), S5_WIDTH ** -0.5)
    s5_b_glu = nrm((NE, S5_WIDTH), 0.01)
    gdn_conv_w = nrm((NE, GDN_CONV, 3 * GDN_WIDTH), GDN_CONV ** -0.5)
    gdn_a_log = jnp.log(jax.random.uniform(nk(), (NE, GDN_HEADS), F32, 1.0, 16.0))
    gdn_dt = jnp.exp(jax.random.uniform(nk(), (NE, GDN_HEADS), F32, math.log(GDN_DT_MIN), math.log(GDN_DT_MAX)))
    gdn_dt_bias = gdn_dt + jnp.log(-jnp.expm1(-gdn_dt))
    gdn_out_norm_g = gain((NE, GDN_HEAD_DIM))
    c_norm_g = gain((NO, D))
    c_w_qkv = nrm((NO, D, 3 * D), D ** -0.5)
    c_w_out = nrm((NO, D, D), D ** -0.5)
    c_q_norm_g = gain((NO, CA_HEAD_DIM))
    c_k_norm_g = gain((NO, CA_HEAD_DIM))
    c_rel_bias = nrm((NO, CA_HEADS, 2 * MAX_REL_DIST + 1), 0.1)
    mem_norm_g = gain((D,))
    xa_norm_g = gain((DEPTH, D))
    xa_w_q = nrm((DEPTH, D, D), D ** -0.5)
    xa_w_kv = nrm((DEPTH, D, 2 * D), D ** -0.5)
    xa_w_out = nrm((DEPTH, D, D), D ** -0.5)
    xa_q_norm_g = gain((DEPTH, XA_HEAD_DIM))
    xa_k_norm_g = gain((DEPTH, XA_HEAD_DIM))
    f_norm_g = gain((DEPTH, D))
    f_w_gate = nrm((DEPTH, D, FFN_HIDDEN), D ** -0.5)
    f_w_up = nrm((DEPTH, D, FFN_HIDDEN), D ** -0.5)
    f_w_down = nrm((DEPTH, FFN_HIDDEN, D), FFN_HIDDEN ** -0.5)
    return {
        "x": x, "mem": mem,
        "ab_norm_g": ab_norm_g, "ab_w_in": ab_w_in, "ab_w_out": ab_w_out,
        "s5_a_re": s5_a_re, "s5_a_im": s5_a_im, "s5_log_dt": s5_log_dt,
        "s5_b_re": s5_b_re, "s5_b_im": s5_b_im, "s5_c_re": s5_c_re, "s5_c_im": s5_c_im,
        "s5_d": s5_d, "s5_w_glu": s5_w_glu, "s5_b_glu": s5_b_glu,
        "gdn_conv_w": gdn_conv_w, "gdn_a_log": gdn_a_log, "gdn_dt_bias": gdn_dt_bias,
        "gdn_out_norm_g": gdn_out_norm_g,
        "c_norm_g": c_norm_g, "c_w_qkv": c_w_qkv, "c_w_out": c_w_out,
        "c_q_norm_g": c_q_norm_g, "c_k_norm_g": c_k_norm_g, "c_rel_bias": c_rel_bias,
        "mem_norm_g": mem_norm_g, "xa_norm_g": xa_norm_g, "xa_w_q": xa_w_q,
        "xa_w_kv": xa_w_kv, "xa_w_out": xa_w_out, "xa_q_norm_g": xa_q_norm_g,
        "xa_k_norm_g": xa_k_norm_g,
        "f_norm_g": f_norm_g, "f_w_gate": f_w_gate, "f_w_up": f_w_up, "f_w_down": f_w_down,
    }

def reference(x, mem, ab_norm_g, ab_w_in, ab_w_out, s5_a_re, s5_a_im, s5_log_dt,
              s5_b_re, s5_b_im, s5_c_re, s5_c_im, s5_d, s5_w_glu, s5_b_glu,
              gdn_conv_w, gdn_a_log, gdn_dt_bias, gdn_out_norm_g,
              c_norm_g, c_w_qkv, c_w_out, c_q_norm_g, c_k_norm_g, c_rel_bias,
              mem_norm_g, xa_norm_g, xa_w_q, xa_w_kv, xa_w_out, xa_q_norm_g, xa_k_norm_g,
              f_norm_g, f_w_gate, f_w_up, f_w_down):
    split_points = [S5_WIDTH, S5_WIDTH + GDN_WIDTH, S5_WIDTH + 2 * GDN_WIDTH,
                    S5_WIDTH + 3 * GDN_WIDTH, S5_WIDTH + 4 * GDN_WIDTH,
                    S5_WIDTH + 4 * GDN_WIDTH + GDN_HEADS]
    mem_n = rms_norm(mem, mem_norm_g)
    for layer in range(DEPTH):
        i = layer // 2
        if layer % 2 == 0:
            h = rms_norm(x, ab_norm_g[i])
            proj = h @ ab_w_in[i]
            u, q, k, v, gate, a_logit, b_logit = jnp.split(proj, split_points, axis=-1)
            a_out = s5_mixer(u, s5_a_re[i], s5_a_im[i], s5_log_dt[i], s5_b_re[i], s5_b_im[i],
                             s5_c_re[i], s5_c_im[i], s5_d[i], s5_w_glu[i], s5_b_glu[i])
            b_out = gated_deltanet(q, k, v, gate, a_logit, b_logit, gdn_conv_w[i],
                                   gdn_a_log[i], gdn_dt_bias[i], gdn_out_norm_g[i])
            x = x + jnp.concatenate([a_out, b_out], axis=-1) @ ab_w_out[i]
        else:
            x = x + chunk_attention(rms_norm(x, c_norm_g[i]), c_w_qkv[i], c_w_out[i],
                                    c_q_norm_g[i], c_k_norm_g[i], c_rel_bias[i])
        x = x + memory_cross_attention(rms_norm(x, xa_norm_g[layer]), mem_n, xa_w_q[layer],
                                       xa_w_kv[layer], xa_w_out[layer],
                                       xa_q_norm_g[layer], xa_k_norm_g[layer])
        x = x + swiglu(rms_norm(x, f_norm_g[layer]), f_w_gate[layer], f_w_up[layer], f_w_down[layer])
    return x


_drawn_inputs = setup_inputs


def setup_inputs(seed=0):
    import zlib

    import numpy as np

    out = dict(_drawn_inputs(seed))
    spreads = {}
    factors = {'ab_norm_g': 3.446,
     's5_a_re': 64.0,
     's5_a_im': 3.598,
     's5_log_dt': 3.684,
     's5_b_re': 13.9,
     's5_b_im': 5.154,
     's5_c_re': 5.112,
     's5_c_im': 14.61,
     's5_b_glu': 8.0,
     'gdn_out_norm_g': 6.529,
     'c_norm_g': 8.0,
     'c_q_norm_g': 8.0,
     'c_k_norm_g': 8.0,
     'c_rel_bias': 6.311,
     'mem_norm_g': 8.0,
     'xa_norm_g': 8.0,
     'xa_q_norm_g': 8.0,
     'xa_k_norm_g': 8.0,
     'f_norm_g': 2.844}
    for name, (base, spread) in spreads.items():
        noise = np.random.default_rng([zlib.crc32(name.encode()), seed]).standard_normal(out[name].shape)
        drawn = base * np.exp(spread * noise) if base else spread * noise
        out[name] = __import__('jax').numpy.asarray(drawn.astype(out[name].dtype))
    for name, factor in factors.items():
        out[name] = (out[name] * factor).astype(out[name].dtype)
    return out
```

```python
from contextlib import ExitStack

import concourse.bass as bass
from concourse import mybir

F32 = mybir.dt.float32
ALU = mybir.AluOpType
ACT = mybir.ActivationFunctionType
AX = mybir.AxisListType.X

P = 128
D = 1024
SEQ = 512
N_MEM = 256
DEPTH = 2
KT = D // P
TT = SEQ // P
MT = N_MEM // P
CHUNK = 64
EPS = 1e-6
S5_W = D // 2
S5_CH = 16
S5_G = S5_W // S5_CH
S5_P = 64
S5_L = 8
S5_C = SEQ // S5_L
S5_GP = S5_G // 2
S5_COLS = S5_G + S5_GP
GH = 4
GD = 128
NCH = SEQ // CHUNK
CH = 16
CD = D // CH
XH = 4
XD = D // XH
FH = -(-8 * D // (3 * 256)) * 256
FT = FH // P
FPAN = FH // 256
REL = 128
BAND_W = SEQ
BAND_E = BAND_W + P - 1

PAR = {}
_at = 0
for _name, _n in (
    ("ab_g", KT), ("c_g", KT), ("mem_g", KT), ("xa_g0", KT), ("xa_g1", KT), ("f_g0", KT), ("f_g1", KT),
    ("s5_d", 4), ("b_glu", 4), ("conv", 48), ("gdn_g", 1), ("xq_g0", 2), ("xq_g1", 2), ("xk_g0", 2), ("xk_g1", 2),
    ("cq_g", 1), ("ck_g", 1), ("dt_bias", GH), ("a_log", GH), ("a_re", S5_COLS), ("a_im", S5_COLS), ("log_dt", S5_COLS),
    ("eps", 1), ("half_pi", 1), ("sgn", 1), ("one", 1), ("nsgn", 1),
):
    PAR[_name] = (_at, _n)
    _at += _n
N_PAR = _at
CON = {n: i * P for i, n in enumerate(["ident", "inc", "neg", "m1", "m2", "m3", "m4", "m5", "m6", "same", "first", "second"])}
N_CON = len(CON) * P

TWO_PI = 6.283185307179586
PI_PARTS = (6.28125, 0.0019353071693331003, 1.0253114e-11)
ROUND = 12582912.0


def build_program(nc, A, upto=99, dump=None):
    ctx = ExitStack()
    with ctx:
        sb = ctx.enter_context(nc.sbuf_tensor("sb", [P, 53120], F32))
        ps = ctx.enter_context(nc.psum_tensor("ps", [P, 8, 512], F32))
        sems = {}

        PER_LAYER = {
            "kv_mm": 4, "kv_sq": 8, "kv_rt": 1, "kv_v": 4, "kv_kTa": 4, "kv_k": 4, "kv_kTv": 4, "kv_turned": 8,
            "xq_mm": 6, "xq_sq": 16, "xq_rt": 1, "xq_qTa": 4, "xq_q": 8, "xq_qTv": 4, "xq_turned": 8,
            "xa_s": 4, "xa_exp": 16, "xa_max": 4, "xa_p": 4, "xa_tr": 8, "xa_pTa": 4, "xa_pTv": 4,
            "xa_o": 8, "xa_oa": 4, "xa_ov": 4,
            "f_mm": FPAN, "f_silu": FT, "f_free": FT + 4, "d_mm": 7, "d_x": 8,
        }
        SERIES = {"norm": ("n0", "m", "x0", "f0", "c", "x1", "f1"), "back": ("mo", "xo0", "co", "xo1")}

        def in_series(what, tail, tag):
            if what == "back":
                return {"mm": 6, "x": 8}.get(tail)
            n = MT if tag == "m" else TT
            return {"sq": 2 * n, "sum": 1, "root": 1, "rinv": 1, "hv": n // 2, "ha": n // 2,
                    "turned": KT, "outa": KT // 2, "outv": KT // 2}.get(tail)

        def named(name):
            head, _, tail = name.partition("_")
            for what, tags in SERIES.items():
                if head in tags and in_series(what, tail, head) is not None:
                    return f"{what}_{tail}", sum(in_series(what, tail, t) for t in tags[:tags.index(head)])
            if head[-1].isdigit() and f"{head[:-1]}_{tail}" in PER_LAYER:
                base_name = f"{head[:-1]}_{tail}"
                return base_name, int(head[-1]) * PER_LAYER[base_name]
            return name, 0

        def sem(name):
            name = named(name)[0]
            if name not in sems:
                sems[name] = ctx.enter_context(nc.semaphore(name))
            return sems[name]

        def reg(at, *shape):
            n = 1
            for s in shape:
                n *= s
            v = sb[:, at:at + n]
            if len(shape) == 2:
                v = v.rearrange("p (a b) -> p a b", a=shape[0])
            if len(shape) == 3:
                v = v.rearrange("p (a b c) -> p a b c", a=shape[0], b=shape[1])
            if len(shape) == 4:
                v = v.rearrange("p (a b c d) -> p a b c d", a=shape[0], b=shape[1], c=shape[2])
            return v

        class Space:
            def __init__(self, at, end):
                self.at, self.end = at, end

            def __call__(self, *shape):
                n = 1
                for s in shape:
                    n *= s
                v = reg(self.at, *shape)
                self.at += n
                assert self.at <= self.end, (self.at, self.end)
                return v

        fixed = Space(0, 14900)
        par = fixed(N_PAR)
        con = fixed(N_CON)
        slots = [fixed(4096), fixed(4096)]
        ss2 = fixed(2, TT)
        nrm = fixed(2, TT)
        rinv = fixed(TT)
        rms_m = fixed(3, MT)
        memT = fixed(KT, N_MEM)
        top = 53120
        base = fixed.at

        def pcol(name, i=0):
            return par[:, PAR[name][0] + i:PAR[name][0] + i + 1]

        def pcols(name):
            return par[:, PAR[name][0]:PAR[name][0] + PAR[name][1]]

        def ccol(name):
            return con[:, CON[name]:CON[name] + P]

        ident = ccol("ident")

        panels = []

        def kview(w, c0, n, k0=0, nk=KT):
            return w[k0 * P:(k0 + nk) * P, c0:c0 + n].rearrange("(k p) n -> p k n", p=P)

        def full(slot, nk=KT, n=512):
            return slot[:, 0:nk * n].rearrange("p (k n) -> p k n", k=nk)

        def add_panel(name, parts):
            panels.append((name, parts))

        def add_full(name, w, c0):
            add_panel(name, [(lambda s: full(s), kview(w, c0, 512))])

        for i, c0 in enumerate((512, 1024, 1536, 2048, 0)):
            add_full(f"ab{i}", A["ab_w_in"], c0)
        add_panel("glu", [(lambda s: full(s, 4), kview(A["s5_w_glu"], 0, 512, 0, 4))])
        for i in range(2):
            add_full(f"abo{i}", A["ab_w_out"], 512 * i)

        def add_xa_ffn(l):
            for i in range(4):
                add_full(f"kv{l}{i}", A["xa_w_kv"][l], 512 * i)
            for i in range(2):
                add_full(f"xq{l}{i}", A["xa_w_q"][l], 512 * i)
            for i in range(2):
                add_full(f"xo{l}{i}", A["xa_w_out"][l], 512 * i)
            for i in range(FPAN):
                add_panel(f"gu{l}_{i}", [
                    (lambda s: full(s)[:, :, 0:256], kview(A["f_w_gate"][l], 256 * i, 256)),
                    (lambda s: full(s)[:, :, 256:512], kview(A["f_w_up"][l], 256 * i, 256))])
            for i in range(FT // 2):
                add_panel(f"dn{l}_{i}", [(lambda s: full(s, 2, 1024), kview(A["f_w_down"][l], 0, 1024, 2 * i, 2))])

        add_xa_ffn(0)
        for i in range(6):
            add_full(f"ca{i}", A["c_w_qkv"], 512 * i)
        for i in range(2):
            add_full(f"cao{i}", A["c_w_out"], 512 * i)
        add_xa_ffn(1)
        where = {name: n for n, (name, _) in enumerate(panels)}
        landed = []
        tally = [0, 0]
        for n, (_, parts) in enumerate(panels):
            tally[n % 2] += 16 * len(parts)
            landed.append(tally[n % 2])
        slot_landed = [sem("slot0_landed"), sem("slot1_landed")]
        panel_used = sem("panel_used")

        def take(pe, name):
            n = where[name]
            pe.wait_ge(slot_landed[n % 2], landed[n])
            return slots[n % 2]

        def bc(ap, axis, n):
            v = ap.unsqueeze(axis)
            shape = list(v.shape)
            shape[axis] = n
            return v.broadcast_to(shape)

        count = {}

        def after(name, n):
            return n + named(name)[1]

        def link(eng, ins, name):
            ins.then_inc(sem(name), 1)
            name = named(name)[0]
            count[name] = count.get(name, 0) + 1
            eng.wait_ge(sem(name), count[name])

        def norm_dve(v, t, x, h, r_in, dst, gain):
            n = x.shape[1]
            v.wait_ge(sem(f"{t}_sq"), after(f"{t}_sq", 2 * n))
            link(v, v.tensor_tensor(nrm[:, 0, 0:n], r_in[:, 0, 0:n], r_in[:, 1, 0:n], ALU.add), f"{t}_sum")
            v.wait_ge(sem(f"{t}_root"), after(f"{t}_root", 1))
            link(v, v.reciprocal(rinv[:, 0:n], nrm[:, 1, 0:n]), f"{t}_rinv")
            for i in range(0, n, 2):
                v.tensor_scalar(h[:, i, :], x[:, i, :], rinv[:, i:i + 1], None, ALU.mult).then_inc(sem(f"{t}_hv"), 1)
            for k in range(1, KT, 2):
                v.wait_ge(sem(f"{t}_turned"), after(f"{t}_turned", k + 1))
                v.tensor_scalar(dst[:, k, :], ps[:, k, 0:n * P], pcol(gain, k), None, ALU.mult).then_inc(sem(f"{t}_outv"), 1)

        def norm_act(a, t, x, h, r_in, dst, gain):
            n = x.shape[1]
            a.wait_ge(sem(f"{t}_sum"), after(f"{t}_sum", 1))
            a.activation(nrm[:, 1, 0:n], nrm[:, 0, 0:n], ACT.Sqrt, bias=pcol("eps"), scale=1.0 / D).then_inc(sem(f"{t}_root"), 1)
            a.wait_ge(sem(f"{t}_rinv"), after(f"{t}_rinv", 1))
            for i in range(1, n, 2):
                a.activation(h[:, i, :], x[:, i, :], ACT.Copy, scale=rinv[:, i:i + 1]).then_inc(sem(f"{t}_ha"), 1)
            for k in range(0, KT, 2):
                a.wait_ge(sem(f"{t}_turned"), after(f"{t}_turned", k + 1))
                a.activation(dst[:, k, :], ps[:, k, 0:n * P], ACT.Copy, scale=pcol(gain, k)).then_inc(sem(f"{t}_outa"), 1)

        def norm_pe(pe, t, x, h):
            n = x.shape[1]
            for i in range(n):
                pe.wait_ge(sem(f"{t}_h{'va'[i % 2]}"), after(f"{t}_h{'va'[i % 2]}", i // 2 + 1))
                for k in range(KT):
                    ins = pe.transpose(ps[:, k, i * P:(i + 1) * P], h[:, i, k * P:(k + 1) * P], ident)
                    if i == n - 1:
                        ins.then_inc(sem(f"{t}_turned"), 1)

        def squares_act(a, t, x, junk, dst, ready=None):
            for half in range(2):
                for i in range(x.shape[1]):
                    if ready is not None:
                        a.wait_ge(sem(ready), after(ready, half * x.shape[1] + i + 1))
                    n = half * x.shape[1] + i
                    if n >= 2:
                        a.wait_ge(sem(f"{t}_sq"), after(f"{t}_sq", n - 1))
                    a.activation(junk[:, (n % 2) * 512:(n % 2 + 1) * 512], x[:, i, half * 512:(half + 1) * 512], ACT.Square,
                                      accum_out=dst[:, half, i:i + 1]).then_inc(sem(f"{t}_sq"), 1)
            a.wait_ge(sem(f"{t}_sq"), after(f"{t}_sq", 2 * x.shape[1]))

        def ready_T(pe, t, k):
            pe.wait_ge(sem(f"{t}_out{'av'[k % 2]}"), after(f"{t}_out{'av'[k % 2]}", k // 2 + 1))

        def outproj_pe(pe, t, names, srcT, ready):
            for half, name in enumerate(names):
                w = full(take(pe, name))
                for i in range(TT):
                    for k in range(KT):
                        if half == 0 and i == 0:
                            ready(k)
                        ins = pe.matmul(ps[:, 4 * half + i, :], srcT[:, k, i * P:(i + 1) * P], w[:, k, :],
                                        start=(k == 0), stop=(k == KT - 1))
                    if i < TT - 1:
                        ins.then_inc(sem(f"{t}_mm"), 1)
                    else:
                        ins.then_inc(panel_used, 1)

        def outproj_dve(v, t, names, x):
            for half in range(2):
                for i in range(TT):
                    if i < TT - 1:
                        v.wait_ge(sem(f"{t}_mm"), after(f"{t}_mm", half * (TT - 1) + i + 1))
                    else:
                        v.wait_ge(panel_used, where[names[half]] + 1)
                    v.tensor_tensor(x[:, i, half * 512:(half + 1) * 512], ps[:, 4 * half + i, :],
                                         x[:, i, half * 512:(half + 1) * 512], ALU.add).then_inc(sem(f"{t}_x"), 1)

        mix = Space(base, top)
        catT = mix(KT, SEQ)
        qkvT = mix(3 * GH, SEQ)
        gateT = mix(GH, SEQ)
        hT_at = mix.at
        hT0 = mix(KT, SEQ)
        x = reg(hT_at, TT, D)
        arena = mix.at
        x0 = reg(base, TT, D)
        h0 = x0
        sq_junk0 = reg(arena + 2 * D, 1024)
        s5 = Space(arena, top)
        G = s5(S5_G, 15, S5_CH)
        WT = s5(S5_G, P)
        TM = s5(S5_G, P)
        E_re, E_im = s5(S5_GP, S5_C), s5(S5_GP, S5_C)
        R8 = s5(S5_GP, S5_C)
        H_re, H_im = s5(8, S5_COLS), s5(8, S5_COLS)
        B1, B2 = s5(S5_G, S5_CH), s5(S5_G, S5_CH)
        Cst = s5(S5_G, S5_CH)
        C_re, C_im = s5(S5_GP, S5_CH), s5(S5_GP, S5_CH)
        sm = {n: s5(S5_COLS) for n in (
            "dt ar th n r t t2 ab sn cs e e8 L_re L_im den rd f_re f_im L2_re L2_im L4_re L4_im u_re u_im w_re w_im").split()}
        Hs = s5(8, S5_G)
        t_pool2 = s5(S5_GP, S5_C // 2)
        logits = s5(TT, 2 * GH)
        w_ab = s5(KT, 2 * GH)
        late = Space(arena, arena + S5_G * 15 * S5_CH)
        V_re, V_im = late(S5_GP, 8, S5_CH), late(S5_GP, 8, S5_CH)
        z_re, z_im, t_a = late(S5_GP, S5_C), late(S5_GP, S5_C), late(S5_GP, S5_C)
        late2 = Space(hT_at, hT_at + KT * SEQ)
        t_b, t_c = late2(S5_GP, S5_C), late2(S5_GP, S5_C)
        U2 = late2(S5_G, S5_C)
        uP = catT[:, 4:8, :]
        yP = reg(arena + 7680 + 8192, 4, SEQ)
        hg = reg(arena + 7680 + 4096, 4, SEQ)
        sg = reg(arena + 7680 + 4096 + 2048, 4, SEQ)
        s5_bc = sb[:, arena + 7680 + 8192 + 3072 + 768:arena + 7680 + 8192 + 3072 + 768 + 2048]
        t_pool = reg(arena + 7680, 2, 4, S5_COLS)
        u_dram = nc.dram_tensor("u_dram", (S5_G, S5_CH, 8 * S5_C), F32, kind="Internal").ap()
        y_dram = nc.dram_tensor("y_dram", (S5_G, S5_CH, 8 * S5_C), F32, kind="Internal").ap()

        def ab_wait(eng, n):
            if n % 4 < 3:
                eng.wait_ge(sem("ab_mm"), n // 4 * 3 + n % 4 + 1)
            else:
                eng.wait_ge(panel_used, where[f"ab{n // 4}"] + 1)

        def ab_groups_pe(pe, pi):
            w = full(take(pe, f"ab{pi}"))
            for ft in range(4):
                n = 4 * pi + ft
                if n < 8:
                    pe.wait_ge(sem(f"n0_out{'av'[n % 2]}"), after(f"n0_out{'av'[n % 2]}", n // 2 + 1))
                elif n < 16:
                    pe.wait_ge(sem("conv"), n - 7)
                else:
                    pe.wait_ge(sem("conv"), n - 7)
                for k in range(KT):
                    if n == 0:
                        ready_T(pe, "n0", k)
                    ins = pe.matmul(ps[:, n % 8, :], w[:, k, ft * P:(ft + 1) * P], hT0[:, k, :],
                                    start=(k == 0), stop=(k == KT - 1))
                if ft < 3:
                    ins.then_inc(sem("ab_mm"), 1)
                else:
                    ins.then_inc(panel_used, 1)

        conv_y = catT[:, 0:2, :]

        def conv_dve(v, n):
            ab_wait(v, n)
            if n >= 2:
                v.wait_ge(sem("qkv_s"), n - 1)
            y = conv_y[:, n % 2, :]
            b = ps[:, n % 8, :]
            link(v, v.tensor_scalar(y, b, pcol("conv", 3 * 12 + n), None, ALU.mult), "dve_step")
            for s in (1, 2, 3):
                ins = v.scalar_tensor_tensor(y[:, s:SEQ], b[:, 0:SEQ - s], pcol("conv", (3 - s) * 12 + n),
                                             y[:, s:SEQ], ALU.mult, ALU.add)
                if s < 3:
                    link(v, ins, "dve_step")
                else:
                    ins.then_inc(sem("conv"), 1)

        def silu_act(a, n):
            a.wait_ge(sem("conv"), n + 1)
            a.activation(qkvT[:, n, :], conv_y[:, n % 2, :], ACT.Silu).then_inc(sem("qkv_s"), 1)

        def gate_act(a, n):
            ab_wait(a, n)
            a.activation(gateT[:, n - 12, :], ps[:, n % 8, :], ACT.Silu).then_inc(sem("gate_s"), 1)

        def u_act(a, n):
            ab_wait(a, n)
            a.activation(uP[:, n - 16, :].rearrange("p (l c) -> p c l", l=8),
                              ps[:, n % 8, :].rearrange("p (c l) -> p c l", l=8), ACT.Copy).then_inc(sem("u_s"), 1)

        def logits_pe(pe):
            pe.wait_ge(sem("gate_s"), 4)
            pe.wait_ge(sem("wab_in"), 16)
            for i in range(TT):
                for k in range(KT):
                    ins = pe.matmul(ps[:, 7, i * 8:(i + 1) * 8], hT0[:, k, i * P:(i + 1) * P], w_ab[:, k, :],
                                    start=(k == 0), stop=(k == KT - 1))
            ins.then_inc(sem("logit_mm"), 1)

        def cmul(eng, o_re, o_im, a_re, a_im, b_re, b_im, t1, t2, name):
            link(eng, eng.tensor_tensor(t1, a_re, b_re, ALU.mult), name)
            link(eng, eng.tensor_tensor(t2, a_im, b_im, ALU.mult), name)
            link(eng, eng.tensor_tensor(o_re, t1, t2, ALU.subtract), name)
            link(eng, eng.tensor_tensor(t1, a_re, b_im, ALU.mult), name)
            link(eng, eng.tensor_tensor(t2, a_im, b_re, ALU.mult), name)
            link(eng, eng.tensor_tensor(o_im, t1, t2, ALU.add), name)

        def s5_params_act(a):
            a.wait_ge(sem("par_in"), 16)
            a.activation(sm["dt"], pcols("log_dt"), ACT.Exp).then_inc(sem("s5_dt"), 1)
            a.wait_ge(sem("s5_arg"), 1)
            a.activation(sm["e"], sm["ar"], ACT.Exp).then_inc(sem("s5_fn"), 1)
            a.activation(sm["e8"], sm["ar"], ACT.Exp, scale=8.0).then_inc(sem("s5_fn"), 1)
            a.activation(sm["sn"], sm["r"], ACT.Sin).then_inc(sem("s5_fn"), 1)
            link(a, a.activation(sm["ab"], sm["r"], ACT.Abs), "act_step")
            a.activation(sm["cs"], sm["ab"], ACT.Sin, bias=pcol("half_pi"), scale=-1.0).then_inc(sem("s5_fn"), 1)

        def s5_params_pool(g):
            ch = "s5_pool"
            a_re, a_im = pcols("a_re"), pcols("a_im")
            g.wait_ge(sem("s5_dt"), 1)
            link(g, g.tensor_tensor(sm["ar"], a_re, sm["dt"], ALU.mult), ch)
            link(g, g.tensor_tensor(sm["th"], a_im, sm["dt"], ALU.mult), ch)
            link(g, g.tensor_scalar(sm["n"], sm["th"], 1.0 / TWO_PI, ROUND, ALU.mult, ALU.add), ch)
            link(g, g.tensor_scalar(sm["n"], sm["n"], ROUND, None, ALU.subtract), ch)
            src = sm["th"]
            for c in PI_PARTS:
                link(g, g.tensor_scalar(sm["t"], sm["n"], c, None, ALU.mult), ch)
                link(g, g.tensor_tensor(sm["r"], src, sm["t"], ALU.subtract), ch)
                src = sm["r"]
            link(g, g.tensor_scalar(sm["r"], sm["r"], 3.1415925, -3.1415925, ALU.min, ALU.max), "s5_arg")
            g.wait_ge(sem("s5_fn"), 4)
            link(g, g.tensor_tensor(sm["L_re"], sm["e"], sm["cs"], ALU.mult), ch)
            link(g, g.tensor_tensor(sm["L_im"], sm["e"], sm["sn"], ALU.mult), ch)
            link(g, g.tensor_tensor(sm["t"], a_re, a_re, ALU.mult), ch)
            link(g, g.tensor_tensor(sm["t2"], a_im, a_im, ALU.mult), ch)
            link(g, g.tensor_tensor(sm["den"], sm["t"], sm["t2"], ALU.add), "s5_den")
            link(g, g.tensor_scalar(sm["n"], sm["L_re"], 1.0, None, ALU.subtract), ch)
            link(g, g.tensor_tensor(sm["t"], sm["n"], a_re, ALU.mult), ch)
            link(g, g.tensor_tensor(sm["t2"], sm["L_im"], a_im, ALU.mult), ch)
            link(g, g.tensor_tensor(sm["f_re"], sm["t"], sm["t2"], ALU.add), ch)
            link(g, g.tensor_tensor(sm["t"], sm["L_im"], a_re, ALU.mult), ch)
            link(g, g.tensor_tensor(sm["t2"], sm["n"], a_im, ALU.mult), ch)
            link(g, g.tensor_tensor(sm["f_im"], sm["t"], sm["t2"], ALU.subtract), ch)
            g.wait_ge(sem("s5_rd"), 1)
            for h, f, l in ((H_re, "f_re", "L_re"), (H_im, "f_im", "L_im")):
                link(g, g.tensor_tensor(h[:, 7, 0:S5_G], sm[f][:, 0:S5_G], sm["rd"][:, 0:S5_G], ALU.mult), ch)
                link(g, g.tensor_copy(h[:, 7, S5_G:S5_COLS], sm[l][:, S5_G:S5_COLS]), ch)
            L = lambda n: (sm[n + "_re"], sm[n + "_im"])
            cmul(g, *L("L2"), *L("L"), *L("L"), sm["t"], sm["t2"], ch)
            cmul(g, *L("L4"), *L("L2"), *L("L2"), sm["t"], sm["t2"], ch)
            tmp = t_pool
            for lo, n, p in ((6, 1, "L"), (4, 2, "L2"), (0, 4, "L4")):
                l_re, l_im = L(p)
                cmul(g, H_re[:, lo:lo + n, :], H_im[:, lo:lo + n, :], H_re[:, lo + n:lo + 2 * n, :], H_im[:, lo + n:lo + 2 * n, :],
                     bc(l_re, 1, n), bc(l_im, 1, n), tmp[:, 0, 0:n, :], tmp[:, 1, 0:n, :], ch)
            link(g, g.tensor_copy(E_re[:, :, 1:2], sm["cs"][:, S5_G:S5_COLS].unsqueeze(2)), ch)
            g.wait_ge(sem("bc_in"), 16)
            for m in range(8):
                link(g, g.tensor_scalar(Hs[:, m, :], H_im[:, m, 0:S5_G], pcol("sgn"), None, ALU.mult), ch)
            link(g, g.tensor_scalar(Cst, Cst, pcol("nsgn"), None, ALU.mult), "s5_tables")

            u, w = (sm["u_re"][:, 0:S5_GP], sm["u_im"][:, 0:S5_GP]), (sm["w_re"][:, 0:S5_GP], sm["w_im"][:, 0:S5_GP])
            one = (sm["cs"][:, S5_G:S5_COLS], sm["sn"][:, S5_G:S5_COLS])
            tt1, tt2 = sm["t"][:, 0:S5_GP], sm["t2"][:, 0:S5_GP]
            cmul(g, *u, *one, *one, tt1, tt2, ch)
            cmul(g, *w, *u, *u, tt1, tt2, ch)
            cmul(g, *u, *w, *w, tt1, tt2, ch)
            link(g, g.memset(E_re[:, :, 0:1], 1.0), ch)
            link(g, g.memset(E_im[:, :, 0:1], 0.0), ch)
            n = 1
            while n < S5_C:
                cmul(g, E_re[:, :, n:2 * n], E_im[:, :, n:2 * n], E_re[:, :, 0:n], E_im[:, :, 0:n],
                     bc(u[0], 2, n), bc(u[1], 2, n), R8[:, :, 0:n], t_pool2[:, :, 0:n], ch)
                n *= 2
                if n < S5_C:
                    cmul(g, *w, *u, *u, tt1, tt2, ch)
                    u, w = w, u
            link(g, g.memset(R8, 0.0), ch)
            link(g, g.tensor_tensor(R8[:, :, 1:S5_C], R8[:, :, 1:S5_C], bc(sm["e8"][:, S5_G:S5_COLS], 2, S5_C - 1), ALU.add), "s5_turn")

            g.wait_ge(sem("s5_tm"), 16)
            vr = H_re[:, :, S5_G:S5_COLS].rearrange("p i g -> p g i")
            vi = H_im[:, :, S5_G:S5_COLS].rearrange("p i g -> p g i")
            cr, ci = bc(C_re, 2, 8), bc(C_im, 2, 8)
            vr, vi = bc(vr, 3, S5_CH), bc(vi, 3, S5_CH)
            t1 = reg(arena + 4096, S5_GP, 8, S5_CH)
            link(g, g.tensor_tensor(V_re, cr, vr, ALU.mult), ch)
            link(g, g.tensor_tensor(t1, ci, vi, ALU.mult), ch)
            link(g, g.tensor_tensor(V_re, V_re, t1, ALU.subtract), ch)
            link(g, g.tensor_tensor(V_im, cr, vi, ALU.mult), ch)
            link(g, g.tensor_tensor(t1, ci, vr, ALU.mult), ch)
            link(g, g.tensor_tensor(V_im, V_im, t1, ALU.add), ch)
            link(g, g.tensor_scalar(V_im, V_im, -1.0, None, ALU.mult), "s5_v")

        def s5_g_dve(v):
            v.wait_ge(sem("s5_den"), 1)
            v.reciprocal(sm["rd"], sm["den"]).then_inc(sem("s5_rd"), 1)
            v.wait_ge(sem("s5_tables"), 1)
            for g0 in range(0, S5_G, 16):
                gs = slice(g0, g0 + 16)
                o = G[:, gs, 0:8, :]
                hr = bc(H_re[:, :, gs].rearrange("p m g -> p g m"), 3, S5_CH)
                hi = bc(Hs[:, :, gs].rearrange("p m g -> p g m"), 3, S5_CH)
                t = WT[:, gs, :].rearrange("p g (m c) -> p g m c", c=S5_CH)
                v.tensor_tensor(o, hr, bc(B1[:, gs, :], 2, 8), ALU.mult)
                link(v, v.tensor_tensor(t, hi, bc(B2[:, gs, :], 2, 8), ALU.mult), "dve_step")
                v.tensor_tensor(o, o, t, ALU.add).then_inc(sem("s5_g"), 1)
            v.memset(G[:, :, 8:15, :], 0.0).then_inc(sem("s5_g"), 1)

        def s5_tables_pe(pe):
            pe.wait_ge(sem("gate_s"), 4)
            pe.wait_ge(sem("s5_g"), 3)
            for s in range(16):
                if s >= 3:
                    pe.wait_ge(sem("s5_tm"), s - 2)
                bank = ps[:, 4 + s % 3, :]
                for q in range(4):
                    g = 4 * (s % 8) + q
                    if s < 8:
                        ins = pe.transpose(bank[:, q * P:(q + 1) * P], G[:, g, 0:8, :].rearrange("p m c -> p (m c)"), ident)
                    else:
                        for i in range(8):
                            ins = pe.matmul(bank[:, q * P + i * S5_CH:q * P + (i + 1) * S5_CH],
                                            G[:, g, i:i + 8, :].rearrange("p m c -> p (m c)"), Cst[:, g, :], start=True, stop=True)
                ins.then_inc(sem("s5_tab"), 1)

        def s5_tables_act(a):
            for s in range(16):
                a.wait_ge(sem("s5_tab"), s + 1)
                dst = (WT if s < 8 else TM)[:, 4 * (s % 8):4 * (s % 8) + 4, :].rearrange("p g n -> p (g n)")
                a.activation(dst, ps[:, 4 + s % 3, :], ACT.Copy).then_inc(sem("s5_tm"), 1)

        def s5_u_sp(sp):
            sp.wait_ge(sem("u_s"), 4)
            sp.dma_start(u_dram.rearrange("(f g) c n -> (g c) f n", f=4), uP).then_inc(sem("u_out"), 16)
            sp.wait_ge(sem("u_out"), 16)
            sp.wait_ge(panel_used, where["ab4"] + 1)
            sp.wait_ge(sem("logit_mm"), 1)
            for l in range(8):
                sp.dma_start(U2[l * S5_CH:(l + 1) * S5_CH, :, :],
                             u_dram[:, :, l * S5_C:(l + 1) * S5_C].rearrange("g c n -> c g n")).then_inc(sem("u_in"), 16)

        def s5_y_sp(sp):
            sp.wait_ge(sem("y_s"), 4)
            for l in range(8):
                sp.dma_start(y_dram[:, :, l * S5_C:(l + 1) * S5_C].rearrange("g c n -> c g n"),
                             U2[(7 - l) * S5_CH:(8 - l) * S5_CH, :, :]).then_inc(sem("y_out"), 16)
            sp.wait_ge(sem("y_out"), 16 * 8)
            sp.dma_start(yP, y_dram.rearrange("(f g) c n -> (g c) f n", f=4)).then_inc(sem("y_in"), 16)

        def s5_states_pe(pe):
            pe.wait_ge(sem("s5_tm"), 16)
            pe.wait_ge(sem("logit"), 1)
            pe.wait_ge(sem("u_in"), 16 * 8)
            for ri in range(2):
                for g in range(S5_G):
                    gp, g2 = g // 2, g % 2
                    ins = pe.matmul(ps[g2 * 64:g2 * 64 + 64, 4 + 2 * ri + gp // 8, (gp % 8) * S5_C:(gp % 8 + 1) * S5_C],
                                    WT[:, g, ri * 64:ri * 64 + 64], U2[:, g, :], start=True, stop=True)
                ins.then_inc(sem("s5_x"), 1)

        def s5_states_dve(v):
            X_re = ps[:, 4:6, :].rearrange("p b (g c) -> p (b g) c", c=S5_C)
            X_im = ps[:, 6:8, :].rearrange("p b (g c) -> p (b g) c", c=S5_C)
            ch = "dve_step"
            flat = lambda a: a.rearrange("p g c -> p (g c)")
            v.wait_ge(sem("s5_turn"), 1)
            v.wait_ge(sem("s5_v"), 1)
            v.wait_ge(sem("s5_x"), 2)
            link(v, v.tensor_tensor(t_a, X_re, E_re, ALU.mult), ch)
            link(v, v.tensor_tensor(t_b, X_im, E_im, ALU.mult), ch)
            link(v, v.tensor_tensor(t_a, t_a, t_b, ALU.add), ch)
            link(v, v.tensor_tensor_scan(flat(z_re), flat(R8), flat(t_a), 0.0, ALU.mult, ALU.add), ch)
            link(v, v.tensor_tensor(t_c, X_im, E_re, ALU.mult), ch)
            link(v, v.tensor_tensor(t_b, X_re, E_im, ALU.mult), ch)
            link(v, v.tensor_tensor(t_c, t_c, t_b, ALU.subtract), ch)
            link(v, v.tensor_tensor_scan(flat(z_im), flat(R8), flat(t_c), 0.0, ALU.mult, ALU.add), ch)
            n = S5_C - 1
            link(v, v.tensor_tensor(t_a, z_re, E_re, ALU.mult), ch)
            link(v, v.tensor_tensor(t_b, z_im, E_im, ALU.mult), ch)
            link(v, v.tensor_tensor(t_c[:, :, 1:], t_a[:, :, 0:n], t_b[:, :, 0:n], ALU.subtract), ch)
            link(v, v.memset(t_c[:, :, 0:1], 0.0), ch)
            link(v, v.tensor_tensor(t_a, z_re, E_im, ALU.mult), ch)
            link(v, v.tensor_tensor(t_b, z_im, E_re, ALU.mult), ch)
            link(v, v.tensor_tensor(z_re[:, :, 1:], t_a[:, :, 0:n], t_b[:, :, 0:n], ALU.add), ch)
            v.memset(z_re[:, :, 0:1], 0.0).then_inc(sem("s5_carry"), 1)

        def s5_out_pe(pe):
            pe.wait_ge(sem("u_s"), 4)
            pe.wait_ge(sem("s5_carry"), 1)
            for n in range(S5_G):
                gp, g2 = n % S5_GP, n // S5_GP
                g = 2 * gp + g2
                r = slice(g2 * 64, g2 * 64 + 64)
                o = ps[:, n // 8, (n % 8) * S5_C:(n % 8 + 1) * S5_C]
                pe.matmul(o, TM[:, g, :], U2[:, g, :], start=True, stop=False)
                pe.matmul(o, V_re[r, gp, :, :].rearrange("p i c -> p (i c)"), t_c[r, gp, :], start=False, stop=False)
                ins = pe.matmul(o, V_im[r, gp, :, :].rearrange("p i c -> p (i c)"), z_re[r, gp, :], start=False, stop=True)
                if n % 8 == 7:
                    ins.then_inc(sem("s5_y"), 1)

        def s5_out_act(a):
            for b in range(4):
                a.wait_ge(sem("s5_y"), b + 1)
                pairs = U2.rearrange("p (g two) c -> p g two c", two=2)[:, 8 * (b % 2):8 * (b % 2) + 8, b // 2, :]
                a.activation(pairs, ps[:, b, :].rearrange("p (g c) -> p g c", c=S5_C), ACT.Copy).then_inc(sem("y_s"), 1)

        def s5_glu_dve(v):
            v.wait_ge(sem("y_in"), 16)
            for f in range(4):
                v.scalar_tensor_tensor(yP[:, f, :], uP[:, f, :], pcol("s5_d", f), yP[:, f, :], ALU.mult, ALU.add).then_inc(sem("y_d"), 1)
            for f in range(4):
                v.wait_ge(sem("glu_s"), f + 1)
                v.tensor_tensor(catT[:, f, :].rearrange("p (c l) -> p l c", l=8),
                                     sg[:, f, :].rearrange("p (l c) -> p l c", l=8),
                                     hg[:, f, :].rearrange("p (l c) -> p l c", l=8), ALU.mult).then_inc(sem("s5_done"), 1)

        def s5_glu_act(a):
            for f in range(4):
                a.wait_ge(sem("y_d"), f + 1)
                a.activation(hg[:, f, :], yP[:, f, :], ACT.Gelu_apprx_tanh).then_inc(sem("gelu_s"), 1)
            for f in range(4):
                if f < 3:
                    a.wait_ge(sem("glu_mm"), f + 1)
                else:
                    a.wait_ge(panel_used, where["glu"] + 1)
                a.activation(sg[:, f, :], ps[:, 4 + f, :], ACT.Sigmoid, bias=pcol("b_glu", f)).then_inc(sem("glu_s"), 1)

        def s5_glu_pe(pe):
            w = full(take(pe, "glu"), 4)
            pe.wait_ge(sem("s5_carry"), 1)
            for f in range(4):
                for k in range(4):
                    if f == 0:
                        pe.wait_ge(sem("gelu_s"), k + 1)
                    ins = pe.matmul(ps[:, 4 + f, :], w[:, k, f * P:(f + 1) * P], hg[:, k, :], start=(k == 0), stop=(k == 3))
                if f < 3:
                    ins.then_inc(sem("glu_mm"), 1)
                else:
                    ins.then_inc(panel_used, 1)

        gd = Space(hT_at, top)
        q_n, k_n, k_b, q_g = gd(GH, GD), gd(GH, GD), gd(GH, GD), gd(GH, GD)
        q_nT, k_nT, k_bT = gd(GH, P), gd(GH, P), gd(GH, P)
        dec_m = gd(GH, P)
        k_bg, v_b, k_t = gd(TT, GH, GD), gd(TT, GH, GD), gd(TT, GH, GD)
        q_gT = gd(TT, GH, P)
        A_T, QK_T = gd(TT, GH, P), gd(TT, GH, P)
        U_m, T_m, Y_m, A_l = gd(TT, GH, P), gd(TT, GH, P), gd(TT, GH, P), gd(TT, GH, P)
        g_bc = gd(GH, P)
        state = gd(GH, GD)
        w_c = gd(2, GH * GD)
        gs = {n: gd(TT, GH) for n in "z az e1 l1 sp g eb beta gc tail gamma ss_o r_o".split()}
        ea = gd(GH)
        dec = gd(2, TT * GH)
        ssq = gd(2, GH)
        rq = gd(2, GH)
        co = {n: gd(GH) for n in "q qg k kb kbg kt".split()}
        lg = gd(TT, 2 * GH)
        qkv0 = base + KT * SEQ
        u_n, wk_T, o_t = reg(qkv0, TT, GH, GD), reg(qkv0 + 2048, TT, GH, P), reg(qkv0 + 4096, TT, GH, GD)
        flat3 = lambda a: a.rearrange("p a b -> p (a b)")

        def logits_dve(v):
            v.wait_ge(sem("logit_mm"), 1)
            v.tensor_copy(logits, ps[:, 7, 0:TT * 8].rearrange("p (i n) -> p i n", i=TT)).then_inc(sem("logit"), 1)

        def gates_dve(v):
            ch = "dve_step"
            link(v, v.tensor_copy(lg, logits), ch)
            link(v, v.tensor_tensor(gs["z"], lg[:, :, 0:GH], bc(pcols("dt_bias"), 1, TT), ALU.add), ch)
            link(v, v.tensor_scalar(gs["az"], gs["z"], -1.0, None, ALU.mult), ch)
            link(v, v.tensor_tensor(gs["az"], gs["az"], gs["z"], ALU.max), "gate_in")
            v.wait_ge(sem("gate_fn"), 3)
            link(v, v.scalar_tensor_tensor(gs["sp"], gs["z"], 0.0, gs["l1"], ALU.max, ALU.add), ch)
            link(v, v.tensor_tensor(gs["sp"], gs["sp"], bc(ea, 1, TT), ALU.mult), ch)
            link(v, v.tensor_scalar(gs["g"], gs["sp"], -1.0, None, ALU.mult), "g_ready")
            link(v, v.tensor_scalar(gs["eb"], gs["eb"], 1.0, None, ALU.add), ch)
            link(v, v.reciprocal(gs["beta"], gs["eb"]), ch)
            v.wait_ge(sem("gcum_mm"), 1)
            link(v, v.tensor_copy(gs["gc"].rearrange("p a b -> p (a b)"), ps[:, 7, 0:16]), ch)
            link(v, v.tensor_tensor(gs["tail"].rearrange("p a b -> p (a b)"), ps[:, 7, 16:32],
                                    gs["gc"].rearrange("p a b -> p (a b)"), ALU.subtract), "gcum")

        def gates_act(a):
            a.wait_ge(sem("gate_in"), 1)
            link(a, a.activation(gs["e1"], gs["az"], ACT.Exp, scale=-1.0), "act_step")
            a.activation(gs["l1"], gs["e1"], ACT.Ln, bias=pcol("one")).then_inc(sem("gate_fn"), 1)
            a.activation(gs["eb"], lg[:, :, GH:2 * GH], ACT.Exp, scale=-1.0).then_inc(sem("gate_fn"), 1)
            a.activation(ea, pcols("a_log"), ACT.Exp).then_inc(sem("gate_fn"), 1)
            a.wait_ge(sem("gcum"), 1)
            a.activation(gs["gamma"], gs["gc"], ACT.Exp).then_inc(sem("decays"), 1)
            a.activation(gs["tail"], gs["tail"], ACT.Exp).then_inc(sem("decays"), 1)
            a.activation(dec.rearrange("p a b -> p (a b)"), ps[:, 7, 32:64], ACT.Exp).then_inc(sem("decays"), 1)

        def gates_pe(pe):
            pe.wait_ge(sem("glu_s"), 4)
            pe.wait_ge(sem("g_ready"), 1)
            g = gs["g"].rearrange("p a b -> p (a b)")
            for n, m in enumerate(("inc", "same", "first", "second")):
                ins = pe.matmul(ps[:, 7, 16 * n:16 * n + 16], ccol(m), g, start=True, stop=True)
            ins.then_inc(sem("gcum_mm"), 1)

        def gdn_turn_pe(pe, i):
            if i == 0:
                pe.wait_ge(sem("qkv_s"), 12)
                pe.wait_ge(sem("y_s"), 4)
            else:
                pe.wait_ge(sem("g_tok"), 7 * i)
            for n in range(3):
                for h in range(GH):
                    ins = pe.transpose(ps[:, n, h * P:(h + 1) * P], qkvT[:, n * GH + h, i * P:(i + 1) * P], ident)
                ins.then_inc(sem("g_tr"), 1)

        def gdn_back_pe(pe, i):
            pe.wait_ge(sem("g_tok"), 7 * i + 4)
            if i == 0:
                pe.wait_ge(sem("glu_s"), 4)
            else:
                pe.wait_ge(sem("g_at"), 2 * i)
            for n, src in enumerate((q_n, k_n, k_b, q_g)):
                for h in range(GH):
                    ins = pe.transpose(ps[:, 3 + n, h * P:(h + 1) * P], src[:, h, :], ident)
                ins.then_inc(sem("g_back"), 1)

        def gdn_prod_pe(pe, i):
            pe.wait_ge(sem("g_ft"), 4 * i + 4)
            if i == 0:
                pe.wait_ge(sem("decays"), 3)
            for bank, l, r in ((7, k_nT, k_bT), (3, k_nT, q_nT)):
                for h in range(GH):
                    ins = pe.matmul(ps[:, bank, h * P:(h + 1) * P], l[:, h, :], r[:, h, :], start=True, stop=True)
                ins.then_inc(sem("g_prod"), 1)
            pe.wait_ge(sem("g_bc"), i + 1)
            for h in range(GH):
                ins = pe.matmul(ps[:, 4, h * P:(h + 1) * P], g_bc[:, h, :], ccol("inc"), start=True, stop=True)
            ins.then_inc(sem("g_row"), 1)

        def gdn_tok_act(a, i):
            for n in range(2):
                a.wait_ge(sem("g_tr"), 3 * i + n + 1)
                if i > 0:
                    a.wait_ge(sem("g_ss"), 2 * i - 1 + n)
                a.activation(A_l[:, n, :, :].rearrange("p a b -> p (a b)"), ps[:, n, :], ACT.Square).then_inc(sem("g_sq"), 1)
            a.wait_ge(sem("g_ss"), 2 * i + 2)
            a.activation(rq, ssq, ACT.Sqrt, bias=pcol("eps")).then_inc(sem("g_rt"), 1)

        def gdn_back_act(a, i):
            if i > 0:
                a.wait_ge(sem("g_row"), i)
            for n, dst in enumerate((q_nT, k_nT, k_bT, q_gT[:, i, :, :])):
                a.wait_ge(sem("g_back"), 4 * i + n + 1)
                a.activation(dst, ps[:, 3 + n, :].rearrange("p (a b) -> p a b", a=GH), ACT.Copy).then_inc(sem("g_ft"), 1)

        def gdn_dec_act(a, i):
            a.wait_ge(sem("g_diff"), 4 * i + 4)
            a.activation(dec_m, dec_m, ACT.Exp).then_inc(sem("g_dec"), 1)

        def gdn_tok_dve(v, i):
            for n in range(2):
                v.wait_ge(sem("g_sq"), 2 * i + n + 1)
                link(v, v.tensor_reduce(ssq[:, n, :], A_l[:, n, :, :], AX, ALU.add), "g_ss")
            if i == 0:
                v.wait_ge(sem("decays"), 3)
            v.wait_ge(sem("g_rt"), i + 1)
            ch = "dve_step"
            link(v, v.reciprocal(rq, rq), ch)
            link(v, v.tensor_scalar(co["q"], rq[:, 0, :], GD ** -0.5, None, ALU.mult), ch)
            link(v, v.tensor_tensor(co["qg"], co["q"], gs["gamma"][:, i, :], ALU.mult), ch)
            link(v, v.tensor_tensor(co["kb"], rq[:, 1, :], gs["beta"][:, i, :], ALU.mult), ch)
            link(v, v.tensor_tensor(co["kbg"], co["kb"], gs["gamma"][:, i, :], ALU.mult), ch)
            link(v, v.tensor_tensor(co["kt"], rq[:, 1, :], gs["tail"][:, i, :], ALU.mult), ch)
            if i > 0:
                v.wait_ge(sem("g_back"), 4 * i)
                v.wait_ge(sem("g_row"), i)
            v.wait_ge(sem("g_tr"), 3 * i + 3)
            for dst, bank, c in ((q_n, 0, co["q"]), (k_n, 1, rq[:, 1, :]), (k_b, 1, co["kb"]), (q_g, 0, co["qg"]),
                                 (k_bg[:, i], 1, co["kbg"]), (v_b[:, i], 2, gs["beta"][:, i, :]), (k_t[:, i], 1, co["kt"])):
                v.tensor_tensor(dst, ps[:, bank, :].rearrange("p (a b) -> p a b", a=GH), bc(c, 2, GD), ALU.mult).then_inc(sem("g_tok"), 1)
            v.tensor_copy(g_bc, bc(gs["g"][:, i, :], 2, P)).then_inc(sem("g_bc"), 1)

        def gdn_prod_dve(v, i):
            v.wait_ge(sem("g_row"), i + 1)
            for h in range(GH):
                v.scalar_tensor_tensor(dec_m[:, h, :], ps[:, 4, h * P:(h + 1) * P], gs["gc"][:, i, h:h + 1],
                                            ccol("neg"), ALU.subtract, ALU.add).then_inc(sem("g_diff"), 1)
            v.wait_ge(sem("g_dec"), i + 1)
            for dst, bank in ((A_T, 7), (QK_T, 3)):
                v.tensor_tensor(dst[:, i], ps[:, bank, :].rearrange("p (a b) -> p a b", a=GH), dec_m, ALU.mult).then_inc(sem("g_at"), 1)
            v.wait_ge(sem("g_at"), 2 * i + 2)
            link(v, v.tensor_tensor(U_m[:, i], A_T[:, i], bc(ccol("m1"), 1, GH), ALU.mult), "dve_step")
            v.tensor_tensor(U_m[:, i], bc(ident, 1, GH), U_m[:, i], ALU.subtract).then_inc(sem("g_u"), 1)

        LEVELS = 5

        def solve_masks_pool(g):
            for l in range(LEVELS):
                for i in range(TT):
                    if l == 0:
                        g.wait_ge(sem("g_u"), TT)
                    else:
                        g.wait_ge(sem("sv_y"), (l - 1) * TT + i + 1)
                    g.tensor_tensor(A_l[:, i], A_T[:, i], bc(ccol(f"m{l + 2}"), 1, GH), ALU.mult).then_inc(sem("sv_mask"), 1)

        def solve_pe(pe):
            for i in range(TT):
                pe.wait_ge(sem("g_u"), TT)
                if i >= 2:
                    pe.wait_ge(sem("sv_t0"), i - 1)
                for h in range(GH):
                    ins = pe.transpose(ps[:, i % 2, h * P:(h + 1) * P], U_m[:, i, h, :], ident)
                ins.then_inc(sem("sv_tr"), 1)
            for l in range(LEVELS):
                for i in range(TT):
                    n = l * TT + i
                    pe.wait_ge(sem("sv_mask"), n + 1)
                    if l == 0:
                        pe.wait_ge(sem("sv_t0"), min(i + 3, TT))
                    else:
                        pe.wait_ge(sem("sv_t"), n - TT + 1)
                    if n >= 2:
                        pe.wait_ge(sem("sv_yc"), n - 1)
                    for h in range(GH):
                        ins = pe.matmul(ps[:, n % 2, h * P:(h + 1) * P], A_l[:, i, h, :], T_m[:, i, h, :], start=True, stop=True)
                    ins.then_inc(sem("sv_y"), 1)
                for i in range(TT):
                    n = l * TT + i
                    pe.wait_ge(sem("sv_yc"), n + 1)
                    if l > 0:
                        pe.wait_ge(sem("sv_u"), n - TT + 1)
                    if n >= 3:
                        pe.wait_ge(sem("sv_u"), n - 2)
                    for h in range(GH):
                        ins = pe.matmul(ps[:, 2 + n % 3, h * P:(h + 1) * P], Y_m[:, i, h, :], U_m[:, i, h, :], start=True, stop=True)
                    if l < LEVELS - 1:
                        if n >= 3:
                            pe.wait_ge(sem("sv_t"), n - 2)
                        for h in range(GH):
                            ins = pe.matmul(ps[:, 5 + n % 3, h * P:(h + 1) * P], U_m[:, i, h, :], Y_m[:, i, h, :], start=True, stop=True)
                    ins.then_inc(sem("sv_d"), 1)

        def solve_act(a):
            for i in range(TT):
                a.wait_ge(sem("sv_tr"), i + 1)
                a.activation(flat3(T_m[:, i]), ps[:, i % 2, :], ACT.Copy).then_inc(sem("sv_t0"), 1)
            for n in range(LEVELS * TT):
                a.wait_ge(sem("sv_y"), n + 1)
                if n >= TT:
                    a.wait_ge(sem("sv_d"), n - TT + 1)
                a.activation(flat3(Y_m[:, n % TT]), ps[:, n % 2, :], ACT.Copy).then_inc(sem("sv_yc"), 1)

        def solve_dve(v):
            for n in range(LEVELS * TT):
                i = n % TT
                v.wait_ge(sem("sv_d"), n + 1)
                if n >= TT:
                    v.wait_ge(sem("sv_u"), n - TT + 1)
                v.tensor_tensor(flat3(U_m[:, i]), flat3(U_m[:, i]), ps[:, 2 + n % 3, :], ALU.subtract).then_inc(sem("sv_u"), 1)
                if n < (LEVELS - 1) * TT:
                    v.tensor_tensor(flat3(T_m[:, i]), flat3(T_m[:, i]), ps[:, 5 + n % 3, :], ALU.subtract).then_inc(sem("sv_t"), 1)

        def uw_pe(pe):
            pe.wait_ge(sem("sv_u"), LEVELS * TT)
            for i in range(TT):
                for h in range(GH):
                    ins = pe.matmul(ps[:, 2 * i, h * P:(h + 1) * P], U_m[:, i, h, :], v_b[:, i, h, :], start=True, stop=True)
                ins.then_inc(sem("uw"), 1)
                for h in range(GH):
                    ins = pe.matmul(ps[:, 2 * i + 1, h * P:(h + 1) * P], k_bg[:, i, h, :], U_m[:, i, h, :], start=True, stop=True)
                ins.then_inc(sem("uw"), 1)

        def uw_act(a):
            for i in range(TT):
                a.wait_ge(sem("uw"), 2 * i + 1)
                a.activation(flat3(u_n[:, i]), ps[:, 2 * i, :], ACT.Copy).then_inc(sem("u_c"), 1)

        def uw_dve(v):
            v.memset(state, 0.0).then_inc(sem("s_new"), 1)
            for i in range(TT):
                v.wait_ge(sem("uw"), 2 * i + 2)
                v.tensor_copy(flat3(wk_T[:, i]), ps[:, 2 * i + 1, :]).then_inc(sem("wk_c"), 1)

        def rec_pe(pe):
            for c in range(NCH):
                i, r = c // 2, slice(64 * (c % 2), 64 * (c % 2) + 64)
                pe.wait_ge(sem("s_new"), 1 + GH * c)
                if c == 0:
                    pe.wait_ge(sem("u_c"), TT)
                    pe.wait_ge(sem("wk_c"), TT)
                for h in range(GH):
                    ins = pe.matmul(ps[r, c % 2, h * P:(h + 1) * P], wk_T[:, i, h, r], state[:, h, :], start=True, stop=True)
                ins.then_inc(sem("r_ws"), 1)
                if c >= 2:
                    pe.wait_ge(sem("r_o"), c - 1)
                for h in range(GH):
                    pe.matmul(ps[r, 2 + c % 2, h * P:(h + 1) * P], q_gT[:, i, h, r], state[:, h, :], start=(h == 0), stop=False,
                              skip_group_check=True)
                pe.wait_ge(sem("r_w"), c + 1)
                for h in range(GH):
                    ins = pe.matmul(ps[:, 4 + c % 2, h * P:(h + 1) * P], k_t[r, i, h, :], w_c[r, c % 2, h * P:(h + 1) * P], start=True, stop=True)
                ins.then_inc(sem("r_kw"), 1)
                for h in range(GH):
                    ins = pe.matmul(ps[r, 2 + c % 2, h * P:(h + 1) * P], QK_T[r, i, h, r], w_c[r, c % 2, h * P:(h + 1) * P],
                                    start=False, stop=True, skip_group_check=True)
                ins.then_inc(sem("r_om"), 1)

        def rec_dve(v):
            for c in range(NCH):
                i, r = c // 2, slice(64 * (c % 2), 64 * (c % 2) + 64)
                v.wait_ge(sem("r_ws"), c + 1)
                if c == 0:
                    v.wait_ge(sem("u_c"), TT)
                if c >= 2:
                    v.wait_ge(sem("r_om"), c - 1)
                v.tensor_tensor(w_c[r, c % 2, :], flat3(u_n[r, i]), ps[r, c % 2, :], ALU.subtract).then_inc(sem("r_w"), 1)
                v.wait_ge(sem("r_kw"), c + 1)
                v.wait_ge(sem("s_new"), 1 + GH * c)
                for h in range(GH):
                    v.scalar_tensor_tensor(state[:, h, :], state[:, h, :], dec[:, c % 2, i * GH + h:i * GH + h + 1],
                                                ps[:, 4 + c % 2, h * P:(h + 1) * P], ALU.mult, ALU.add).then_inc(sem("s_new"), 1)

        def rec_act(a):
            for c in range(NCH):
                i, r = c // 2, slice(64 * (c % 2), 64 * (c % 2) + 64)
                a.wait_ge(sem("r_om"), c + 1)
                a.activation(flat3(o_t[r, i]), ps[r, 2 + c % 2, :], ACT.Copy).then_inc(sem("r_o"), 1)

        def gout_act(a):
            for i in range(TT):
                a.wait_ge(sem("r_o"), 2 * i + 2)
                a.activation(A_l[:, i], o_t[:, i], ACT.Square).then_inc(sem("go_sq"), 1)
            a.wait_ge(sem("go_ss"), 4)
            a.activation(gs["r_o"], gs["ss_o"], ACT.Sqrt, bias=pcol("eps"), scale=1.0 / GD).then_inc(sem("go_rt"), 1)

        def gout_dve(v):
            for i in range(TT):
                v.wait_ge(sem("go_sq"), i + 1)
                v.tensor_reduce(gs["ss_o"][:, i, :], A_l[:, i], AX, ALU.add).then_inc(sem("go_ss"), 1)
            v.wait_ge(sem("go_rt"), 1)
            link(v, v.reciprocal(gs["r_o"], gs["r_o"]), "dve_step")
            for i in range(TT):
                v.tensor_tensor(o_t[:, i], o_t[:, i], bc(gs["r_o"][:, i, :], 2, GD), ALU.mult).then_inc(sem("go_n"), 1)
            for h in range(GH):
                v.wait_ge(sem("go_tr"), h + 1)
                v.scalar_tensor_tensor(catT[:, 4 + h, :], ps[:, 4 + h, :], pcol("gdn_g"), gateT[:, h, :], ALU.mult, ALU.mult).then_inc(sem("gdn_done"), 1)

        def gout_pe(pe):
            pe.wait_ge(sem("s_new"), 1 + GH * NCH)
            pe.wait_ge(sem("go_n"), TT)
            for h in range(GH):
                for i in range(TT):
                    ins = pe.transpose(ps[:, 4 + h, i * P:(i + 1) * P], o_t[:, i, h, :], ident)
                ins.then_inc(sem("go_tr"), 1)

        def xres_sp(sp):
            sp.wait_ge(sem("g_at"), 2 * TT)
            sp.wait_ge(sem("g_row"), TT)
            sp.dma_start(x, A["x"].rearrange("(i p) n -> p i n", p=P)).then_inc(sem("x_in"), 16)

        low = Space(base, hT_at)
        high = Space(arena, top)
        hT = low(KT, SEQ)
        low_b = low.at
        low_c = low.at + 4096
        high_a = high(4096)
        high_b = high(4096)
        high_c = high(4096)
        high_d = high(4096)
        high_e = high(4096)
        high_f = high(4096)
        rows = lambda v, n=TT: v[:, 0:n * D].rearrange("p (i n) -> p i n", i=n)
        feat = lambda v: v.rearrange("p (k n) -> p k n", k=KT)
        h_rows = rows(high_a)
        q_rows = h_rows
        qT = feat(high_b)
        oT = feat(high_c)
        xk_rows = rows(reg(low_b, 2048), MT)
        xk_T = reg(low_b + 2048, KT, N_MEM)
        xv = reg(low_c, MT, D)
        p_x = [reg(arena + 3 * 4096 + 1024 * n, TT, N_MEM) for n in range(2)]
        pT_x = [reg(arena + 3 * 4096 + 2048 + 1024 * n, MT, SEQ) for n in range(2)]
        xs = Space(arena + 4 * 4096, arena + 5 * 4096)
        sq_junk = xs(1024)
        kss, kr = xs(MT, XH), xs(MT, XH)
        qss, qr = xs(TT, XH), xs(TT, XH)
        nmax = xs(2, TT)
        psum_x = xs(2, TT)
        prec = xs(2, TT)
        mem_x = rows(high_f, MT)
        qr_c, kr_c = xs(TT, CH), xs(TT, CH)
        c_sq = xs(2, 512)

        def mem_sp(sp):
            sp.wait_ge(sem("gdn_done"), GH)
            sp.dma_start(mem_x, A["mem"].rearrange("(i p) n -> p i n", p=P)).then_inc(sem("mem_in"), 16)

        def kv_pe(pe, l):
            t = f"kv{l}"
            for j in range(4):
                w = full(take(pe, f"kv{l}{j}"))
                for i in range(MT):
                    for k in range(KT):
                        ins = pe.matmul(ps[:, 2 * j + i, :], memT[:, k, i * P:(i + 1) * P], w[:, k, :], start=(k == 0), stop=(k == KT - 1))
                    if i == 0:
                        ins.then_inc(sem(f"{t}_mm"), 1)
                    else:
                        ins.then_inc(panel_used, 1)

        def kv_wait(eng, l, j, i):
            if i == 0:
                eng.wait_ge(sem(f"kv{l}_mm"), after(f"kv{l}_mm", j + 1))
            else:
                eng.wait_ge(panel_used, where[f"kv{l}{j}"] + 1)

        def kv_act(a, l):
            t = f"kv{l}"
            for j in range(2):
                for i in range(MT):
                    kv_wait(a, l, j, i)
                    b = ps[:, 2 * j + i, :]
                    for h in range(2):
                        n = 4 * j + 2 * i + h
                        if n >= 4:
                            a.wait_ge(sem(f"{t}_sq"), after(f"{t}_sq", n - 3))
                        a.activation(sq_junk[:, (n % 4) * 256:(n % 4 + 1) * 256], b[:, h * 256:(h + 1) * 256], ACT.Square,
                                          accum_out=kss[:, i, 2 * j + h:2 * j + h + 1]).then_inc(sem(f"{t}_sq"), 1)
            a.wait_ge(sem(f"{t}_sq"), after(f"{t}_sq", 8))
            a.activation(kr, kss, ACT.Sqrt, bias=pcol("eps"), scale=1.0 / XD).then_inc(sem(f"{t}_rt"), 1)
            for i in range(MT):
                kv_wait(a, l, 2, i)
                a.activation(xv[:, i, 0:512], ps[:, 4 + i, :], ACT.Copy).then_inc(sem(f"{t}_v"), 1)
            for i in range(MT):
                kv_wait(a, l, 3, i)
                a.activation(xv[:, i, 512:1024], ps[:, 6 + i, :], ACT.Copy).then_inc(sem(f"{t}_v"), 1)
            for k in range(0, KT, 2):
                a.wait_ge(sem(f"{t}_turned"), after(f"{t}_turned", k + 1))
                a.activation(xk_T[:, k, :], ps[:, k, 0:N_MEM], ACT.Copy, scale=pcol(f"xk_g{l}", 0)).then_inc(sem(f"{t}_kTa"), 1)

        def kv_dve(v, l):
            t = f"kv{l}"
            v.wait_ge(sem(f"{t}_rt"), after(f"{t}_rt", 1))
            link(v, v.reciprocal(kr, kr), "dve_step")
            for j in range(2):
                for i in range(MT):
                    v.tensor_tensor(xk_rows[:, i, j * 512:(j + 1) * 512].rearrange("p (h n) -> p h n", h=2),
                                         ps[:, 2 * j + i, :].rearrange("p (h n) -> p h n", h=2),
                                         bc(kr[:, i, 2 * j:2 * j + 2], 2, XD), ALU.mult).then_inc(sem(f"{t}_k"), 1)
            for k in range(1, KT, 2):
                v.wait_ge(sem(f"{t}_turned"), after(f"{t}_turned", k + 1))
                v.tensor_scalar(xk_T[:, k, :], ps[:, k, 0:N_MEM], pcol(f"xk_g{l}", 1), None, ALU.mult).then_inc(sem(f"{t}_kTv"), 1)

        def kv_turn_pe(pe, l):
            t = f"kv{l}"
            pe.wait_ge(sem(f"{t}_k"), after(f"{t}_k", 4))
            pe.wait_ge(sem(f"{t}_v"), after(f"{t}_v", 4))
            for k in range(KT):
                for i in range(MT):
                    ins = pe.transpose(ps[:, k, i * P:(i + 1) * P], xk_rows[:, i, k * P:(k + 1) * P], ident)
                ins.then_inc(sem(f"{t}_turned"), 1)

        def proj_wait(eng, t, names, per, j, i):
            if i < per - 1:
                eng.wait_ge(sem(f"{t}_mm"), after(f"{t}_mm", j * (per - 1) + i + 1))
            else:
                eng.wait_ge(panel_used, where[names[j]] + 1)

        def xq_pe(pe, l):
            t = f"xq{l}"
            for j in range(2):
                w = full(take(pe, f"xq{l}{j}"))
                for i in range(TT):
                    pe.wait_ge(sem(f"x{l}_out{'av'[(4 * j + i) % 2]}"), after(f"x{l}_out{'av'[(4 * j + i) % 2]}", (4 * j + i) // 2 + 1))
                    for k in range(KT):
                        if j == 0 and i == 0:
                            ready_T(pe, f"x{l}", k)
                        ins = pe.matmul(ps[:, 4 * j + i, :], hT[:, k, i * P:(i + 1) * P], w[:, k, :], start=(k == 0), stop=(k == KT - 1))
                    if i < TT - 1:
                        ins.then_inc(sem(f"{t}_mm"), 1)
                    else:
                        ins.then_inc(panel_used, 1)
            for k in range(KT):
                for i in range(TT):
                    pe.wait_ge(sem(f"{t}_q"), after(f"{t}_q", 8))
                    ins = pe.transpose(ps[:, k, i * P:(i + 1) * P], q_rows[:, i, k * P:(k + 1) * P], ident)
                ins.then_inc(sem(f"{t}_turned"), 1)

        def xq_act(a, l):
            t = f"xq{l}"
            names = [f"xq{l}0", f"xq{l}1"]
            for j in range(2):
                for i in range(TT):
                    proj_wait(a, t, names, TT, j, i)
                    for h in range(2):
                        n = 8 * j + 2 * i + h
                        if n >= 4:
                            a.wait_ge(sem(f"{t}_sq"), after(f"{t}_sq", n - 3))
                        a.activation(sq_junk[:, (n % 4) * 256:(n % 4 + 1) * 256], ps[:, 4 * j + i, h * 256:(h + 1) * 256], ACT.Square,
                                          accum_out=qss[:, i, 2 * j + h:2 * j + h + 1]).then_inc(sem(f"{t}_sq"), 1)
            a.wait_ge(sem(f"{t}_sq"), after(f"{t}_sq", 16))
            a.activation(qr, qss, ACT.Sqrt, bias=pcol("eps"), scale=1.0 / XD).then_inc(sem(f"{t}_rt"), 1)
            for k in range(0, KT, 2):
                a.wait_ge(sem(f"{t}_turned"), after(f"{t}_turned", k + 1))
                a.activation(qT[:, k, :], ps[:, k, :], ACT.Copy, scale=pcol(f"xq_g{l}", 0)).then_inc(sem(f"{t}_qTa"), 1)

        def xq_dve(v, l):
            t = f"xq{l}"
            v.wait_ge(sem(f"{t}_rt"), after(f"{t}_rt", 1))
            link(v, v.reciprocal(qr, qr), "dve_step")
            link(v, v.tensor_scalar(qr, qr, XD ** -0.5, None, ALU.mult), "dve_step")
            for j in range(2):
                for i in range(TT):
                    v.tensor_tensor(q_rows[:, i, j * 512:(j + 1) * 512].rearrange("p (h n) -> p h n", h=2),
                                         ps[:, 4 * j + i, :].rearrange("p (h n) -> p h n", h=2),
                                         bc(qr[:, i, 2 * j:2 * j + 2], 2, XD), ALU.mult).then_inc(sem(f"{t}_q"), 1)
            for k in range(1, KT, 2):
                v.wait_ge(sem(f"{t}_turned"), after(f"{t}_turned", k + 1))
                v.tensor_scalar(qT[:, k, :], ps[:, k, :], pcol(f"xq_g{l}", 1), None, ALU.mult).then_inc(sem(f"{t}_qTv"), 1)

        def xa_scores_pe(pe, l, h):
            t = f"xa{l}"
            if h == 0:
                for k in range(KT):
                    pe.wait_ge(sem(f"xq{l}_qT{'av'[k % 2]}"), after(f"xq{l}_qT{'av'[k % 2]}", k // 2 + 1))
                    pe.wait_ge(sem(f"kv{l}_kT{'av'[k % 2]}"), after(f"kv{l}_kT{'av'[k % 2]}", k // 2 + 1))
            if h >= 2:
                pe.wait_ge(sem(f"{t}_exp"), after(f"{t}_exp", TT * (h - 1)))
            for i in range(TT):
                for d in range(2):
                    ins = pe.matmul(ps[:, 2 * (h % 2) + i // 2, (i % 2) * 256:(i % 2) * 256 + 256],
                                    qT[:, 2 * h + d, i * P:(i + 1) * P], xk_T[:, 2 * h + d, :], start=(d == 0), stop=(d == 1))
            ins.then_inc(sem(f"{t}_s"), 1)

        def xa_values_pe(pe, l, h):
            t = f"xa{l}"
            pe.wait_ge(sem(f"{t}_p"), after(f"{t}_p", h + 1))
            if h > 0:
                pe.wait_ge(sem(f"{t}_pTa"), after(f"{t}_pTa", h))
                pe.wait_ge(sem(f"{t}_pTv"), after(f"{t}_pTv", h))
            for s in range(MT):
                for i in range(TT):
                    ins = pe.transpose(ps[:, 4 + s, i * P:(i + 1) * P], p_x[h % 2][:, i, s * P:(s + 1) * P], ident)
                ins.then_inc(sem(f"{t}_tr"), 1)
            pe.wait_ge(sem(f"{t}_pTa"), after(f"{t}_pTa", h + 1))
            pe.wait_ge(sem(f"{t}_pTv"), after(f"{t}_pTv", h + 1))
            if h > 0:
                pe.wait_ge(sem(f"{t}_oa"), after(f"{t}_oa", h))
                pe.wait_ge(sem(f"{t}_ov"), after(f"{t}_ov", h))
            for d in range(2):
                for s in range(MT):
                    ins = pe.matmul(ps[:, 6 + d, :], xv[:, s, h * XD + d * P:h * XD + (d + 1) * P], pT_x[h % 2][:, s, :], start=(s == 0), stop=(s == 1))
                ins.then_inc(sem(f"{t}_o"), 1)

        def xa_act(a, l):
            t = f"xa{l}"

            def exps(h):
                a.wait_ge(sem(f"{t}_max"), after(f"{t}_max", h + 1))
                if h >= 2:
                    a.wait_ge(sem(f"{t}_tr"), after(f"{t}_tr", 2 * (h - 1)))
                for i in range(TT):
                    a.activation(p_x[h % 2][:, i, :], ps[:, 2 * (h % 2) + i // 2, (i % 2) * 256:(i % 2) * 256 + 256], ACT.Exp,
                                      bias=nmax[:, h % 2, i:i + 1], accum_out=psum_x[:, h % 2, i:i + 1]).then_inc(sem(f"{t}_exp"), 1)
            exps(0)
            for h in range(XH):
                if h + 1 < XH:
                    exps(h + 1)
                a.wait_ge(sem(f"{t}_tr"), after(f"{t}_tr", 2 * h + 1))
                if h >= 2:
                    a.wait_ge(sem(f"{t}_o"), after(f"{t}_o", 2 * (h - 1)))
                a.activation(pT_x[h % 2][:, 0, :], ps[:, 4, :], ACT.Copy).then_inc(sem(f"{t}_pTa"), 1)
                a.wait_ge(sem(f"{t}_o"), after(f"{t}_o", 2 * h + 1))
                a.activation(oT[:, 2 * h, :], ps[:, 6, :], ACT.Copy).then_inc(sem(f"{t}_oa"), 1)

        def xa_dve(v, l):
            t = f"xa{l}"

            def maxes(h):
                v.wait_ge(sem(f"{t}_s"), after(f"{t}_s", h + 1))
                v.tensor_reduce(nmax[:, h % 2, :], ps[:, 2 * (h % 2):2 * (h % 2) + 2, :].rearrange("p b (i n) -> p (b i) n", i=2),
                                     AX, ALU.max, negate=True).then_inc(sem(f"{t}_max"), 1)
            maxes(0)
            for h in range(XH):
                if h + 1 < XH:
                    if h >= 1:
                        v.wait_ge(sem(f"{t}_exp"), after(f"{t}_exp", TT * h))
                    maxes(h + 1)
                v.wait_ge(sem(f"{t}_exp"), after(f"{t}_exp", TT * (h + 1)))
                link(v, v.reciprocal(prec[:, h % 2, :], psum_x[:, h % 2, :]), "dve_step")
                v.tensor_tensor(p_x[h % 2], p_x[h % 2], bc(prec[:, h % 2, :], 2, N_MEM), ALU.mult).then_inc(sem(f"{t}_p"), 1)
                v.wait_ge(sem(f"{t}_tr"), after(f"{t}_tr", 2 * h + 2))
                if h >= 2:
                    v.wait_ge(sem(f"{t}_o"), after(f"{t}_o", 2 * (h - 1)))
                v.tensor_copy(pT_x[h % 2][:, 1, :], ps[:, 5, :]).then_inc(sem(f"{t}_pTv"), 1)
                v.wait_ge(sem(f"{t}_o"), after(f"{t}_o", 2 * h + 2))
                v.tensor_copy(oT[:, 2 * h + 1, :], ps[:, 7, :]).then_inc(sem(f"{t}_ov"), 1)

        def xa_pe(pe, l):
            xa_scores_pe(pe, l, 0)
            for h in range(XH):
                if h + 1 < XH:
                    xa_scores_pe(pe, l, h + 1)
                xa_values_pe(pe, l, h)

        aT = reg(arena, FT, SEQ)
        gsil = reg(low_b, 4, 512)

        def ffn_up_panel_pe(pe, l, w, half, first):
            for c in range(2):
                for gu in range(2):
                    for k in range(KT):
                        if first and c == 0 and gu == 0:
                            ready_T(pe, f"f{l}", k)
                        ins = pe.matmul(ps[:, 4 * half + 2 * c + gu, :], w[:, k, gu * 256 + c * P:gu * 256 + (c + 1) * P], hT[:, k, :],
                                        start=(k == 0), stop=(k == KT - 1))
                if c == 0:
                    ins.then_inc(sem(f"f{l}_mm"), 1)
                else:
                    ins.then_inc(panel_used, 1)

        def ffn_up_pe(pe, l):
            n0 = where[f"gu{l}_0"]
            s0 = n0 % 2
            with pe.Fori(0, FPAN // 2) as j:
                for half in range(2):
                    s = (s0 + half) % 2
                    pe.wait_ge(slot_landed[s], j * 32 + landed[n0 + half])
                    pe.wait_ge(sem(f"f{l}_free"), after(f"f{l}_free", j * 4 + 2 * half + 2))
                    ffn_up_panel_pe(pe, l, full(slots[s]), half, False)
            n = n0 + FPAN - 1
            pe.wait_ge(slot_landed[n % 2], landed[n])
            pe.wait_ge(sem(f"f{l}_free"), after(f"f{l}_free", 2 * (FPAN - 1) + 2))
            ffn_up_panel_pe(pe, l, full(slots[n % 2]), 0, False)

        def ffn_up_act(a, l):
            def body(j, half, c, static=None):
                if c == 0:
                    a.wait_ge(sem(f"f{l}_mm"), after(f"f{l}_mm", j * 2 + half + 1))
                else:
                    a.wait_ge(panel_used, j * 2 + half + where[f"gu{l}_0"] + 1)
                a.wait_ge(sem(f"f{l}_free"), after(f"f{l}_free", j * 4 + 2 * half + c + 1))
                a.activation(gsil[:, 2 * half + c, :], ps[:, 4 * half + 2 * c, :], ACT.Silu).then_inc(sem(f"f{l}_silu"), 1)
            with a.Fori(0, FPAN // 2) as j:
                for half in range(2):
                    for c in range(2):
                        body(j, half, c)
            for c in range(2):
                body(FPAN // 2, 0, c)

        def ffn_up_dve(v, l):
            def body(j, half, c):
                v.wait_ge(sem(f"f{l}_silu"), after(f"f{l}_silu", j * 4 + 2 * half + c + 1))
                if isinstance(j, int):
                    o = aT[:, 4 * j + 2 * half + c, :]
                else:
                    o = sb[:, bass.ds(j * 2048 + (arena + (2 * half + c) * SEQ), SEQ)]
                v.tensor_tensor(o, gsil[:, 2 * half + c, :], ps[:, 4 * half + 2 * c + 1, :], ALU.mult).then_inc(sem(f"f{l}_free"), 1)
            with v.Fori(0, FPAN // 2) as j:
                for half in range(2):
                    for c in range(2):
                        body(j, half, c)
            for c in range(2):
                body(FPAN // 2, 0, c)

        def ffn_down_pe(pe, l):
            pe.wait_ge(sem(f"f{l}_free"), after(f"f{l}_free", FFN_OFF + FT))
            for j in range(FT // 2):
                w = full(take(pe, f"dn{l}_{j}"), 2, 1024)
                for kk in range(2):
                    k = 2 * j + kk
                    for half in range(2):
                        for i in range(TT):
                            ins = pe.matmul(ps[:, 4 * half + i, :], aT[:, k, i * P:(i + 1) * P], w[:, kk, half * 512:(half + 1) * 512],
                                            start=(k == 0), stop=(k == FT - 1))
                            if k == FT - 1 and not (half == 1 and i == TT - 1):
                                ins.then_inc(sem(f"d{l}_mm"), 1)
                ins.then_inc(panel_used, 1)

        FFN_OFF = 4

        def down_dve(v, l):
            for half in range(2):
                for i in range(TT):
                    if half == 1 and i == TT - 1:
                        v.wait_ge(panel_used, where[f"dn{l}_{FT // 2 - 1}"] + 1)
                    else:
                        v.wait_ge(sem(f"d{l}_mm"), after(f"d{l}_mm", 4 * half + i + 1))
                    v.tensor_tensor(x[:, i, half * 512:(half + 1) * 512], ps[:, 4 * half + i, :],
                                         x[:, i, half * 512:(half + 1) * 512], ALU.add).then_inc(sem(f"d{l}_x"), 1)

        v_rows = rows(reg(low_b, 4096))
        bias_ring = reg(low_c, 4, BAND_W)
        cs = Space(low_c + 2048, low_c + 4096)
        cq_scaled = cs(1)
        c_tmp = cs(2, CH // 2, CD)
        c_ss, c_rt, c_r = cs(2, CH // 2), cs(2, CH // 2), cs(2, CH // 2)
        c_max, c_neg, c_sum, c_rec = cs(2, TT), cs(2, TT), cs(2, TT), cs(2, TT)
        ck_rows = rows(high_b)
        cqT, ckT = feat(high_c), feat(high_d)
        p_c = [reg(arena + 4 * 4096 + 2048 * n, TT, SEQ) for n in range(2)]
        pT_c = [reg(arena + 5 * 4096 + 2048 * n, TT, SEQ) for n in range(2)]
        c_oT = hT
        ca_names = [f"ca{i}" for i in range(6)]

        def ca_proj_pe(pe):
            for p in range(6):
                w = full(take(pe, f"ca{p}"))
                for i in range(TT):
                    n = 4 * p + i
                    if n < 8:
                        pe.wait_ge(sem(f"c_out{'av'[n % 2]}"), after(f"c_out{'av'[n % 2]}", n // 2 + 1))
                    else:
                        pe.wait_ge(sem("c_rows"), n - 7)
                    for k in range(KT):
                        if n == 0:
                            ready_T(pe, "c", k)
                        ins = pe.matmul(ps[:, n % 8, :], hT[:, k, i * P:(i + 1) * P], w[:, k, :], start=(k == 0), stop=(k == KT - 1))
                    if i < TT - 1:
                        ins.then_inc(sem("ca_mm"), 1)
                    else:
                        ins.then_inc(panel_used, 1)

        def ca_proj_act(a):
            for n in range(16):
                proj_wait(a, "ca", ca_names, TT, n // 4, n % 4)
                if n >= 2:
                    a.wait_ge(sem("c_rows"), n - 1)
                a.activation(c_tmp[:, n % 2].rearrange("p a b -> p (a b)"), ps[:, n % 8, :], ACT.Square).then_inc(sem("c_sqs"), 1)
                a.wait_ge(sem("c_ss"), n + 1)
                a.activation(c_rt[:, n % 2, :], c_ss[:, n % 2, :], ACT.Sqrt, bias=pcol("eps"), scale=1.0 / CD).then_inc(sem("ca_root"), 1)
            for n in range(16, 24):
                proj_wait(a, "ca", ca_names, TT, n // 4, n % 4)
                c0 = (n // 4 - 4) * 512
                a.activation(v_rows[:, n % 4, c0:c0 + 512], ps[:, n % 8, :], ACT.Copy).then_inc(sem("c_v"), 1)

        def ca_proj_dve(v):
            link(v, v.tensor_scalar(cq_scaled, pcol("cq_g"), CD ** -0.5, None, ALU.mult), "c_scale")
            for n in range(16):
                v.wait_ge(sem("c_sqs"), n + 1)
                v.tensor_reduce(c_ss[:, n % 2, :], c_tmp[:, n % 2], AX, ALU.add).then_inc(sem("c_ss"), 1)
                v.wait_ge(sem("ca_root"), n + 1)
                link(v, v.reciprocal(c_r[:, n % 2, :], c_rt[:, n % 2, :]), "dve_step")
                dst = (q_rows if n < 8 else ck_rows)[:, n % 4, (n // 4 % 2) * 512:(n // 4 % 2 + 1) * 512]
                v.tensor_tensor(dst.rearrange("p (h n) -> p h n", n=CD), ps[:, n % 8, :].rearrange("p (h n) -> p h n", n=CD),
                                     bc(c_r[:, n % 2, :], 2, CD), ALU.mult).then_inc(sem("c_rows"), 1)

        def ca_turn_pe(pe):
            for m in range(16):
                if m < 8:
                    pe.wait_ge(sem("c_v"), m + 1)
                    if m == 0:
                        pe.wait_ge(sem("c_rows"), 16)
                else:
                    pe.wait_ge(sem(f"c_T{'av'[m % 2]}"), after(f"c_T{'av'[m % 2]}", (m - 8) // 2 + 1))
                for i in range(TT):
                    ins = pe.transpose(ps[:, m % 8, i * P:(i + 1) * P], (q_rows if m < 8 else ck_rows)[:, i, (m % 8) * P:(m % 8 + 1) * P], ident)
                ins.then_inc(sem("ca_turned"), 1)

        def ca_turn_evac(eng, act):
            for m in range(0 if act else 1, 16, 2):
                eng.wait_ge(sem("ca_turned"), m + 1)
                dst, src = (cqT if m < 8 else ckT)[:, m % 8, :], ps[:, m % 8, :]
                if m < 8:
                    dst, src = dst.rearrange("p (i n) -> p i n", i=TT), src.rearrange("p (i n) -> p i n", i=TT)[:, :, ::-1]
                scale = cq_scaled if m < 8 else pcol("ck_g")
                if act:
                    if m == 0:
                        eng.wait_ge(sem("c_scale"), 1)
                    eng.activation(dst, src, ACT.Copy, scale=scale).then_inc(sem("c_Ta"), 1)
                else:
                    eng.tensor_scalar(dst, src, scale, None, ALU.mult).then_inc(sem("c_Tv"), 1)

        def ca_scores_pe(pe, h):
            r = slice(64 * (h % 2), 64 * (h % 2) + 64)
            if h == 0:
                pe.wait_ge(sem("c_Ta"), 8)
                pe.wait_ge(sem("c_Tv"), 8)
            for i in range(TT):
                if h > 0:
                    pe.wait_ge(sem("c_s2"), 4 * (h - 1) + i + 1)
                n = (i + 1) * P
                pe.matmul(ps[:, i, 0:n], cqT[r, h // 2, i * P:(i + 1) * P], ckT[r, h // 2, 0:n], start=True, stop=True).then_inc(sem("c_s"), 1)

        def ca_values_pe(pe, h):
            r = slice(64 * (h % 2), 64 * (h % 2) + 64)
            for s in range(TT):
                m = 4 * h + s
                if m >= 3:
                    pe.wait_ge(sem(COPY[(m - 3) % 4][0]), 2 * ((m - 3) // 4) + COPY[(m - 3) % 4][1])
                for i in range(s, TT):
                    if s == 0:
                        pe.wait_ge(sem("c_p"), 4 * h + i + 1)
                    ins = pe.transpose(ps[:, 4 + m % 3, i * P:(i + 1) * P], p_c[h % 2][:, i, s * P:(s + 1) * P], ident)
                ins.then_inc(sem("c_tr"), 1)
            if h > 0:
                pe.wait_ge(sem("c_oc"), h)
            for s in range(TT):
                pe.wait_ge(sem(COPY[s][0]), 2 * h + COPY[s][1])
                ins = pe.matmul(ps[r, 7, s * P:SEQ], v_rows[:, s, h * CD:(h + 1) * CD], pT_c[h % 2][:, s, s * P:SEQ],
                                start=(s == 0), stop=(s == TT - 1), skip_group_check=True)
            ins.then_inc(sem("c_o"), 1)

        COPY = [("c_pa", 1), ("c_pv", 1), ("c_pv", 2), ("c_pa", 2)]

        def ca_copy(eng, h, s):
            eng.wait_ge(sem("c_tr"), 4 * h + s + 1)
            if h >= 2:
                eng.wait_ge(sem("c_o"), h - 1)
            dst, src = pT_c[h % 2][:, s, s * P:SEQ], ps[:, 4 + (4 * h + s) % 3, s * P:SEQ]
            if COPY[s][0] == "c_pa":
                eng.activation(dst, src, ACT.Copy).then_inc(sem("c_pa"), 1)
            else:
                eng.tensor_copy(dst, src).then_inc(sem("c_pv"), 1)

        def ca_pe(pe):
            ca_scores_pe(pe, 0)
            for h in range(CH):
                if h + 1 < CH:
                    ca_scores_pe(pe, h + 1)
                ca_values_pe(pe, h)

        def ca_sp(sp, h):
            if h == 0:
                sp.wait_ge(sem("c_rows"), 1)
            if h >= 4:
                sp.wait_ge(sem("c_s2"), 4 * (h - 3))
            e = A["rel_rows"]
            src = bass.AP(e.tensor, h * BAND_E, [[1, P], [1, BAND_W]])
            sp.dma_start(bias_ring[:, h % 4, :], src).then_inc(sem(f"bias_in{h % 4}"), 16)

        def ca_pool(g):
            for h in range(CH):
                g.wait_ge(sem("c_rc"), h + 1)
                for i in range(TT):
                    n = (i + 1) * P
                    g.tensor_scalar(p_c[h % 2][:, i, 0:n], p_c[h % 2][:, i, 0:n], c_rec[:, h % 2, i:i + 1], None, ALU.mult).then_inc(sem("c_p"), 1)

        def ca_act(a):
            def exps(h):
                a.wait_ge(sem("c_max"), h + 1)
                for i in range(TT):
                    n = (i + 1) * P
                    a.activation(p_c[h % 2][:, i, 0:n], p_c[h % 2][:, i, 0:n], ACT.Exp, bias=c_neg[:, h % 2, i:i + 1],
                                      accum_out=c_sum[:, h % 2, i:i + 1]).then_inc(sem("c_exp"), 1)
            exps(0)
            for h in range(CH):
                if h + 1 < CH:
                    exps(h + 1)
                ca_copy(a, h, 0)
                ca_copy(a, h, 3)
                a.wait_ge(sem("c_o"), h + 1)
                r = slice(64 * (h % 2), 64 * (h % 2) + 64)
                a.activation(c_oT[r, h // 2, :].rearrange("p (i n) -> p i n", i=TT),
                                  ps[r, 7, :].rearrange("p (i n) -> p i n", i=TT)[:, :, ::-1], ACT.Copy).then_inc(sem("c_oc"), 1)

        def ca_dve(v):
            def sums(h):
                v.wait_ge(sem(f"bias_in{h % 4}"), after(f"bias_in{h % 4}", 16 * (h // 4 + 1)))
                link(v, v.memset(bias_ring[64:P, h % 4, BAND_W - 64:BAND_W], -1e30), "dve_step")
                if h >= 2:
                    v.wait_ge(sem("c_tr"), 4 * (h - 1))
                for i in range(TT):
                    n = (i + 1) * P
                    v.wait_ge(sem("c_s"), 4 * h + i + 1)
                    v.tensor_tensor_reduce(out=p_c[h % 2][:, i, 0:n], in0=ps[:, i, 0:n],
                                                in1=bias_ring[:, h % 4, BAND_W - n:BAND_W], scale=1.0, scalar=-3.0e38,
                                                op0=ALU.add, op1=ALU.max, accum_out=c_max[:, h % 2, i:i + 1]).then_inc(sem("c_s2"), 1)
                v.wait_ge(sem("c_s2"), 4 * h + 4)
                v.tensor_scalar(c_neg[:, h % 2, :], c_max[:, h % 2, :], -1.0, None, ALU.mult).then_inc(sem("c_max"), 1)
            sums(0)
            for h in range(CH):
                v.wait_ge(sem("c_exp"), 4 * h + 4)
                v.reciprocal(c_rec[:, h % 2, :], c_sum[:, h % 2, :]).then_inc(sem("c_rc"), 1)
                if h + 1 < CH:
                    sums(h + 1)
                ca_copy(v, h, 1)
                ca_copy(v, h, 2)

        def load_panel(sp, name):
            n = where[name]
            if n >= 2:
                sp.wait_ge(panel_used, n - 1)
            for dst, src in panels[n][1]:
                sp.dma_start(dst(slots[n % 2]), src).then_inc(slot_landed[n % 2], 16)

        def layer_panels(l):
            return ([f"kv{l}{i}" for i in range(4)] + [f"xq{l}{i}" for i in range(2)] + [f"xo{l}{i}" for i in range(2)]
                    + [f"gu{l}_{i}" for i in range(FPAN)] + [f"dn{l}_{i}" for i in range(FT // 2)])


        block = ctx.enter_context(nc.Block())
        abo, cao = ["abo0", "abo1"], ["cao0", "cao1"]
        xo = [[f"xo{l}0", f"xo{l}1"] for l in range(DEPTH)]

        @block.sync
        def _(sp):
            sp.dma_start(par, A["par"]).then_inc(sem("par_in"), 16)
            sp.dma_start(x0, A["x"].rearrange("(i p) n -> p i n", p=P)).then_inc(sem("x_in"), 16)
            sp.dma_start(con, A["con"]).then_inc(sem("con_in"), 16)
            load_panel(sp, "ab0")
            load_panel(sp, "ab1")
            sp.dma_start(w_ab, A["ab_w_in"][:, 2560:2568].rearrange("(k p) n -> p k n", p=P)).then_inc(sem("wab_in"), 16)
            sp.dma_start(s5_bc, A["s5_bc"]).then_inc(sem("bc_in"), 16)
            for name in ("ab2", "ab3", "ab4", "glu", "abo0"):
                load_panel(sp, name)
                if name == "glu":
                    s5_u_sp(sp)
                    s5_y_sp(sp)
            load_panel(sp, "abo1")
            xres_sp(sp)
            mem_sp(sp)
            for name in layer_panels(0):
                load_panel(sp, name)
            for i in range(6):
                load_panel(sp, f"ca{i}")
            for h in range(4):
                ca_sp(sp, h)
            load_panel(sp, "cao0")
            load_panel(sp, "cao1")
            for h in range(4, CH):
                ca_sp(sp, h)
            for name in layer_panels(1):
                load_panel(sp, name)
            for i in range(TT):
                sp.wait_ge(sem("d1_x"), after("d1_x", TT + i + 1))
                sp.dma_start(A["out"][i * P:(i + 1) * P, :], x[:, i, :]).then_inc(sem("stored"), 16)
            sp.wait_ge(sem("stored"), 16 * TT)

        @block.tensor
        def _(pe):
            pe.wait_ge(sem("con_in"), 16)
            norm_pe(pe, "n0", x0, h0)
            for p in range(4):
                ab_groups_pe(pe, p)
            logits_pe(pe)
            s5_tables_pe(pe)
            ab_groups_pe(pe, 4)
            s5_states_pe(pe)
            s5_out_pe(pe)
            s5_glu_pe(pe)
            gates_pe(pe)
            gdn_turn_pe(pe, 0)
            gdn_back_pe(pe, 0)
            for i in range(TT):
                if i + 1 < TT:
                    gdn_turn_pe(pe, i + 1)
                gdn_prod_pe(pe, i)
                if i + 1 < TT:
                    gdn_back_pe(pe, i + 1)
            solve_pe(pe)
            uw_pe(pe)
            rec_pe(pe)
            gout_pe(pe)

            def cat_ready(k):
                if k == 0:
                    pe.wait_ge(sem("gdn_done"), GH)
            outproj_pe(pe, "mo", abo, catT, cat_ready)
            pe.wait_ge(sem("mo_x"), after("mo_x", 8))
            norm_pe(pe, "m", mem_x, mem_x)
            for l in range(DEPTH):
                if l == 0:
                    for k in range(KT):
                        ready_T(pe, "m", k)
                else:
                    pe.wait_ge(sem("d0_x"), after("d0_x", 8))
                kv_pe(pe, l)
                kv_turn_pe(pe, l)
                pe.wait_ge(sem(f"kv{l}_v"), after(f"kv{l}_v", 4))
                pe.wait_ge(sem(f"kv{l}_kTa"), after(f"kv{l}_kTa", 4))
                pe.wait_ge(sem(f"kv{l}_kTv"), after(f"kv{l}_kTv", 4))
                norm_pe(pe, f"x{l}", x, h_rows)
                xq_pe(pe, l)
                xa_pe(pe, l)

                def o_ready(k):
                    pe.wait_ge(sem(f"xa{l}_o{'av'[k % 2]}"), after(f"xa{l}_o{'av'[k % 2]}", k // 2 + 1))
                pe.wait_ge(sem(f"xa{l}_oa"), after(f"xa{l}_oa", XH))
                pe.wait_ge(sem(f"xa{l}_ov"), after(f"xa{l}_ov", XH))
                outproj_pe(pe, f"xo{l}", xo[l], oT, lambda k: None)
                pe.wait_ge(sem(f"xo{l}_x"), after(f"xo{l}_x", 8))
                norm_pe(pe, f"f{l}", x, h_rows)
                for k in range(KT):
                    ready_T(pe, f"f{l}", k)
                ffn_up_pe(pe, l)
                ffn_down_pe(pe, l)
                if l == 0:
                    pe.wait_ge(sem("d0_x"), after("d0_x", 8))
                    norm_pe(pe, "c", x, h_rows)
                    ca_proj_pe(pe)
                    ca_turn_pe(pe)
                    ca_pe(pe)
                    pe.wait_ge(sem("c_oc"), CH)
                    outproj_pe(pe, "co", cao, c_oT, lambda k: None)
                    pe.wait_ge(sem("co_x"), after("co_x", 8))

        @block.scalar
        def _(a):
            a.wait_ge(sem("x_in"), 16)
            squares_act(a, "n0", x0, sq_junk0, ss2)
            a.wait_ge(sem("par_in"), 16)
            norm_act(a, "n0", x0, h0, ss2, hT0, "ab_g")
            s5_params_act(a)
            for n in range(12):
                silu_act(a, n)
            for n in range(12, 16):
                gate_act(a, n)
            s5_tables_act(a)
            for n in range(16, 20):
                u_act(a, n)
            s5_out_act(a)
            s5_glu_act(a)
            gates_act(a)
            gdn_tok_act(a, 0)
            gdn_back_act(a, 0)
            for i in range(TT):
                if i + 1 < TT:
                    gdn_tok_act(a, i + 1)
                gdn_dec_act(a, i)
                if i + 1 < TT:
                    gdn_back_act(a, i + 1)
            solve_act(a)
            uw_act(a)
            rec_act(a)
            gout_act(a)
            a.wait_ge(sem("mem_in"), 16)
            squares_act(a, "m", mem_x, sq_junk, rms_m)
            norm_act(a, "m", mem_x, mem_x, rms_m, memT, "mem_g")
            squares_act(a, "x0", x, sq_junk, ss2, "mo_x")
            for l in range(DEPTH):
                if l == 1:
                    squares_act(a, "x1", x, sq_junk, ss2, "co_x")
                kv_act(a, l)
                norm_act(a, f"x{l}", x, h_rows, ss2, hT, f"xa_g{l}")
                xq_act(a, l)
                xa_act(a, l)
                squares_act(a, f"f{l}", x, sq_junk, ss2, f"xo{l}_x")
                norm_act(a, f"f{l}", x, h_rows, ss2, hT, f"f_g{l}")
                ffn_up_act(a, l)
                if l == 0:
                    squares_act(a, "c", x, sq_junk, ss2, "d0_x")
                    norm_act(a, "c", x, h_rows, ss2, hT, "c_g")
                    ca_proj_act(a)
                    ca_turn_evac(a, True)
                    ca_act(a)

        @block.vector
        def _(v):
            v.wait_ge(sem("x_in"), 16)
            v.wait_ge(sem("par_in"), 16)
            norm_dve(v, "n0", x0, h0, ss2, hT0, "ab_g")
            v.wait_ge(sem("con_in"), 16)
            for n in range(4):
                conv_dve(v, n)
            s5_g_dve(v)
            for n in range(4, 12):
                conv_dve(v, n)
            logits_dve(v)
            s5_states_dve(v)
            s5_glu_dve(v)
            gates_dve(v)
            gdn_tok_dve(v, 0)
            for i in range(TT):
                if i + 1 < TT:
                    gdn_tok_dve(v, i + 1)
                gdn_prod_dve(v, i)
            solve_dve(v)
            uw_dve(v)
            rec_dve(v)
            gout_dve(v)
            v.wait_ge(sem("x_in"), 32)
            outproj_dve(v, "mo", abo, x)
            norm_dve(v, "m", mem_x, mem_x, rms_m, memT, "mem_g")
            for l in range(DEPTH):
                kv_dve(v, l)
                norm_dve(v, f"x{l}", x, h_rows, ss2, hT, f"xa_g{l}")
                xq_dve(v, l)
                xa_dve(v, l)
                outproj_dve(v, f"xo{l}", xo[l], x)
                norm_dve(v, f"f{l}", x, h_rows, ss2, hT, f"f_g{l}")
                v.memset(prec[:, 0, 0:1], 0.0).then_inc(sem(f"f{l}_free"), FFN_OFF)
                ffn_up_dve(v, l)
                down_dve(v, l)
                if l == 0:
                    norm_dve(v, "c", x, h_rows, ss2, hT, "c_g")
                    ca_proj_dve(v)
                    ca_turn_evac(v, False)
                    ca_dve(v)
                    outproj_dve(v, "co", cao, x)

        @block.gpsimd
        def _(g):
            g.wait_ge(sem("par_in"), 16)
            s5_params_pool(g)
            g.wait_ge(sem("con_in"), 16)
            solve_masks_pool(g)
            ca_pool(g)


def _layout(inputs):
    import numpy as np

    f = {k: np.ascontiguousarray(np.asarray(v)) for k, v in inputs.items()}

    def cols(v):
        return v.reshape(-1, P).T

    gp = lambda a: a.reshape(S5_GP, 2, S5_P).transpose(1, 2, 0).reshape(P, S5_GP)
    ri = lambda a: np.concatenate([a.T, a.T], 0)
    rep = lambda row: np.broadcast_to(row[None, :], (P, row.size))
    both = lambda a: np.concatenate([ri(a), gp(a)], 1)
    ones = np.ones((P, 1), np.float32)
    sgn = np.concatenate([-ones[:64], ones[64:]], 0)
    parts = {
        "ab_g": cols(f["ab_norm_g"][0]), "c_g": cols(f["c_norm_g"][0]), "mem_g": cols(f["mem_norm_g"]),
        "xa_g0": cols(f["xa_norm_g"][0]), "xa_g1": cols(f["xa_norm_g"][1]), "f_g0": cols(f["f_norm_g"][0]), "f_g1": cols(f["f_norm_g"][1]),
        "s5_d": cols(f["s5_d"][0].reshape(-1)), "b_glu": cols(f["s5_b_glu"][0]),
        "conv": f["gdn_conv_w"][0].reshape(4, 12, P).transpose(2, 0, 1).reshape(P, 48),
        "gdn_g": cols(f["gdn_out_norm_g"][0]),
        "xq_g0": cols(f["xa_q_norm_g"][0]), "xq_g1": cols(f["xa_q_norm_g"][1]),
        "xk_g0": cols(f["xa_k_norm_g"][0]), "xk_g1": cols(f["xa_k_norm_g"][1]),
        "cq_g": np.concatenate([f["c_q_norm_g"][0]] * 2)[:, None], "ck_g": np.concatenate([f["c_k_norm_g"][0]] * 2)[:, None],
        "dt_bias": rep(f["gdn_dt_bias"][0]), "a_log": rep(f["gdn_a_log"][0]),
        "a_re": both(f["s5_a_re"][0]), "a_im": both(f["s5_a_im"][0]),
        "log_dt": both(np.broadcast_to(f["s5_log_dt"][0][:, None], (S5_G, S5_P))),
        "eps": ones * EPS, "half_pi": ones * (TWO_PI / 4), "sgn": sgn, "one": ones, "nsgn": -sgn,
    }
    par = np.empty((P, N_PAR), np.float32)
    for name, (at, n) in PAR.items():
        par[:, at:at + n] = parts[name]
    j, t = np.meshgrid(np.arange(P), np.arange(P), indexing="ij")
    same = (j // CHUNK) == (t // CHUNK)
    con = {"ident": j == t, "inc": same & (j <= t), "neg": np.where(same & (j <= t), 0.0, -1e30),
           "same": same, "first": j < CHUNK, "second": j >= CHUNK}
    for l in range(1, 7):
        s = 2 ** (l - 1)
        con[f"m{l}"] = (j // (2 * s) == t // (2 * s)) & (t % (2 * s) >= s) & (j % (2 * s) < s)
    con = np.concatenate([np.asarray(con[n], np.float32) for n in CON], 1)
    bt = [f[n][0].transpose(1, 0, 2) for n in ("s5_b_re", "s5_b_im")]
    ct = [f[n][0].transpose(2, 0, 1) for n in ("s5_c_re", "s5_c_im")]
    cg = [f[n][0].reshape(S5_GP, 2, S5_CH, S5_P).transpose(1, 3, 0, 2).reshape(P, -1) for n in ("s5_c_re", "s5_c_im")]
    s5_bc = np.concatenate([np.concatenate([bt[0], bt[1]], 0).reshape(P, -1), np.concatenate([bt[1], bt[0]], 0).reshape(P, -1),
                            np.concatenate([ct[0], ct[1]], 0).reshape(P, -1), cg[0], cg[1]], 1)
    rel = f["c_rel_bias"][0][:, np.clip(BAND_W - 1 - np.arange(BAND_E), -REL, REL) + REL]
    return {
        "x": f["x"][0], "mem": f["mem"][0], "par": par, "con": con, "s5_bc": s5_bc, "rel_rows": rel,
        "ab_w_in": f["ab_w_in"][0], "ab_w_out": f["ab_w_out"][0], "s5_w_glu": f["s5_w_glu"][0],
        "c_w_qkv": f["c_w_qkv"][0], "c_w_out": f["c_w_out"][0],
        "xa_w_q": f["xa_w_q"], "xa_w_kv": f["xa_w_kv"], "xa_w_out": f["xa_w_out"],
        "f_w_gate": f["f_w_gate"], "f_w_up": f["f_w_up"], "f_w_down": f["f_w_down"],
    }


def kernel(**inputs):
    import numpy as np
    import concourse.bacc as bacc
    from concourse.bass_utils import run_bass_kernel_spmd

    nc = bacc.Bacc("TRN2", target_bir_lowering=False, num_devices=1)
    arrays = {f"in_{k}": np.ascontiguousarray(v) for k, v in _layout(inputs).items()}
    A = {k[3:]: nc.dram_tensor(k, v.shape, mybir.dt.from_np(v.dtype), kind="ExternalInput").ap() for k, v in arrays.items()}
    A["out"] = nc.dram_tensor("out_0", (SEQ, D), F32, kind="ExternalOutput").ap()
    build_program(nc, A)
    r = run_bass_kernel_spmd(nc, [arrays], core_ids=[0])
    return r.results[0]["out_0"].reshape(1, SEQ, D)
```

```python
from contextlib import ExitStack

import concourse.bass as bass
from concourse import mybir

F32 = mybir.dt.float32
F32R = mybir.dt.float32r
ALU = mybir.AluOpType
ACT = mybir.ActivationFunctionType
AX = mybir.AxisListType.X

P = 128
D = 1024
SEQ = 512
N_MEM = 256
DEPTH = 2
KT = D // P
TT = SEQ // P
MT = N_MEM // P
CHUNK = 64
EPS = 1e-6
S5_W = D // 2
S5_CH = 16
S5_G = S5_W // S5_CH
S5_P = 64
S5_L = 8
S5_C = SEQ // S5_L
S5_GP = S5_G // 2
S5_COLS = S5_G + S5_GP
GH = 4
GD = 128
NCH = SEQ // CHUNK
CH = 16
CD = D // CH
XH = 4
XD = D // XH
FH = -(-8 * D // (3 * 256)) * 256
FT = FH // P
REL = 128
BAND_W = SEQ
BAND_E = BAND_W + P - 1

PAR = {}
_at = 0
for _name, _n in (
    ("ab_g", KT), ("c_g", KT), ("mem_g", KT), ("xa_g0", KT), ("xa_g1", KT), ("f_g0", KT), ("f_g1", KT),
    ("s5_d", 4), ("b_glu", 4), ("conv", 48), ("gdn_g", 1), ("xq_g0", 2), ("xq_g1", 2), ("xk_g0", 2), ("xk_g1", 2),
    ("cq_g", 1), ("ck_g", 1), ("dt_bias", GH), ("a_log", GH), ("a_re", S5_COLS), ("a_im", S5_COLS), ("log_dt", S5_COLS),
    ("eps", 1), ("half_pi", 1), ("sgn", 1), ("one", 1), ("nsgn", 1),
):
    PAR[_name] = (_at, _n)
    _at += _n
N_PAR = _at
CON = {n: i * P for i, n in enumerate(["ident", "inc", "neg", "m1", "m2", "m3", "m4", "m5", "m6", "same", "first", "second"])}
N_CON = len(CON) * P
TOP = 53120

TWO_PI = 6.283185307179586
PI_PARTS = (6.28125, 0.0019353071693331003, 1.0253114e-11)
ROUND = 12582912.0


def build_program(nc, A, upto=99, dump=None):
    ctx = ExitStack()
    with ctx:
        def tensor_at(name, at, dtype, *shape):
            assert at % 8 == 0
            with nc.sbuf_tensor(f"below_{name}", [P, at], F32), nc.sbuf_tensor(name, [P, *shape], dtype) as v:
                return v[(slice(None),) * (1 + len(shape))]

        def rounded(name, at, *shape):
            return tensor_at(name, at, F32R, *shape)

        with nc.sbuf_tensor("params", [P, N_PAR], F32) as par:
            par = par[:, :]
        memT = tensor_at("memT", N_PAR, F32, KT, N_MEM)
        SB0 = N_PAR + KT * N_MEM
        sb = tensor_at("sb", SB0, F32, TOP - SB0)
        ps = ctx.enter_context(nc.psum_tensor("ps", [P, 8, 512], F32))
        sems = {}

        PER_LAYER = {
            "kv_sq": 8, "kv_rt": 1, "kv_v": 4, "kv_kTa": 4, "kv_k": 4, "kv_kTv": 4, "kv_turned": 8,
            "xq_sq": 16, "xq_rt": 2, "xq_qTa": 4, "xq_q": 8, "xq_qTv": 4, "xq_turned": 8,
            "xa_s": 4, "xa_exp": 16, "xa_max": 4, "xa_p": 4, "xa_tr": 8, "xa_pTa": 4, "xa_pTv": 4,
            "xa_o": 8, "xa_oa": 8, "xa_ov": 8,
            "f_mm": FT, "f_silu": FT, "f_free": FT + 2, "f_ahi": FT, "f_alo": FT + 2,
        }
        SERIES = {"norm": ("n0", "m", "x0", "f0", "c", "x1", "f1"), "back": ("mo", "kv0", "xq0", "xo0", "d0", "ca", "co", "kv1", "xq1", "xo1", "d1")}

        PLAIN = ("n0", "m")

        def in_series(what, tail, tag):
            if what == "back":
                if tail == "mm":
                    return {"kv": 4 * (MT - 1), "ca": 6 * (TT - 1), "d": 2 * TT - 1}.get(tag.rstrip("01"), 2 * (TT - 1))
                return 2 * TT if tail == "x" and tag.rstrip("01") in ("mo", "xo", "d", "co") else None
            n = MT if tag == "m" else TT
            return {"sq": 2 * n, "sum": 1, "root": 1, "rinv": 1, "hv": n // 2 if tag in PLAIN else n, "ha": n // 2 if tag in PLAIN else 0,
                    "turned": KT, "outa": KT // 2 if tag in PLAIN else KT, "outv": KT // 2 if tag in PLAIN else KT}.get(tail)

        def named(name):
            head, _, tail = name.partition("_")
            for what, tags in SERIES.items():
                if head in tags and in_series(what, tail, head) is not None:
                    return f"{what}_{tail}", sum(in_series(what, tail, t) or 0 for t in tags[:tags.index(head)])
            if head[-1].isdigit() and f"{head[:-1]}_{tail}" in PER_LAYER:
                base_name = f"{head[:-1]}_{tail}"
                return base_name, int(head[-1]) * PER_LAYER[base_name]
            return name, 0

        def sem(name):
            name = named(name)[0]
            if name not in sems:
                sems[name] = ctx.enter_context(nc.semaphore(name))
            return sems[name]

        def reg(at, *shape):
            n = 1
            for s in shape:
                n *= s
            v = sb[:, at - SB0:at - SB0 + n]
            if len(shape) == 2:
                v = v.rearrange("p (a b) -> p a b", a=shape[0])
            if len(shape) == 3:
                v = v.rearrange("p (a b c) -> p a b c", a=shape[0], b=shape[1])
            if len(shape) == 4:
                v = v.rearrange("p (a b c d) -> p a b c d", a=shape[0], b=shape[1], c=shape[2])
            return v

        class Space:
            def __init__(self, at, end):
                self.at, self.end = at, end

            def __call__(self, *shape):
                n = 1
                for s in shape:
                    n *= s
                v = reg(self.at, *shape)
                self.at += n
                assert self.at <= self.end, (self.at, self.end)
                return v

        fixed = Space(SB0, 14900)
        con = fixed(N_CON)
        slots_at = fixed.at
        slots = [fixed(4096), fixed(4096)]
        ss2 = fixed(2, TT)
        nrm = fixed(2, TT)
        rinv = fixed(TT)
        spare = fixed(2)
        warm = fixed(1)
        rms_m = fixed(3, MT)
        top = TOP
        base = -(-fixed.at // 8) * 8

        def pcol(name, i=0):
            return par[:, PAR[name][0] + i:PAR[name][0] + i + 1]

        def pcols(name):
            return par[:, PAR[name][0]:PAR[name][0] + PAR[name][1]]

        def ccol(name):
            return con[:, CON[name]:CON[name] + P]

        ident = ccol("ident")

        panels = []

        def kview(w, c0, n, k0=0, nk=KT):
            return w[k0 * P:(k0 + nk) * P, c0:c0 + n].rearrange("(k p) n -> p k n", p=P)

        def full(slot, nk=KT, n=512):
            return slot[:, 0:nk * n].rearrange("p (k n) -> p k n", k=nk)

        def add_panel(name, parts):
            panels.append((name, parts))

        def add_full(name, w, c0):
            add_panel(name, [(lambda s: full(s), kview(w, c0, 512))])

        for i, c0 in enumerate((512, 1024, 1536, 2048, 0)):
            add_full(f"ab{i}", A["ab_w_in"], c0)
        add_panel("glu", [(lambda s: full(s, 4), kview(A["s5_w_glu"], 0, 512, 0, 4))])
        for i in range(2):
            add_full(f"abo{i}", A["ab_w_out"], 512 * i)

        def add_pieces(name, w, c0):
            for kh in range(2):
                add_panel(f"{name}_{kh}", [(lambda s: full(s, 4), kview(w, c0, 512, 4 * kh, 4))])

        def add_xa_ffn(l):
            for i in range(4):
                add_pieces(f"kv{l}{i}", A["xa_w_kv"][l], 512 * i)
            for i in range(2):
                add_pieces(f"xq{l}{i}", A["xa_w_q"][l], 512 * i)
            for i in range(2):
                add_pieces(f"xo{l}{i}", A["xa_w_out"][l], 512 * i)
            for i in range(FT):
                add_panel(f"gu{l}_{i}", [
                    (lambda s: full(s, KT, 2 * P)[:, :, 0:P], kview(A["f_w_gate"][l], P * i, P)),
                    (lambda s: full(s, KT, 2 * P)[:, :, P:2 * P], kview(A["f_w_up"][l], P * i, P))])
            for i in range(FT // 2):
                add_panel(f"dn{l}_{i}", [
                    (lambda s: full(s, 2, D)[:, 0, :], A["f_w_down"][l][2 * i * P:(2 * i + 1) * P, :]),
                    (lambda s: full(s, 2, D)[:, 1, :], A["f_w_down"][l][(2 * i + 1) * P:(2 * i + 2) * P, :])])

        PIECE0 = len(panels)
        add_xa_ffn(0)
        for i in range(6):
            add_pieces(f"ca{i}", A["c_w_qkv"], 512 * i)
        for i in range(2):
            add_pieces(f"cao{i}", A["c_w_out"], 512 * i)
        add_xa_ffn(1)
        where = {name: n for n, (name, _) in enumerate(panels)}
        landed = []
        tally = [0, 0]
        for n, (_, parts) in enumerate(panels):
            tally[n % 2] += 16 * len(parts)
            landed.append(tally[n % 2])
        slot_landed = [sem("slot0_landed"), sem("slot1_landed")]
        panel_used = sem("panel_used")

        def take(pe, name):
            n = where[name]
            pe.wait_ge(slot_landed[n % 2], landed[n])
            return slots[n % 2]

        PIECE = 2048
        raw_all = tensor_at("raw", slots_at, F32, 2, PIECE)
        raw = [raw_all[:, s, :] for s in range(2)]
        w_hi = rounded("w_hi", slots_at + 2 * PIECE, 2, PIECE)
        w_lo = rounded("w_lo", base + 8192, 2, PIECE)

        def piece_hi(a, n):
            a.wait_ge(slot_landed[n % 2], landed[n])
            a.wait_ge(panel_used, max(n - 1, PIECE0))
            a.activation(w_hi[:, n % 2, :], raw[n % 2], ACT.Copy).then_inc(sem("w_hi"), 1)

        def piece_lo(v, n):
            v.wait_ge(sem("w_hi"), n - PIECE0 + 1)
            v.tensor_tensor(w_lo[:, n % 2, :], raw[n % 2], w_hi[:, n % 2, :].bitcast(F32), ALU.subtract).then_inc(sem("w_lo"), 1)

        split = {"a": PIECE0, "v": PIECE0}

        def upto(name, ahead=0):
            return min(where[name] + ahead, len(panels) - 1) + 1

        def pieces_hi(a, name, ahead=0):
            for n in range(split["a"], upto(name, ahead)):
                piece_hi(a, n)
            split["a"] = upto(name, ahead)

        def pieces_lo(v, name, ahead=0):
            for n in range(split["v"], upto(name, ahead)):
                piece_lo(v, n)
            split["v"] = upto(name, ahead)

        def take_split(pe, name, nk):
            i = where[name]
            pe.wait_ge(sem("w_lo"), i - PIECE0 + 1)
            return tuple(w[:, i % 2, :].rearrange("p (k n) -> p k n", k=nk) for w in (w_hi, w_lo))

        def product(pe, out, a, b, start, stop):
            pe.matmul(out, a[0], b[0], start=start, stop=False)
            pe.matmul(out, a[0], b[1], start=False, stop=False)
            return pe.matmul(out, a[1], b[0], start=False, stop=stop)

        def of(pair, *at):
            return tuple(v[(slice(None), *at)] for v in pair)

        def bc(ap, axis, n):
            v = ap.unsqueeze(axis)
            shape = list(v.shape)
            shape[axis] = n
            return v.broadcast_to(shape)

        count = {}

        def after(name, n):
            return n + named(name)[1]

        def link(eng, ins, name):
            ins.then_inc(sem(name), 1)
            name = named(name)[0]
            count[name] = count.get(name, 0) + 1
            eng.wait_ge(sem(name), count[name])

        def norm_dve(v, t, x, h, r_in, dst, gain, ahead=None):
            n = x.shape[1]
            v.wait_ge(sem(f"{t}_sq"), after(f"{t}_sq", 2 * n))
            link(v, v.tensor_tensor(nrm[:, 0, 0:n], r_in[:, 0, 0:n], r_in[:, 1, 0:n], ALU.add), f"{t}_sum")
            v.wait_ge(sem(f"{t}_root"), after(f"{t}_root", 1))
            link(v, v.reciprocal(rinv[:, 0:n], nrm[:, 1, 0:n]), f"{t}_rinv")
            for i in range(0, n, 2 if t in PLAIN else 1):
                v.tensor_scalar(h[:, i, :], x[:, i, :], rinv[:, i:i + 1], None, ALU.mult).then_inc(sem(f"{t}_hv"), 1)
            if ahead is not None:
                pieces_lo(v, *ahead)
            if t not in PLAIN:
                for k in range(KT):
                    v.wait_ge(sem(f"{t}_outa"), after(f"{t}_outa", k + 1))
                    v.scalar_tensor_tensor(dst[1][:, k, :], ps[:, k, :], pcol(gain, k), dst[0][:, k, :].bitcast(F32),
                                           ALU.mult, ALU.subtract).then_inc(sem(f"{t}_outv"), 1)
                return
            for k in range(1, KT, 2):
                v.wait_ge(sem(f"{t}_turned"), after(f"{t}_turned", k + 1))
                v.tensor_scalar(dst[:, k, :], ps[:, k, 0:n * P], pcol(gain, k), None, ALU.mult).then_inc(sem(f"{t}_outv"), 1)

        def norm_act(a, t, x, h, r_in, dst, gain, ahead=None):
            n = x.shape[1]
            a.wait_ge(sem(f"{t}_sum"), after(f"{t}_sum", 1))
            a.activation(nrm[:, 1, 0:n], nrm[:, 0, 0:n], ACT.Sqrt, bias=pcol("eps"), scale=1.0 / D).then_inc(sem(f"{t}_root"), 1)
            if t in PLAIN:
                a.wait_ge(sem(f"{t}_rinv"), after(f"{t}_rinv", 1))
            if t in PLAIN:
                for i in range(1, n, 2):
                    a.activation(h[:, i, :], x[:, i, :], ACT.Copy, scale=rinv[:, i:i + 1]).then_inc(sem(f"{t}_ha"), 1)
            if ahead is not None:
                pieces_hi(a, *ahead)
            if t not in PLAIN:
                for k in range(KT):
                    a.wait_ge(sem(f"{t}_turned"), after(f"{t}_turned", k + 1))
                    a.activation(dst[0][:, k, :], ps[:, k, :], ACT.Copy, scale=pcol(gain, k)).then_inc(sem(f"{t}_outa"), 1)
                return
            for k in range(0, KT, 2):
                a.wait_ge(sem(f"{t}_turned"), after(f"{t}_turned", k + 1))
                a.activation(dst[:, k, :], ps[:, k, 0:n * P], ACT.Copy, scale=pcol(gain, k)).then_inc(sem(f"{t}_outa"), 1)

        def norm_pe(pe, t, x, h):
            n = x.shape[1]
            if t not in PLAIN:
                for k in range(KT):
                    for i in range(n):
                        if k == 0:
                            pe.wait_ge(sem(f"{t}_hv"), after(f"{t}_hv", i + 1))
                        ins = pe.transpose(ps[:, k, i * P:(i + 1) * P], h[:, i, k * P:(k + 1) * P], ident)
                    ins.then_inc(sem(f"{t}_turned"), 1)
                return
            for i in range(n):
                pe.wait_ge(sem(f"{t}_h{'va'[i % 2]}"), after(f"{t}_h{'va'[i % 2]}", i // 2 + 1))
                for k in range(KT):
                    ins = pe.transpose(ps[:, k, i * P:(i + 1) * P], h[:, i, k * P:(k + 1) * P], ident)
                    if i == n - 1:
                        ins.then_inc(sem(f"{t}_turned"), 1)

        def sqrt_table(a):
            a.activation(warm, pcol("one"), ACT.Sqrt).then_inc(sem("act_warm"), 1)
            name = "act_warm"
            count[name] = count.get(name, 0) + 1
            a.wait_ge(sem("act_warm"), count[name])

        def squares_act(a, t, x, junk, dst, ready=None, ahead=None):
            for half in range(2):
                if ahead is not None:
                    pieces_hi(a, ahead, half)
                if half == 1:
                    sqrt_table(a)
                for i in range(x.shape[1]):
                    if ready is not None:
                        a.wait_ge(sem(ready), after(ready, half * x.shape[1] + i + 1))
                    n = half * x.shape[1] + i
                    if n >= 2:
                        a.wait_ge(sem(f"{t}_sq"), after(f"{t}_sq", n - 1))
                    a.activation(junk[:, (n % 2) * 512:(n % 2 + 1) * 512], x[:, i, half * 512:(half + 1) * 512], ACT.Square,
                                      accum_out=dst[:, half, i:i + 1]).then_inc(sem(f"{t}_sq"), 1)
            a.wait_ge(sem(f"{t}_sq"), after(f"{t}_sq", 2 * x.shape[1]))

        def plain_ready(pe, t, k):
            pe.wait_ge(sem(f"{t}_out{'av'[k % 2]}"), after(f"{t}_out{'av'[k % 2]}", k // 2 + 1))

        def ready_T(pe, t, k):
            pe.wait_ge(sem(f"{t}_outv"), after(f"{t}_outv", k + 1))

        def rows_pe(pe, t, name, srcT, tiles, bank, ready=None, bank_free=None):
            for kh in range(2):
                w = take_split(pe, f"{name}_{kh}", 4)
                for i in range(tiles):
                    if kh == 0 and bank_free is not None:
                        bank_free(i)
                    for k in range(4):
                        kk = 4 * kh + k
                        if i == 0 and ready is not None:
                            ready(kk)
                        ins = product(pe, ps[:, bank + i, :], of(srcT, kk, slice(i * P, (i + 1) * P)), of(w, k), kk == 0, kk == KT - 1)
                    if i == tiles - 1:
                        ins.then_inc(panel_used, 1)
                    elif kh == 1:
                        ins.then_inc(sem(f"{t}_mm"), 1)

        def rows_wait(eng, t, name, tiles, j, i):
            if i < tiles - 1:
                eng.wait_ge(sem(f"{t}_mm"), after(f"{t}_mm", j * (tiles - 1) + i + 1))
            else:
                eng.wait_ge(panel_used, where[f"{name}_1"] + 1)

        def outproj_pe(pe, t, names, srcT, ready):
            for half, name in enumerate(names):
                w = full(take(pe, name))
                for i in range(TT):
                    for k in range(KT):
                        if half == 0 and i == 0:
                            ready(k)
                        ins = pe.matmul(ps[:, 4 * half + i, :], srcT[:, k, i * P:(i + 1) * P], w[:, k, :],
                                        start=(k == 0), stop=(k == KT - 1))
                    if i < TT - 1:
                        ins.then_inc(sem(f"{t}_mm"), 1)
                    else:
                        ins.then_inc(panel_used, 1)

        def split_outproj_pe(pe, t, names, srcT):
            for half, name in enumerate(names):
                rows_pe(pe, t, name, srcT, TT, 4 * half)

        def outproj_dve(v, t, names, x):
            for half in range(2):
                if t != "mo":
                    pieces_lo(v, f"{names[1]}_1", half)
                for i in range(TT):
                    if t != "mo":
                        rows_wait(v, t, names[half], TT, half, i)
                    elif i < TT - 1:
                        v.wait_ge(sem(f"{t}_mm"), after(f"{t}_mm", half * (TT - 1) + i + 1))
                    else:
                        v.wait_ge(panel_used, where[names[half]] + 1)
                    v.tensor_tensor(x[:, i, half * 512:(half + 1) * 512], ps[:, 4 * half + i, :],
                                         x[:, i, half * 512:(half + 1) * 512], ALU.add).then_inc(sem(f"{t}_x"), 1)

        mix = Space(base, top)
        catT = mix(KT, SEQ)
        qkvT = mix(3 * GH, SEQ)
        gateT = mix(GH, SEQ)
        hT_at = mix.at
        hT0 = mix(KT, SEQ)
        x = reg(hT_at, TT, D)
        arena = mix.at
        x0 = reg(base, TT, D)
        h0 = x0
        sq_junk0 = reg(arena + 2 * D, 1024)
        s5 = Space(arena, top)
        G = s5(S5_G, 15, S5_CH)
        WT = s5(S5_G, P)
        TM = s5(S5_G, P)
        E_re, E_im = s5(S5_GP, S5_C), s5(S5_GP, S5_C)
        R8 = s5(S5_GP, S5_C)
        H_re, H_im = s5(8, S5_COLS), s5(8, S5_COLS)
        B1, B2 = s5(S5_G, S5_CH), s5(S5_G, S5_CH)
        Cst = s5(S5_G, S5_CH)
        C_re, C_im = s5(S5_GP, S5_CH), s5(S5_GP, S5_CH)
        sm = {n: s5(S5_COLS) for n in (
            "dt ar th n r t t2 ab sn cs e e8 L_re L_im den rd f_re f_im L2_re L2_im L4_re L4_im u_re u_im w_re w_im").split()}
        Hs = s5(8, S5_G)
        t_pool2 = s5(S5_GP, S5_C // 2)
        logits = s5(TT, 2 * GH)
        w_ab = s5(KT, 2 * GH)
        late = Space(arena, arena + S5_G * 15 * S5_CH)
        V_re, V_im = late(S5_GP, 8, S5_CH), late(S5_GP, 8, S5_CH)
        z_re, z_im, t_a = late(S5_GP, S5_C), late(S5_GP, S5_C), late(S5_GP, S5_C)
        late2 = Space(hT_at, hT_at + KT * SEQ)
        t_b, t_c = late2(S5_GP, S5_C), late2(S5_GP, S5_C)
        U2 = late2(S5_G, S5_C)
        uP = catT[:, 4:8, :]
        yP = reg(arena + 7680 + 8192, 4, SEQ)
        hg = reg(arena + 7680 + 4096, 4, SEQ)
        sg = reg(arena + 7680 + 4096 + 2048, 4, SEQ)
        s5_bc = reg(arena + 7680 + 8192 + 3072 + 768, 2048)
        t_pool = reg(arena + 7680, 2, 4, S5_COLS)
        C_pad = TM
        K8 = reg(arena + 7680 + 8192 + 3072 + 768, 4, 15 * S5_CH)
        yS = reg(arena + 7680, 8, S5_W)
        u_dram = nc.dram_tensor("u_dram", (S5_G, S5_CH, 8 * S5_C), F32, kind="Internal").ap()

        def ab_wait(eng, n):
            if n % 4 < 3:
                eng.wait_ge(sem("ab_mm"), n // 4 * 3 + n % 4 + 1)
            else:
                eng.wait_ge(panel_used, where[f"ab{n // 4}"] + 1)

        def ab_groups_pe(pe, pi):
            w = full(take(pe, f"ab{pi}"))
            for ft in range(4):
                n = 4 * pi + ft
                if n < 8:
                    pe.wait_ge(sem(f"n0_out{'av'[n % 2]}"), after(f"n0_out{'av'[n % 2]}", n // 2 + 1))
                elif n < 16:
                    pe.wait_ge(sem("conv"), n - 7)
                else:
                    pe.wait_ge(sem("conv"), n - 7)
                for k in range(KT):
                    if n == 0:
                        plain_ready(pe, "n0", k)
                    ins = pe.matmul(ps[:, n % 8, :], w[:, k, ft * P:(ft + 1) * P], hT0[:, k, :],
                                    start=(k == 0), stop=(k == KT - 1))
                if ft < 3:
                    ins.then_inc(sem("ab_mm"), 1)
                else:
                    ins.then_inc(panel_used, 1)

        conv_y = catT[:, 0:2, :]

        def conv_dve(v, n):
            ab_wait(v, n)
            if n >= 2:
                v.wait_ge(sem("qkv_s"), n - 1)
            y = conv_y[:, n % 2, :]
            b = ps[:, n % 8, :]
            link(v, v.tensor_scalar(y, b, pcol("conv", 3 * 12 + n), None, ALU.mult), "dve_step")
            for s in (1, 2, 3):
                ins = v.scalar_tensor_tensor(y[:, s:SEQ], b[:, 0:SEQ - s], pcol("conv", (3 - s) * 12 + n),
                                             y[:, s:SEQ], ALU.mult, ALU.add)
                if s < 3:
                    link(v, ins, "dve_step")
                else:
                    ins.then_inc(sem("conv"), 1)

        def silu_act(a, n):
            a.wait_ge(sem("conv"), n + 1)
            a.activation(qkvT[:, n, :], conv_y[:, n % 2, :], ACT.Silu).then_inc(sem("qkv_s"), 1)

        def gate_act(a, n):
            ab_wait(a, n)
            a.activation(gateT[:, n - 12, :], ps[:, n % 8, :], ACT.Silu).then_inc(sem("gate_s"), 1)

        def u_act(a, n):
            ab_wait(a, n)
            a.activation(uP[:, n - 16, :].rearrange("p (l c) -> p c l", l=8),
                              ps[:, n % 8, :].rearrange("p (c l) -> p c l", l=8), ACT.Copy).then_inc(sem("u_s"), 1)

        def logits_pe(pe):
            pe.wait_ge(sem("gate_s"), 4)
            pe.wait_ge(sem("wab_in"), 16)
            for i in range(TT):
                for k in range(KT):
                    ins = pe.matmul(ps[:, 7, i * 8:(i + 1) * 8], hT0[:, k, i * P:(i + 1) * P], w_ab[:, k, :],
                                    start=(k == 0), stop=(k == KT - 1))
            ins.then_inc(sem("logit_mm"), 1)

        def cmul(eng, o_re, o_im, a_re, a_im, b_re, b_im, t1, t2, name):
            link(eng, eng.tensor_tensor(t1, a_re, b_re, ALU.mult), name)
            link(eng, eng.tensor_tensor(t2, a_im, b_im, ALU.mult), name)
            link(eng, eng.tensor_tensor(o_re, t1, t2, ALU.subtract), name)
            link(eng, eng.tensor_tensor(t1, a_re, b_im, ALU.mult), name)
            link(eng, eng.tensor_tensor(t2, a_im, b_re, ALU.mult), name)
            link(eng, eng.tensor_tensor(o_im, t1, t2, ALU.add), name)

        def s5_params_act(a):
            a.wait_ge(sem("par_in"), 16)
            a.activation(sm["dt"], pcols("log_dt"), ACT.Exp).then_inc(sem("s5_dt"), 1)
            a.wait_ge(sem("s5_arg"), 1)
            a.activation(sm["e"], sm["ar"], ACT.Exp).then_inc(sem("s5_fn"), 1)
            a.activation(sm["e8"], sm["ar"], ACT.Exp, scale=8.0).then_inc(sem("s5_fn"), 1)
            a.activation(sm["sn"], sm["r"], ACT.Sin).then_inc(sem("s5_fn"), 1)
            link(a, a.activation(sm["ab"], sm["r"], ACT.Abs), "act_step")
            a.activation(sm["cs"], sm["ab"], ACT.Sin, bias=pcol("half_pi"), scale=-1.0).then_inc(sem("s5_fn"), 1)

        def s5_params_pool(g):
            ch = "s5_pool"
            a_re, a_im = pcols("a_re"), pcols("a_im")
            link(g, g.memset(C_pad, 0.0), ch)
            g.wait_ge(sem("s5_dt"), 1)
            link(g, g.tensor_tensor(sm["ar"], a_re, sm["dt"], ALU.mult), ch)
            link(g, g.tensor_tensor(sm["th"], a_im, sm["dt"], ALU.mult), ch)
            link(g, g.tensor_scalar(sm["n"], sm["th"], 1.0 / TWO_PI, ROUND, ALU.mult, ALU.add), ch)
            link(g, g.tensor_scalar(sm["n"], sm["n"], ROUND, None, ALU.subtract), ch)
            src = sm["th"]
            for c in PI_PARTS:
                link(g, g.tensor_scalar(sm["t"], sm["n"], c, None, ALU.mult), ch)
                link(g, g.tensor_tensor(sm["r"], src, sm["t"], ALU.subtract), ch)
                src = sm["r"]
            link(g, g.tensor_scalar(sm["r"], sm["r"], 3.1415925, -3.1415925, ALU.min, ALU.max), "s5_arg")
            g.wait_ge(sem("s5_fn"), 4)
            link(g, g.tensor_tensor(sm["L_re"], sm["e"], sm["cs"], ALU.mult), ch)
            link(g, g.tensor_tensor(sm["L_im"], sm["e"], sm["sn"], ALU.mult), ch)
            link(g, g.tensor_tensor(sm["t"], a_re, a_re, ALU.mult), ch)
            link(g, g.tensor_tensor(sm["t2"], a_im, a_im, ALU.mult), ch)
            link(g, g.tensor_tensor(sm["den"], sm["t"], sm["t2"], ALU.add), "s5_den")
            link(g, g.tensor_scalar(sm["n"], sm["L_re"], 1.0, None, ALU.subtract), ch)
            link(g, g.tensor_tensor(sm["t"], sm["n"], a_re, ALU.mult), ch)
            link(g, g.tensor_tensor(sm["t2"], sm["L_im"], a_im, ALU.mult), ch)
            link(g, g.tensor_tensor(sm["f_re"], sm["t"], sm["t2"], ALU.add), ch)
            link(g, g.tensor_tensor(sm["t"], sm["L_im"], a_re, ALU.mult), ch)
            link(g, g.tensor_tensor(sm["t2"], sm["n"], a_im, ALU.mult), ch)
            link(g, g.tensor_tensor(sm["f_im"], sm["t"], sm["t2"], ALU.subtract), ch)
            g.wait_ge(sem("s5_rd"), 1)
            for h, f, l in ((H_re, "f_re", "L_re"), (H_im, "f_im", "L_im")):
                link(g, g.tensor_tensor(h[:, 7, 0:S5_G], sm[f][:, 0:S5_G], sm["rd"][:, 0:S5_G], ALU.mult), ch)
                link(g, g.tensor_copy(h[:, 7, S5_G:S5_COLS], sm[l][:, S5_G:S5_COLS]), ch)
            L = lambda n: (sm[n + "_re"], sm[n + "_im"])
            cmul(g, *L("L2"), *L("L"), *L("L"), sm["t"], sm["t2"], ch)
            cmul(g, *L("L4"), *L("L2"), *L("L2"), sm["t"], sm["t2"], ch)
            tmp = t_pool
            for lo, n, p in ((6, 1, "L"), (4, 2, "L2"), (0, 4, "L4")):
                l_re, l_im = L(p)
                cmul(g, H_re[:, lo:lo + n, :], H_im[:, lo:lo + n, :], H_re[:, lo + n:lo + 2 * n, :], H_im[:, lo + n:lo + 2 * n, :],
                     bc(l_re, 1, n), bc(l_im, 1, n), tmp[:, 0, 0:n, :], tmp[:, 1, 0:n, :], ch)
            link(g, g.tensor_copy(E_re[:, :, 1:2], sm["cs"][:, S5_G:S5_COLS].unsqueeze(2)), ch)
            g.wait_ge(sem("bc_in"), 16)
            for m in range(8):
                link(g, g.tensor_scalar(Hs[:, m, :], H_im[:, m, 0:S5_G], pcol("sgn"), None, ALU.mult), ch)
            c8 = Cst.rearrange("p (o r) c -> p o r c", o=4)
            pad = C_pad.rearrange("p (o r) n -> p o r n", o=4)
            for r in range(8):
                link(g, g.tensor_scalar(pad[:, :, r, r * S5_CH:(r + 1) * S5_CH], c8[:, :, r, :], pcol("nsgn"), None, ALU.mult),
                     ch if r < 7 else "s5_tables")

            u, w = (sm["u_re"][:, 0:S5_GP], sm["u_im"][:, 0:S5_GP]), (sm["w_re"][:, 0:S5_GP], sm["w_im"][:, 0:S5_GP])
            one = (sm["cs"][:, S5_G:S5_COLS], sm["sn"][:, S5_G:S5_COLS])
            tt1, tt2 = sm["t"][:, 0:S5_GP], sm["t2"][:, 0:S5_GP]
            cmul(g, *u, *one, *one, tt1, tt2, ch)
            cmul(g, *w, *u, *u, tt1, tt2, ch)
            cmul(g, *u, *w, *w, tt1, tt2, ch)
            link(g, g.memset(E_re[:, :, 0:1], 1.0), ch)
            link(g, g.memset(E_im[:, :, 0:1], 0.0), ch)
            n = 1
            while n < S5_C:
                cmul(g, E_re[:, :, n:2 * n], E_im[:, :, n:2 * n], E_re[:, :, 0:n], E_im[:, :, 0:n],
                     bc(u[0], 2, n), bc(u[1], 2, n), R8[:, :, 0:n], t_pool2[:, :, 0:n], ch)
                n *= 2
                if n < S5_C:
                    cmul(g, *w, *u, *u, tt1, tt2, ch)
                    u, w = w, u
            link(g, g.memset(R8, 0.0), ch)
            link(g, g.tensor_tensor(R8[:, :, 1:S5_C], R8[:, :, 1:S5_C], bc(sm["e8"][:, S5_G:S5_COLS], 2, S5_C - 1), ALU.add), "s5_turn")

            g.wait_ge(sem("s5_copied"), 10)
            cr, ci, vr, vi = s5_v_operands()
            t1 = reg(base, S5_GP, 8, S5_CH)
            link(g, g.tensor_tensor(V_im, cr, vi, ALU.mult), ch)
            link(g, g.tensor_tensor(t1, ci, vr, ALU.mult), ch)
            link(g, g.tensor_tensor(V_im, V_im, t1, ALU.add), "s5_v")

        def s5_v_operands():
            vr = H_re[:, :, S5_G:S5_COLS].rearrange("p i g -> p g i")
            vi = H_im[:, :, S5_G:S5_COLS].rearrange("p i g -> p g i")
            return bc(C_re, 2, 8), bc(C_im, 2, 8), bc(vr, 3, S5_CH), bc(vi, 3, S5_CH)

        def s5_v_dve(v):
            v.wait_ge(sem("s5_tables"), 1)
            v.wait_ge(sem("s5_copied"), 10)
            cr, ci, vr, vi = s5_v_operands()
            t1 = reg(arena + 4096, S5_GP, 8, S5_CH)
            link(v, v.tensor_tensor(V_re, cr, vr, ALU.mult), "dve_step")
            link(v, v.tensor_tensor(t1, ci, vi, ALU.mult), "dve_step")
            v.tensor_tensor(V_re, V_re, t1, ALU.subtract).then_inc(sem("s5_vre"), 1)

        def s5_g_dve(v):
            v.wait_ge(sem("s5_den"), 1)
            v.reciprocal(sm["rd"], sm["den"]).then_inc(sem("s5_rd"), 1)
            v.wait_ge(sem("s5_tables"), 1)
            for g0 in range(0, S5_G, 16):
                gs = slice(g0, g0 + 16)
                o = G[:, gs, 0:8, :]
                hr = bc(H_re[:, :, gs].rearrange("p m g -> p g m"), 3, S5_CH)
                hi = bc(Hs[:, :, gs].rearrange("p m g -> p g m"), 3, S5_CH)
                t = WT[:, gs, :].rearrange("p g (m c) -> p g m c", c=S5_CH)
                v.tensor_tensor(o, hr, bc(B1[:, gs, :], 2, 8), ALU.mult)
                link(v, v.tensor_tensor(t, hi, bc(B2[:, gs, :], 2, 8), ALU.mult), "dve_step")
                v.tensor_tensor(o, o, t, ALU.add).then_inc(sem("s5_g"), 1)
            v.memset(G[:, :, 8:15, :], 0.0).then_inc(sem("s5_g"), 1)

        def s5_tables_pe(pe):
            pe.wait_ge(sem("s5_g"), 3)
            for s in range(10):
                if s == 0:
                    pe.wait_ge(sem("gate_s"), 4)
                if s >= 3:
                    pe.wait_ge(sem("s5_copied"), s - 2)
                bank = ps[:, 4 + s % 3, :]
                if s < 8:
                    for q in range(4):
                        ins = pe.transpose(bank[:, q * P:(q + 1) * P], G[:, 4 * s + q, 0:8, :].rearrange("p m c -> p (m c)"), ident)
                else:
                    for o in range(2):
                        for r in range(8):
                            g = 8 * (2 * (s - 8) + o) + r
                            ins = pe.matmul(bank[:, o * 240:(o + 1) * 240], C_pad[:, g, :], G[:, g, :, :].rearrange("p m c -> p (m c)"),
                                            start=(r == 0), stop=(r == 7))
                ins.then_inc(sem("s5_tab"), 1)

        def s5_tables_act(a):
            for s in range(10):
                a.wait_ge(sem("s5_tab"), s + 1)
                if s < 8:
                    a.activation(WT[:, 4 * s:4 * s + 4, :].rearrange("p g n -> p (g n)"), ps[:, 4 + s % 3, :], ACT.Copy).then_inc(sem("s5_copied"), 1)
                else:
                    a.activation(K8[:, 2 * (s - 8):2 * (s - 8) + 2, :].rearrange("p o n -> p (o n)"), ps[:, 4 + s % 3, 0:480],
                                 ACT.Copy).then_inc(sem("s5_copied"), 1)

        def s5_tm_pe(pe):
            pe.wait_ge(sem("u_s"), 4)
            pe.wait_ge(sem("s5_copied"), 10)
            for s in range(8):
                if s >= 4:
                    pe.wait_ge(sem("s5_copied"), 10 + s - 3)
                for q in range(4):
                    i = 4 * (s % 2) + q
                    ins = pe.transpose(ps[:, s % 4, q * P:(q + 1) * P], K8[:, s // 2, i * S5_CH:i * S5_CH + P], ident)
                ins.then_inc(sem("s5_tab"), 1)

        def s5_tm_act(a):
            for s in range(8):
                o, ih = s // 2, s % 2
                a.wait_ge(sem("s5_tab"), 10 + s + 1)
                a.activation(TM[:, 8 * o:8 * o + 8, ih * 64:(ih + 1) * 64].rearrange("p r (i c) -> p i r c", i=4),
                             ps[:, s % 4, :].rearrange("p (i r c) -> p i r c", i=4, r=8), ACT.Copy).then_inc(sem("s5_copied"), 1)

        def s5_u_sp(sp):
            sp.wait_ge(sem("u_s"), 4)
            sp.dma_start(u_dram.rearrange("(f g) c n -> (g c) f n", f=4), uP).then_inc(sem("u_out"), 16)
            sp.wait_ge(sem("u_out"), 16)
            sp.wait_ge(panel_used, where["ab4"] + 1)
            sp.wait_ge(sem("logit_mm"), 1)
            for l in range(8):
                sp.dma_start(U2[l * S5_CH:(l + 1) * S5_CH, :, :],
                             u_dram[:, :, l * S5_C:(l + 1) * S5_C].rearrange("g c n -> c g n")).then_inc(sem("u_in"), 16)

        def s5_states_pe(pe):
            pe.wait_ge(sem("s5_copied"), 10)
            pe.wait_ge(sem("logit"), 1)
            pe.wait_ge(sem("u_in"), 16 * 8)
            for ri in range(2):
                for g in range(S5_G):
                    gp, g2 = g // 2, g % 2
                    ins = pe.matmul(ps[g2 * 64:g2 * 64 + 64, 4 + 2 * ri + gp // 8, (gp % 8) * S5_C:(gp % 8 + 1) * S5_C],
                                    WT[:, g, ri * 64:ri * 64 + 64], U2[:, g, :], start=True, stop=True)
                ins.then_inc(sem("s5_x"), 1)

        def s5_states_dve(v):
            X_re = ps[:, 4:6, :].rearrange("p b (g c) -> p (b g) c", c=S5_C)
            X_im = ps[:, 6:8, :].rearrange("p b (g c) -> p (b g) c", c=S5_C)
            ch = "dve_step"
            flat = lambda a: a.rearrange("p g c -> p (g c)")
            v.wait_ge(sem("s5_turn"), 1)
            v.wait_ge(sem("s5_vre"), 1)
            v.wait_ge(sem("s5_x"), 2)
            link(v, v.tensor_tensor(t_a, X_re, E_re, ALU.mult), ch)
            link(v, v.tensor_tensor(t_b, X_im, E_im, ALU.mult), ch)
            link(v, v.tensor_tensor(t_a, t_a, t_b, ALU.add), ch)
            link(v, v.tensor_tensor_scan(flat(z_re), flat(R8), flat(t_a), 0.0, ALU.mult, ALU.add), ch)
            link(v, v.tensor_tensor(t_c, X_im, E_re, ALU.mult), ch)
            link(v, v.tensor_tensor(t_b, X_re, E_im, ALU.mult), "s5_xread")
            link(v, v.tensor_tensor(t_c, t_c, t_b, ALU.subtract), ch)
            link(v, v.tensor_tensor_scan(flat(z_im), flat(R8), flat(t_c), 0.0, ALU.mult, ALU.add), ch)
            n = S5_C - 1
            link(v, v.tensor_tensor(t_a, z_re, E_re, ALU.mult), ch)
            link(v, v.tensor_tensor(t_b, z_im, E_im, ALU.mult), ch)
            link(v, v.tensor_tensor(t_c[:, :, 1:], t_a[:, :, 0:n], t_b[:, :, 0:n], ALU.subtract), ch)
            link(v, v.memset(t_c[:, :, 0:1], 0.0), ch)
            link(v, v.tensor_tensor(t_a, z_re, E_im, ALU.mult), ch)
            link(v, v.tensor_tensor(t_b, z_im, E_re, ALU.mult), ch)
            link(v, v.scalar_tensor_tensor(z_re[:, :, 1:], t_a[:, :, 0:n], -1.0, t_b[:, :, 0:n], ALU.mult, ALU.subtract), ch)
            v.memset(z_re[:, :, 0:1], 0.0).then_inc(sem("s5_carry"), 1)

        def s5_out_pe(pe):
            def place(n):
                gp, g2 = n % S5_GP, n // S5_GP
                return gp, g2, ps[0:S5_C, 4 * g2 + gp // 4, (gp % 4) * P:(gp % 4 + 1) * P]
            pe.wait_ge(sem("s5_copied"), 10 + 8)
            for n in range(S5_G):
                gp, g2, o = place(n)
                if n == S5_GP:
                    pe.wait_ge(sem("s5_xread"), 1)
                pe.matmul(o, U2[:, 2 * gp + g2, :], TM[:, 2 * gp + g2, :], start=(gp % 4 == 0), stop=False, skip_group_check=True)
            pe.wait_ge(sem("s5_carry"), 1)
            pe.wait_ge(sem("s5_v"), 1)
            for n in range(S5_G):
                gp, g2, o = place(n)
                r = slice(g2 * 64, g2 * 64 + 64)
                pe.matmul(o, t_c[r, gp, :], V_re[r, gp, :, :].rearrange("p i c -> p (i c)"), start=False, stop=False, skip_group_check=True)
                ins = pe.matmul(o, z_re[r, gp, :], V_im[r, gp, :, :].rearrange("p i c -> p (i c)"), start=False, stop=True, skip_group_check=True)
                if gp % 4 == 3:
                    ins.then_inc(sem("s5_y"), 1)

        def s5_y_evac(eng, b):
            dst = yS[0:S5_C].rearrange("p i (g two c) -> p i g two c", two=2, c=S5_CH)[:, :, 4 * (b % 4):4 * (b % 4) + 4, b // 4, :]
            return dst, ps[0:S5_C, b, :].rearrange("p (g i c) -> p i g c", g=4, i=8)

        def s5_out_act(a):
            for b in range(0, 8, 2):
                a.wait_ge(sem("s5_y"), b + 1)
                a.activation(*s5_y_evac(a, b), ACT.Copy).then_inc(sem("y_a"), 1)

        def s5_out_dve(v):
            for b in range(1, 8, 2):
                v.wait_ge(sem("s5_y"), b + 1)
                v.tensor_copy(*s5_y_evac(v, b)).then_inc(sem("y_v"), 1)

        def s5_back_pe(pe):
            for f in range(4):
                pe.wait_ge(sem(("y_a", "y_v")[f % 2]), 3 + f // 2)
                for i in range(8):
                    ins = pe.transpose(ps[:, f, (7 - i) * S5_C:(8 - i) * S5_C], yS[0:S5_C, i, f * P:(f + 1) * P], ident[0:S5_C, 0:S5_C])
                ins.then_inc(sem("s5_yt"), 1)

        def s5_glu_dve(v):
            for f in range(4):
                v.wait_ge(sem("s5_yt"), f + 1)
                v.scalar_tensor_tensor(yP[:, f, :], uP[:, f, :], pcol("s5_d", f), ps[:, f, :], ALU.mult, ALU.add).then_inc(sem("y_d"), 1)
            for f in range(4):
                v.wait_ge(sem("glu_s"), f + 1)
                v.tensor_tensor(catT[:, f, :].rearrange("p (c l) -> p l c", l=8),
                                     sg[:, f, :].rearrange("p (l c) -> p l c", l=8),
                                     hg[:, f, :].rearrange("p (l c) -> p l c", l=8), ALU.mult)

        def s5_glu_act(a):
            for f in range(4):
                a.wait_ge(sem("y_d"), f + 1)
                a.activation(hg[:, f, :], yP[:, f, :], ACT.Gelu_apprx_tanh).then_inc(sem("gelu_s"), 1)
            for f in range(4):
                if f < 3:
                    a.wait_ge(sem("glu_mm"), f + 1)
                else:
                    a.wait_ge(panel_used, where["glu"] + 1)
                a.activation(sg[:, f, :], ps[:, 4 + f, :], ACT.Sigmoid, bias=pcol("b_glu", f)).then_inc(sem("glu_s"), 1)

        def s5_glu_pe(pe):
            w = full(take(pe, "glu"), 4)
            for f in range(4):
                for k in range(4):
                    if f == 0:
                        pe.wait_ge(sem("gelu_s"), k + 1)
                    ins = pe.matmul(ps[:, 4 + f, :], w[:, k, f * P:(f + 1) * P], hg[:, k, :], start=(k == 0), stop=(k == 3))
                if f < 3:
                    ins.then_inc(sem("glu_mm"), 1)
                else:
                    ins.then_inc(panel_used, 1)

        gd = Space(hT_at, top)
        q_n, k_n, k_b, q_g = gd(GH, GD), gd(GH, GD), gd(GH, GD), gd(GH, GD)
        q_nT, k_nT, k_bT = gd(GH, P), gd(GH, P), gd(GH, P)
        dec_m = gd(GH, P)
        k_bg, v_b, k_t = gd(TT, GH, GD), gd(TT, GH, GD), gd(TT, GH, GD)
        q_gT = gd(TT, GH, P)
        A_T, QK_T = gd(TT, GH, P), gd(TT, GH, P)
        U_m, T_m, Y_m, A_l = gd(TT, GH, P), gd(TT, GH, P), gd(TT, GH, P), gd(TT, GH, P)
        g_bc = gd(GH, P)
        state = gd(GH, GD)
        w_c = gd(2, GH * GD)
        gs = {n: gd(TT, GH) for n in "z az e1 l1 sp g eb beta gc tail gamma ss_o r_o".split()}
        ea = gd(GH)
        dec = gd(2, TT * GH)
        ssq = gd(2, GH)
        rq = gd(2, GH)
        co = {n: gd(GH) for n in "q qg k kb kbg kt".split()}
        lg = gd(TT, 2 * GH)
        qkv0 = base + KT * SEQ
        u_n, wk_T, o_t = reg(qkv0, TT, GH, GD), reg(qkv0 + 2048, TT, GH, P), reg(qkv0 + 4096, TT, GH, GD)
        flat3 = lambda a: a.rearrange("p a b -> p (a b)")

        def logits_dve(v):
            v.wait_ge(sem("logit_mm"), 1)
            v.tensor_copy(logits, ps[:, 7, 0:TT * 8].rearrange("p (i n) -> p i n", i=TT)).then_inc(sem("logit"), 1)

        def gates_dve(v):
            ch = "dve_step"
            link(v, v.tensor_copy(lg, logits), ch)
            link(v, v.tensor_tensor(gs["z"], lg[:, :, 0:GH], bc(pcols("dt_bias"), 1, TT), ALU.add), ch)
            link(v, v.tensor_scalar(gs["az"], gs["z"], -1.0, None, ALU.mult), ch)
            link(v, v.tensor_tensor(gs["az"], gs["az"], gs["z"], ALU.max), "gate_in")
            v.wait_ge(sem("gate_fn"), 3)
            link(v, v.scalar_tensor_tensor(gs["sp"], gs["z"], 0.0, gs["l1"], ALU.max, ALU.add), ch)
            link(v, v.tensor_tensor(gs["sp"], gs["sp"], bc(ea, 1, TT), ALU.mult), ch)
            link(v, v.tensor_scalar(gs["g"], gs["sp"], -1.0, None, ALU.mult), "g_ready")
            link(v, v.tensor_scalar(gs["eb"], gs["eb"], 1.0, None, ALU.add), ch)
            link(v, v.reciprocal(gs["beta"], gs["eb"]), ch)
            v.wait_ge(sem("gcum_mm"), 1)
            link(v, v.tensor_copy(gs["gc"].rearrange("p a b -> p (a b)"), ps[:, 7, 0:16]), ch)
            link(v, v.tensor_tensor(gs["tail"].rearrange("p a b -> p (a b)"), ps[:, 7, 16:32],
                                    gs["gc"].rearrange("p a b -> p (a b)"), ALU.subtract), "gcum")

        def gates_act(a):
            a.wait_ge(sem("gate_in"), 1)
            link(a, a.activation(gs["e1"], gs["az"], ACT.Exp, scale=-1.0), "act_step")
            a.activation(gs["l1"], gs["e1"], ACT.Ln, bias=pcol("one")).then_inc(sem("gate_fn"), 1)
            a.activation(gs["eb"], lg[:, :, GH:2 * GH], ACT.Exp, scale=-1.0).then_inc(sem("gate_fn"), 1)
            a.activation(ea, pcols("a_log"), ACT.Exp).then_inc(sem("gate_fn"), 1)
            a.wait_ge(sem("gcum"), 1)
            a.activation(gs["gamma"], gs["gc"], ACT.Exp).then_inc(sem("decays"), 1)
            a.activation(gs["tail"], gs["tail"], ACT.Exp).then_inc(sem("decays"), 1)
            a.activation(dec.rearrange("p a b -> p (a b)"), ps[:, 7, 32:64], ACT.Exp).then_inc(sem("decays"), 1)

        def gates_pe(pe):
            pe.wait_ge(sem("glu_s"), 4)
            pe.wait_ge(sem("g_ready"), 1)
            g = gs["g"].rearrange("p a b -> p (a b)")
            for n, m in enumerate(("inc", "same", "first", "second")):
                ins = pe.matmul(ps[:, 7, 16 * n:16 * n + 16], ccol(m), g, start=True, stop=True)
            ins.then_inc(sem("gcum_mm"), 1)

        def gdn_turn_pe(pe, i):
            if i == 0:
                pe.wait_ge(sem("qkv_s"), 12)
                pe.wait_ge(sem("y_d"), 4)
            else:
                pe.wait_ge(sem("g_tok"), 7 * i)
            for n in range(3):
                for h in range(GH):
                    ins = pe.transpose(ps[:, n, h * P:(h + 1) * P], qkvT[:, n * GH + h, i * P:(i + 1) * P], ident)
                ins.then_inc(sem("g_tr"), 1)

        def gdn_back_pe(pe, i):
            pe.wait_ge(sem("g_tok"), 7 * i + 4)
            if i == 0:
                pe.wait_ge(sem("glu_s"), 4)
            else:
                pe.wait_ge(sem("g_at"), 2 * i)
            for n, src in enumerate((q_n, k_n, k_b, q_g)):
                for h in range(GH):
                    ins = pe.transpose(ps[:, 3 + n, h * P:(h + 1) * P], src[:, h, :], ident)
                ins.then_inc(sem("g_back"), 1)

        def gdn_prod_pe(pe, i):
            pe.wait_ge(sem("g_ft"), 4 * i + 4)
            if i == 0:
                pe.wait_ge(sem("decays"), 3)
            for bank, l, r in ((7, k_nT, k_bT), (3, k_nT, q_nT)):
                for h in range(GH):
                    ins = pe.matmul(ps[:, bank, h * P:(h + 1) * P], l[:, h, :], r[:, h, :], start=True, stop=True)
                ins.then_inc(sem("g_prod"), 1)
            pe.wait_ge(sem("g_bc"), i + 1)
            for h in range(GH):
                ins = pe.matmul(ps[:, 4, h * P:(h + 1) * P], g_bc[:, h, :], ccol("inc"), start=True, stop=True)
            ins.then_inc(sem("g_row"), 1)

        def gdn_tok_act(a, i):
            for n in range(2):
                a.wait_ge(sem("g_tr"), 3 * i + n + 1)
                if i > 0:
                    a.wait_ge(sem("g_ss"), 2 * i - 1 + n)
                a.activation(A_l[:, n, :, :].rearrange("p a b -> p (a b)"), ps[:, n, :], ACT.Square).then_inc(sem("g_sq"), 1)
            a.wait_ge(sem("g_ss"), 2 * i + 2)
            a.activation(rq, ssq, ACT.Sqrt, bias=pcol("eps")).then_inc(sem("g_rt"), 1)

        def gdn_back_act(a, i):
            if i > 0:
                a.wait_ge(sem("g_row"), i)
            for n, dst in enumerate((q_nT, k_nT, k_bT, q_gT[:, i, :, :])):
                a.wait_ge(sem("g_back"), 4 * i + n + 1)
                a.activation(dst, ps[:, 3 + n, :].rearrange("p (a b) -> p a b", a=GH), ACT.Copy).then_inc(sem("g_ft"), 1)

        def gdn_dec_act(a, i):
            a.wait_ge(sem("g_diff"), 4 * i + 4)
            a.activation(dec_m, dec_m, ACT.Exp).then_inc(sem("g_dec"), 1)

        def gdn_tok_dve(v, i):
            for n in range(2):
                v.wait_ge(sem("g_sq"), 2 * i + n + 1)
                link(v, v.tensor_reduce(ssq[:, n, :], A_l[:, n, :, :], AX, ALU.add), "g_ss")
            if i == 0:
                v.wait_ge(sem("decays"), 3)
            v.wait_ge(sem("g_rt"), i + 1)
            ch = "dve_step"
            link(v, v.reciprocal(rq, rq), ch)
            link(v, v.tensor_scalar(co["q"], rq[:, 0, :], GD ** -0.5, None, ALU.mult), ch)
            link(v, v.tensor_tensor(co["qg"], co["q"], gs["gamma"][:, i, :], ALU.mult), ch)
            link(v, v.tensor_tensor(co["kb"], rq[:, 1, :], gs["beta"][:, i, :], ALU.mult), ch)
            link(v, v.tensor_tensor(co["kbg"], co["kb"], gs["gamma"][:, i, :], ALU.mult), ch)
            link(v, v.tensor_tensor(co["kt"], rq[:, 1, :], gs["tail"][:, i, :], ALU.mult), ch)
            if i > 0:
                v.wait_ge(sem("g_back"), 4 * i)
                v.wait_ge(sem("g_row"), i)
            v.wait_ge(sem("g_tr"), 3 * i + 3)
            for dst, bank, c in ((q_n, 0, co["q"]), (k_n, 1, rq[:, 1, :]), (k_b, 1, co["kb"]), (q_g, 0, co["qg"]),
                                 (k_bg[:, i], 1, co["kbg"]), (v_b[:, i], 2, gs["beta"][:, i, :]), (k_t[:, i], 1, co["kt"])):
                v.tensor_tensor(dst, ps[:, bank, :].rearrange("p (a b) -> p a b", a=GH), bc(c, 2, GD), ALU.mult).then_inc(sem("g_tok"), 1)
            v.tensor_copy(g_bc, bc(gs["g"][:, i, :], 2, P)).then_inc(sem("g_bc"), 1)

        def gdn_prod_dve(v, i):
            v.wait_ge(sem("g_row"), i + 1)
            for h in range(GH):
                v.scalar_tensor_tensor(dec_m[:, h, :], ps[:, 4, h * P:(h + 1) * P], gs["gc"][:, i, h:h + 1],
                                            ccol("neg"), ALU.subtract, ALU.add).then_inc(sem("g_diff"), 1)
            v.wait_ge(sem("g_dec"), i + 1)
            for dst, bank in ((A_T, 7), (QK_T, 3)):
                v.tensor_tensor(dst[:, i], ps[:, bank, :].rearrange("p (a b) -> p a b", a=GH), dec_m, ALU.mult).then_inc(sem("g_at"), 1)
            v.wait_ge(sem("g_at"), 2 * i + 2)
            link(v, v.tensor_tensor(U_m[:, i], A_T[:, i], bc(ccol("m1"), 1, GH), ALU.mult), "dve_step")
            v.tensor_tensor(U_m[:, i], bc(ident, 1, GH), U_m[:, i], ALU.subtract).then_inc(sem("g_u"), 1)

        LEVELS = 5

        def solve_masks_pool(g):
            for l in range(LEVELS):
                for i in range(TT):
                    if l == 0:
                        g.wait_ge(sem("g_u"), TT)
                    else:
                        g.wait_ge(sem("sv_y"), (l - 1) * TT + i + 1)
                    g.tensor_tensor(A_l[:, i], A_T[:, i], bc(ccol(f"m{l + 2}"), 1, GH), ALU.mult).then_inc(sem("sv_mask"), 1)

        def solve_pe(pe):
            for i in range(TT):
                pe.wait_ge(sem("g_u"), TT)
                if i >= 2:
                    pe.wait_ge(sem("sv_t0"), i - 1)
                for h in range(GH):
                    ins = pe.transpose(ps[:, i % 2, h * P:(h + 1) * P], U_m[:, i, h, :], ident)
                ins.then_inc(sem("sv_tr"), 1)
            for l in range(LEVELS):
                for i in range(TT):
                    n = l * TT + i
                    pe.wait_ge(sem("sv_mask"), n + 1)
                    if l == 0:
                        pe.wait_ge(sem("sv_t0"), min(i + 3, TT))
                    else:
                        pe.wait_ge(sem("sv_t"), n - TT + 1)
                    if n >= 2:
                        pe.wait_ge(sem("sv_yc"), n - 1)
                    for h in range(GH):
                        ins = pe.matmul(ps[:, n % 2, h * P:(h + 1) * P], A_l[:, i, h, :], T_m[:, i, h, :], start=True, stop=True)
                    ins.then_inc(sem("sv_y"), 1)
                for i in range(TT):
                    n = l * TT + i
                    pe.wait_ge(sem("sv_yc"), n + 1)
                    if l > 0:
                        pe.wait_ge(sem("sv_u"), n - TT + 1)
                    if n >= 3:
                        pe.wait_ge(sem("sv_u"), n - 2)
                    for h in range(GH):
                        ins = pe.matmul(ps[:, 2 + n % 3, h * P:(h + 1) * P], Y_m[:, i, h, :], U_m[:, i, h, :], start=True, stop=True)
                    if l < LEVELS - 1:
                        if n >= 3:
                            pe.wait_ge(sem("sv_t"), n - 2)
                        for h in range(GH):
                            ins = pe.matmul(ps[:, 5 + n % 3, h * P:(h + 1) * P], U_m[:, i, h, :], Y_m[:, i, h, :], start=True, stop=True)
                    ins.then_inc(sem("sv_d"), 1)

        def solve_act(a):
            for i in range(TT):
                a.wait_ge(sem("sv_tr"), i + 1)
                a.activation(flat3(T_m[:, i]), ps[:, i % 2, :], ACT.Copy).then_inc(sem("sv_t0"), 1)
            for n in range(LEVELS * TT):
                a.wait_ge(sem("sv_y"), n + 1)
                if n >= TT:
                    a.wait_ge(sem("sv_d"), n - TT + 1)
                a.activation(flat3(Y_m[:, n % TT]), ps[:, n % 2, :], ACT.Copy).then_inc(sem("sv_yc"), 1)

        def solve_dve(v):
            for n in range(LEVELS * TT):
                i = n % TT
                v.wait_ge(sem("sv_d"), n + 1)
                if n >= TT:
                    v.wait_ge(sem("sv_u"), n - TT + 1)
                v.tensor_tensor(flat3(U_m[:, i]), flat3(U_m[:, i]), ps[:, 2 + n % 3, :], ALU.subtract).then_inc(sem("sv_u"), 1)
                if n < (LEVELS - 1) * TT:
                    v.tensor_tensor(flat3(T_m[:, i]), flat3(T_m[:, i]), ps[:, 5 + n % 3, :], ALU.subtract).then_inc(sem("sv_t"), 1)

        def uw_pe(pe):
            pe.wait_ge(sem("sv_u"), LEVELS * TT)
            for i in range(TT):
                for h in range(GH):
                    ins = pe.matmul(ps[:, 2 * i, h * P:(h + 1) * P], U_m[:, i, h, :], v_b[:, i, h, :], start=True, stop=True)
                ins.then_inc(sem("uw"), 1)
                for h in range(GH):
                    ins = pe.matmul(ps[:, 2 * i + 1, h * P:(h + 1) * P], k_bg[:, i, h, :], U_m[:, i, h, :], start=True, stop=True)
                ins.then_inc(sem("uw"), 1)

        def uw_act(a):
            for i in range(TT):
                a.wait_ge(sem("uw"), 2 * i + 1)
                a.activation(flat3(u_n[:, i]), ps[:, 2 * i, :], ACT.Copy).then_inc(sem("u_c"), 1)

        def uw_dve(v):
            v.memset(state, 0.0).then_inc(sem("s_new"), 1)
            for i in range(TT):
                v.wait_ge(sem("uw"), 2 * i + 2)
                v.tensor_copy(flat3(wk_T[:, i]), ps[:, 2 * i + 1, :]).then_inc(sem("wk_c"), 1)

        def rec_pe(pe):
            for c in range(NCH):
                i, r = c // 2, slice(64 * (c % 2), 64 * (c % 2) + 64)
                pe.wait_ge(sem("s_new"), 1 + GH * c)
                if c == 0:
                    pe.wait_ge(sem("u_c"), TT)
                    pe.wait_ge(sem("wk_c"), TT)
                for h in range(GH):
                    ins = pe.matmul(ps[r, c % 2, h * P:(h + 1) * P], wk_T[:, i, h, r], state[:, h, :], start=True, stop=True)
                ins.then_inc(sem("r_ws"), 1)
                if c >= 2:
                    pe.wait_ge(sem("r_o"), c - 1)
                for h in range(GH):
                    pe.matmul(ps[r, 2 + c % 2, h * P:(h + 1) * P], q_gT[:, i, h, r], state[:, h, :], start=(h == 0), stop=False,
                              skip_group_check=True)
                pe.wait_ge(sem("r_w"), c + 1)
                for h in range(GH):
                    ins = pe.matmul(ps[:, 4 + c % 2, h * P:(h + 1) * P], k_t[r, i, h, :], w_c[r, c % 2, h * P:(h + 1) * P], start=True, stop=True)
                ins.then_inc(sem("r_kw"), 1)
                for h in range(GH):
                    ins = pe.matmul(ps[r, 2 + c % 2, h * P:(h + 1) * P], QK_T[r, i, h, r], w_c[r, c % 2, h * P:(h + 1) * P],
                                    start=False, stop=True, skip_group_check=True)
                ins.then_inc(sem("r_om"), 1)

        def rec_dve(v):
            for c in range(NCH):
                i, r = c // 2, slice(64 * (c % 2), 64 * (c % 2) + 64)
                v.wait_ge(sem("r_ws"), c + 1)
                if c == 0:
                    v.wait_ge(sem("u_c"), TT)
                if c >= 2:
                    v.wait_ge(sem("r_om"), c - 1)
                v.tensor_tensor(w_c[r, c % 2, :], flat3(u_n[r, i]), ps[r, c % 2, :], ALU.subtract).then_inc(sem("r_w"), 1)
                v.wait_ge(sem("r_kw"), c + 1)
                v.wait_ge(sem("s_new"), 1 + GH * c)
                for h in range(GH):
                    v.scalar_tensor_tensor(state[:, h, :], state[:, h, :], dec[:, c % 2, i * GH + h:i * GH + h + 1],
                                                ps[:, 4 + c % 2, h * P:(h + 1) * P], ALU.mult, ALU.add).then_inc(sem("s_new"), 1)

        def rec_act(a):
            for c in range(NCH):
                i, r = c // 2, slice(64 * (c % 2), 64 * (c % 2) + 64)
                a.wait_ge(sem("r_om"), c + 1)
                a.activation(flat3(o_t[r, i]), ps[r, 2 + c % 2, :], ACT.Copy).then_inc(sem("r_o"), 1)

        def gout_act(a):
            for i in range(TT):
                a.wait_ge(sem("r_o"), 2 * i + 2)
                a.activation(A_l[:, i], o_t[:, i], ACT.Square).then_inc(sem("go_sq"), 1)
            a.wait_ge(sem("go_ss"), 4)
            a.activation(gs["r_o"], gs["ss_o"], ACT.Sqrt, bias=pcol("eps"), scale=1.0 / GD).then_inc(sem("go_rt"), 1)

        def gout_dve(v):
            for i in range(TT):
                v.wait_ge(sem("go_sq"), i + 1)
                v.tensor_reduce(gs["ss_o"][:, i, :], A_l[:, i], AX, ALU.add).then_inc(sem("go_ss"), 1)
            v.wait_ge(sem("go_rt"), 1)
            link(v, v.reciprocal(gs["r_o"], gs["r_o"]), "dve_step")
            for i in range(TT):
                v.tensor_tensor(o_t[:, i], o_t[:, i], bc(gs["r_o"][:, i, :], 2, GD), ALU.mult).then_inc(sem("go_n"), 1)
            for h in range(GH):
                v.wait_ge(sem("go_tr"), h + 1)
                v.scalar_tensor_tensor(catT[:, 4 + h, :], ps[:, 4 + h, :], pcol("gdn_g"), gateT[:, h, :], ALU.mult, ALU.mult).then_inc(sem("gdn_done"), 1)

        def gout_pe(pe):
            pe.wait_ge(sem("s_new"), 1 + GH * NCH)
            pe.wait_ge(sem("go_n"), TT)
            for h in range(GH):
                for i in range(TT):
                    ins = pe.transpose(ps[:, 4 + h, i * P:(i + 1) * P], o_t[:, i, h, :], ident)
                ins.then_inc(sem("go_tr"), 1)

        def xres_sp(sp):
            sp.wait_ge(sem("g_at"), 2 * TT)
            sp.wait_ge(sem("g_row"), TT)
            sp.dma_start(x, A["x"].rearrange("(i p) n -> p i n", p=P)).then_inc(sem("x_in"), 16)

        low = Space(base, hT_at)
        high = Space(arena, top)
        hT = (rounded("h_hi", low.at, KT, SEQ), rounded("h_lo", low.at + 4096, KT, SEQ))
        oT = hT
        high_a = high(4096)
        high_b = high(4096)
        high_c = high(4096)
        high_d = high(4096)
        high_e = high(4096)
        high_f = high(4096)
        at_b, at_c, at_d, at_e, at_f = (arena + 4096 * n for n in range(1, 6))
        rows = lambda v, n=TT: v[:, 0:n * D].rearrange("p (i n) -> p i n", i=n)
        feat = lambda v: v.rearrange("p (k n) -> p k n", k=KT)
        h_rows = rows(high_a)
        q_rows = h_rows
        qT = feat(high_b)
        mem_T = (rounded("mem_hi", at_b, KT, N_MEM), rounded("mem_lo", at_b + 2048, KT, N_MEM))
        xk_rows = rows(reg(at_c, 2048), MT)
        sq_junk = reg(at_c + 2048, 1024)
        xk_T = reg(at_d, KT, N_MEM)
        xv = reg(at_d + 2048, MT, D)
        p_x = [reg(at_e + 1024 * n, TT, N_MEM) for n in range(2)]
        pT_x = [reg(at_e + 2048 + 1024 * n, MT, SEQ) for n in range(2)]
        mem_x = rows(high_f, MT)
        xs = Space(at_f + 2048 + 1200, at_f + 4096)
        kss, kr = xs(MT, XH), xs(MT, XH)
        qss, qr = xs(TT, XH), xs(TT, XH)
        nmax = xs(2, TT)
        psum_x = xs(2, TT)
        prec = xs(2, TT)

        def mem_split_act(a):
            a.activation(mem_T[0], memT, ACT.Copy).then_inc(sem("mem_hi"), 1)

        def mem_split_dve(v, l):
            v.wait_ge(sem("mem_hi"), l + 1)
            v.tensor_tensor(mem_T[1], memT, mem_T[0].bitcast(F32), ALU.subtract).then_inc(sem("mem_lo"), 1)

        def mem_sp(sp):
            sp.wait_ge(sem("gdn_done"), GH)
            sp.dma_start(mem_x, A["mem"].rearrange("(i p) n -> p i n", p=P)).then_inc(sem("mem_in"), 16)

        def kv_pe(pe, l):
            t = f"kv{l}"
            for j in range(4):
                rows_pe(pe, t, f"kv{l}{j}", mem_T, MT, 2 * j)

        def kv_wait(eng, l, j, i):
            rows_wait(eng, f"kv{l}", f"kv{l}{j}", MT, j, i)

        def kv_act(a, l):
            t = f"kv{l}"
            for j in range(2):
                pieces_hi(a, f"kv{l}{j}_1", 2)
                for i in range(MT):
                    kv_wait(a, l, j, i)
                    b = ps[:, 2 * j + i, :]
                    for h in range(2):
                        n = 4 * j + 2 * i + h
                        if n >= 4:
                            a.wait_ge(sem(f"{t}_sq"), after(f"{t}_sq", n - 3))
                        a.activation(sq_junk[:, (n % 4) * 256:(n % 4 + 1) * 256], b[:, h * 256:(h + 1) * 256], ACT.Square,
                                          accum_out=kss[:, i, 2 * j + h:2 * j + h + 1]).then_inc(sem(f"{t}_sq"), 1)
            a.wait_ge(sem(f"{t}_sq"), after(f"{t}_sq", 8))
            a.activation(kr, kss, ACT.Sqrt, bias=pcol("eps"), scale=1.0 / XD).then_inc(sem(f"{t}_rt"), 1)
            pieces_hi(a, f"kv{l}3_1")
            for i in range(MT):
                kv_wait(a, l, 2, i)
                a.activation(xv[:, i, 0:512], ps[:, 4 + i, :], ACT.Copy).then_inc(sem(f"{t}_v"), 1)
            pieces_hi(a, f"kv{l}3_1", 1)
            for i in range(MT):
                kv_wait(a, l, 3, i)
                a.activation(xv[:, i, 512:1024], ps[:, 6 + i, :], ACT.Copy).then_inc(sem(f"{t}_v"), 1)
            for k in range(0, KT, 2):
                a.wait_ge(sem(f"{t}_turned"), after(f"{t}_turned", k + 1))
                a.activation(xk_T[:, k, :], ps[:, k, 0:N_MEM], ACT.Copy, scale=pcol(f"xk_g{l}", 0)).then_inc(sem(f"{t}_kTa"), 1)

        def kv_dve(v, l):
            t = f"kv{l}"
            pieces_lo(v, f"kv{l}2_1")
            v.wait_ge(sem(f"{t}_rt"), after(f"{t}_rt", 1))
            link(v, v.reciprocal(kr, kr), "dve_step")
            for j in range(2):
                for i in range(MT):
                    v.tensor_tensor(xk_rows[:, i, j * 512:(j + 1) * 512].rearrange("p (h n) -> p h n", h=2),
                                         ps[:, 2 * j + i, :].rearrange("p (h n) -> p h n", h=2),
                                         bc(kr[:, i, 2 * j:2 * j + 2], 2, XD), ALU.mult).then_inc(sem(f"{t}_k"), 1)
            pieces_lo(v, f"kv{l}3_1", 1)
            for k in range(1, KT, 2):
                v.wait_ge(sem(f"{t}_turned"), after(f"{t}_turned", k + 1))
                v.tensor_scalar(xk_T[:, k, :], ps[:, k, 0:N_MEM], pcol(f"xk_g{l}", 1), None, ALU.mult).then_inc(sem(f"{t}_kTv"), 1)

        def kv_turn_pe(pe, l):
            t = f"kv{l}"
            pe.wait_ge(sem(f"{t}_k"), after(f"{t}_k", 4))
            pe.wait_ge(sem(f"{t}_v"), after(f"{t}_v", 4))
            for k in range(KT):
                for i in range(MT):
                    ins = pe.transpose(ps[:, k, i * P:(i + 1) * P], xk_rows[:, i, k * P:(k + 1) * P], ident)
                ins.then_inc(sem(f"{t}_turned"), 1)

        def xq_pe(pe, l):
            t = f"xq{l}"
            for j in range(2):
                rows_pe(pe, t, f"xq{l}{j}", hT, TT, 4 * j,
                        ready=(lambda k: ready_T(pe, f"x{l}", k)) if j == 0 else None,
                        bank_free=lambda i: ready_T(pe, f"x{l}", 4 * j + i))
            for k in range(KT):
                for i in range(TT):
                    pe.wait_ge(sem(f"{t}_q"), after(f"{t}_q", 4 * (k // 4) + i + 1))
                    ins = pe.transpose(ps[:, k, i * P:(i + 1) * P], q_rows[:, i, k * P:(k + 1) * P], ident)
                ins.then_inc(sem(f"{t}_turned"), 1)

        def xq_act(a, l):
            t = f"xq{l}"
            for j in range(2):
                pieces_hi(a, f"xq{l}1_1", j)
                sqrt_table(a)
                for i in range(TT):
                    rows_wait(a, t, f"xq{l}{j}", TT, j, i)
                    for h in range(2):
                        n = 8 * j + 2 * i + h
                        if n >= 4:
                            a.wait_ge(sem(f"{t}_sq"), after(f"{t}_sq", n - 3))
                        a.activation(sq_junk[:, (n % 4) * 256:(n % 4 + 1) * 256], ps[:, 4 * j + i, h * 256:(h + 1) * 256], ACT.Square,
                                          accum_out=qss[:, i, 2 * j + h:2 * j + h + 1]).then_inc(sem(f"{t}_sq"), 1)
                a.wait_ge(sem(f"{t}_sq"), after(f"{t}_sq", 8 * (j + 1)))
                a.activation(qr[:, :, 2 * j:2 * j + 2], qss[:, :, 2 * j:2 * j + 2], ACT.Sqrt, bias=pcol("eps"),
                             scale=1.0 / XD).then_inc(sem(f"{t}_rt"), 1)
            for k in range(0, KT, 2):
                a.wait_ge(sem(f"{t}_turned"), after(f"{t}_turned", k + 1))
                a.activation(qT[:, k, :], ps[:, k, :], ACT.Copy, scale=pcol(f"xq_g{l}", 0)).then_inc(sem(f"{t}_qTa"), 1)

        def xq_dve(v, l):
            t = f"xq{l}"
            for j in range(2):
                pieces_lo(v, f"xq{l}1_1", j)
                v.wait_ge(sem(f"{t}_rt"), after(f"{t}_rt", j + 1))
                r = qr[:, :, 2 * j:2 * j + 2]
                link(v, v.reciprocal(r, r), "dve_step")
                link(v, v.tensor_scalar(r, r, XD ** -0.5, None, ALU.mult), "dve_step")
                for i in range(TT):
                    v.tensor_tensor(q_rows[:, i, j * 512:(j + 1) * 512].rearrange("p (h n) -> p h n", h=2),
                                         ps[:, 4 * j + i, :].rearrange("p (h n) -> p h n", h=2),
                                         bc(qr[:, i, 2 * j:2 * j + 2], 2, XD), ALU.mult).then_inc(sem(f"{t}_q"), 1)
            for k in range(1, KT, 2):
                v.wait_ge(sem(f"{t}_turned"), after(f"{t}_turned", k + 1))
                v.tensor_scalar(qT[:, k, :], ps[:, k, :], pcol(f"xq_g{l}", 1), None, ALU.mult).then_inc(sem(f"{t}_qTv"), 1)

        def xa_scores_pe(pe, l, h):
            t = f"xa{l}"
            if h == 0:
                for k in range(KT):
                    pe.wait_ge(sem(f"xq{l}_qT{'av'[k % 2]}"), after(f"xq{l}_qT{'av'[k % 2]}", k // 2 + 1))
                    pe.wait_ge(sem(f"kv{l}_kT{'av'[k % 2]}"), after(f"kv{l}_kT{'av'[k % 2]}", k // 2 + 1))
            if h >= 2:
                pe.wait_ge(sem(f"{t}_exp"), after(f"{t}_exp", TT * (h - 1)))
            for i in range(TT):
                for d in range(2):
                    ins = pe.matmul(ps[:, 2 * (h % 2) + i // 2, (i % 2) * 256:(i % 2) * 256 + 256],
                                    qT[:, 2 * h + d, i * P:(i + 1) * P], xk_T[:, 2 * h + d, :], start=(d == 0), stop=(d == 1))
            ins.then_inc(sem(f"{t}_s"), 1)

        def xa_turn_pe(pe, l, h):
            t = f"xa{l}"
            pe.wait_ge(sem(f"{t}_p"), after(f"{t}_p", h + 1))
            if h > 0:
                pe.wait_ge(sem(f"{t}_pTa"), after(f"{t}_pTa", h))
                pe.wait_ge(sem(f"{t}_pTv"), after(f"{t}_pTv", h))
            for s in range(MT):
                for i in range(TT):
                    ins = pe.transpose(ps[:, 4 + s, i * P:(i + 1) * P], p_x[h % 2][:, i, s * P:(s + 1) * P], ident)
                ins.then_inc(sem(f"{t}_tr"), 1)

        def xa_values_pe(pe, l, h):
            t = f"xa{l}"
            pe.wait_ge(sem(f"{t}_pTa"), after(f"{t}_pTa", h + 1))
            pe.wait_ge(sem(f"{t}_pTv"), after(f"{t}_pTv", h + 1))
            if h > 0:
                pe.wait_ge(sem(f"{t}_ov"), after(f"{t}_ov", 2 * h))
            for d in range(2):
                for s in range(MT):
                    ins = pe.matmul(ps[:, 6 + d, :], xv[:, s, h * XD + d * P:h * XD + (d + 1) * P], pT_x[h % 2][:, s, :], start=(s == 0), stop=(s == 1))
                ins.then_inc(sem(f"{t}_o"), 1)

        def xa_act(a, l):
            t = f"xa{l}"

            def exps(h):
                a.wait_ge(sem(f"{t}_max"), after(f"{t}_max", h + 1))
                if h >= 2:
                    a.wait_ge(sem(f"{t}_tr"), after(f"{t}_tr", 2 * (h - 1)))
                for i in range(TT):
                    a.activation(p_x[h % 2][:, i, :], ps[:, 2 * (h % 2) + i // 2, (i % 2) * 256:(i % 2) * 256 + 256], ACT.Exp,
                                      bias=nmax[:, h % 2, i:i + 1], accum_out=psum_x[:, h % 2, i:i + 1]).then_inc(sem(f"{t}_exp"), 1)
            exps(0)
            for h in range(XH):
                a.wait_ge(sem(f"{t}_tr"), after(f"{t}_tr", 2 * h + 1))
                if h >= 2:
                    a.wait_ge(sem(f"{t}_o"), after(f"{t}_o", 2 * (h - 1)))
                a.activation(pT_x[h % 2][:, 0, :], ps[:, 4, :], ACT.Copy).then_inc(sem(f"{t}_pTa"), 1)
                if h + 1 < XH:
                    exps(h + 1)
                for d in range(2):
                    a.wait_ge(sem(f"{t}_o"), after(f"{t}_o", 2 * h + d + 1))
                    a.activation(oT[0][:, 2 * h + d, :], ps[:, 6 + d, :], ACT.Copy).then_inc(sem(f"{t}_oa"), 1)
                if h == 0:
                    pieces_hi(a, f"xq{l}1_1", 2)

        def xa_dve(v, l):
            t = f"xa{l}"

            def maxes(h):
                v.wait_ge(sem(f"{t}_s"), after(f"{t}_s", h + 1))
                v.tensor_reduce(nmax[:, h % 2, :], ps[:, 2 * (h % 2):2 * (h % 2) + 2, :].rearrange("p b (i n) -> p (b i) n", i=2),
                                     AX, ALU.max, negate=True).then_inc(sem(f"{t}_max"), 1)
            def rescale(h):
                v.wait_ge(sem(f"{t}_exp"), after(f"{t}_exp", TT * (h + 1)))
                link(v, v.reciprocal(prec[:, h % 2, :], psum_x[:, h % 2, :]), "dve_step")
                v.tensor_tensor(p_x[h % 2], p_x[h % 2], bc(prec[:, h % 2, :], 2, N_MEM), ALU.mult).then_inc(sem(f"{t}_p"), 1)

            maxes(0)
            maxes(1)
            rescale(0)
            for h in range(XH):
                v.wait_ge(sem(f"{t}_tr"), after(f"{t}_tr", 2 * h + 2))
                if h >= 2:
                    v.wait_ge(sem(f"{t}_o"), after(f"{t}_o", 2 * (h - 1)))
                v.tensor_copy(pT_x[h % 2][:, 1, :], ps[:, 5, :]).then_inc(sem(f"{t}_pTv"), 1)
                if h + 1 < XH:
                    rescale(h + 1)
                if h + 2 < XH:
                    maxes(h + 2)
                for d in range(2):
                    v.wait_ge(sem(f"{t}_oa"), after(f"{t}_oa", 2 * h + d + 1))
                    v.tensor_tensor(oT[1][:, 2 * h + d, :], ps[:, 6 + d, :], oT[0][:, 2 * h + d, :].bitcast(F32),
                                    ALU.subtract).then_inc(sem(f"{t}_ov"), 1)
                if h == 0:
                    pieces_lo(v, f"xq{l}1_1", 2)

        def xa_pe(pe, l):
            xa_scores_pe(pe, l, 0)
            xa_scores_pe(pe, l, 1)
            for h in range(XH):
                xa_turn_pe(pe, l, h)
                if h + 2 < XH:
                    xa_scores_pe(pe, l, h + 2)
                xa_values_pe(pe, l, h)

        aT = (rounded("a_hi", arena, FT * SEQ), rounded("a_lo", arena + FT * SEQ, FT * SEQ))
        up = tensor_at("up", at_f + 2048, F32, 4, SEQ)
        gsil, prod = up[:, 0:2, :], up[:, 2:4, :]
        gs_junk = reg(at_f + 2048, 2 * SEQ)

        def ffn_up_pe(pe, l):
            n0 = where[f"gu{l}_0"]
            with pe.Fori(0, FT // 2) as j:
                for s in range(2):
                    pe.wait_ge(sem("w_lo"), j * 2 + (n0 - PIECE0 + s + 1))
                    pe.wait_ge(sem(f"f{l}_free"), j * 2 + after(f"f{l}_free", s + 1))
                    w = tuple(v[:, (n0 + s) % 2, :].rearrange("p (k n) -> p k n", k=KT) for v in (w_hi, w_lo))
                    for gu in range(2):
                        for k in range(KT):
                            ins = product(pe, ps[:, 4 * s + gu, :], of(w, k, slice(gu * P, (gu + 1) * P)), of(hT, k), k == 0, k == KT - 1)
                        if gu == 0:
                            ins.then_inc(sem(f"f{l}_mm"), 1)
                        else:
                            ins.then_inc(panel_used, 1)

        def ffn_up_act(a, l):
            n0 = where[f"gu{l}_0"]
            with a.Fori(0, FT // 2) as j:
                for s in range(2):
                    slot = (n0 + s) % 2
                    a.wait_ge(sem(f"f{l}_mm"), j * 2 + after(f"f{l}_mm", s + 1))
                    a.wait_ge(sem(f"f{l}_free"), j * 2 + after(f"f{l}_free", s + 1))
                    a.activation(gsil[:, s, :], ps[:, 4 * s, :], ACT.Silu).then_inc(sem(f"f{l}_silu"), 1)
                    a.wait_ge(slot_landed[slot], j * 32 + landed[n0 + s + 2])
                    a.wait_ge(panel_used, j * 2 + (n0 + s + 1))
                    a.activation(w_hi[:, slot, :], raw[slot], ACT.Copy).then_inc(sem("w_hi"), 1)
            split["a"] = n0 + FT + 2

        def ffn_up_dve(v, l):
            n0 = where[f"gu{l}_0"]
            v.memset(spare[:, 0:1], 0.0).then_inc(sem(f"f{l}_free"), 2)
            with v.Fori(0, FT // 2) as j:
                for s in range(2):
                    slot = (n0 + s) % 2
                    v.wait_ge(sem(f"f{l}_silu"), j * 2 + after(f"f{l}_silu", s + 1))
                    v.wait_ge(panel_used, j * 2 + (n0 + s + 1))
                    v.wait_ge(sem(f"f{l}_alo"), j * 2 + after(f"f{l}_alo", s + 1))
                    v.tensor_tensor(prod[:, s, :], gsil[:, s, :], ps[:, 4 * s + 1, :], ALU.mult).then_inc(sem(f"f{l}_free"), 1)
                    v.wait_ge(sem("w_hi"), j * 2 + (n0 + s + 3 - PIECE0))
                    v.tensor_tensor(w_lo[:, slot, :], raw[slot], w_hi[:, slot, :].bitcast(F32), ALU.subtract).then_inc(sem("w_lo"), 1)
            split["v"] = n0 + FT + 2

        def ffn_up_pool(g, l):
            g.memset(spare[:, 1:2], 0.0).then_inc(sem(f"f{l}_alo"), 2)
            with g.Fori(0, FT // 2) as j:
                for s in range(2):
                    at = bass.ds(j * (2 * SEQ) + s * SEQ, SEQ)
                    g.wait_ge(sem(f"f{l}_free"), j * 2 + after(f"f{l}_free", s + 3))
                    g.tensor_copy(aT[0][:, at], prod[:, s, :]).then_inc(sem(f"f{l}_ahi"), 1)
                    g.wait_ge(sem(f"f{l}_ahi"), j * 2 + after(f"f{l}_ahi", s + 1))
                    g.tensor_tensor(aT[1][:, at], prod[:, s, :], aT[0][:, at].bitcast(F32), ALU.subtract).then_inc(sem(f"f{l}_alo"), 1)

        def ffn_down_pe(pe, l):
            pe.wait_ge(sem(f"f{l}_free"), after(f"f{l}_free", 2 + FT))
            for j in range(FT // 2):
                w = take_split(pe, f"dn{l}_{j}", 2)
                for kk in range(2):
                    k = 2 * j + kk
                    pe.wait_ge(sem(f"f{l}_alo"), after(f"f{l}_alo", 2 + k + 1))
                    for half in range(2):
                        for i in range(TT):
                            ins = product(pe, ps[:, 4 * half + i, :], of(aT, slice(k * SEQ + i * P, k * SEQ + (i + 1) * P)),
                                          of(w, kk, slice(half * 512, (half + 1) * 512)), k == 0, k == FT - 1)
                            if k == FT - 1 and not (half == 1 and i == TT - 1):
                                ins.then_inc(sem(f"d{l}_mm"), 1)
                ins.then_inc(panel_used, 1)

        def down_dve(v, l):
            pieces_lo(v, f"dn{l}_{FT // 2 - 1}", 1)
            for half in range(2):
                for i in range(TT):
                    if half == 1 and i == TT - 1:
                        v.wait_ge(panel_used, where[f"dn{l}_{FT // 2 - 1}"] + 1)
                    else:
                        v.wait_ge(sem(f"d{l}_mm"), after(f"d{l}_mm", 4 * half + i + 1))
                    v.tensor_tensor(x[:, i, half * 512:(half + 1) * 512], ps[:, 4 * half + i, :],
                                         x[:, i, half * 512:(half + 1) * 512], ALU.add).then_inc(sem(f"d{l}_x"), 1)

        v_rows = rows(high_e)
        bias_ring = reg(at_f, 4, BAND_W)
        cs = Space(at_f + 2048, at_f + 2048 + 1200)
        cq_scaled = cs(1)
        c_tmp = cs(2, CH // 2, CD)
        c_ss, c_rt, c_r = cs(2, CH // 2), cs(2, CH // 2), cs(2, CH // 2)
        c_max, c_neg, c_sum, c_rec = cs(2, TT), cs(2, TT), cs(2, TT), cs(2, TT)
        ck_rows = rows(high_b)
        cqT, ckT = feat(high_c), feat(high_d)
        p_c = [reg(arena + 2048 * n, TT, SEQ) for n in range(2)]
        pT_c = [reg(at_b + 2048 * n, TT, SEQ) for n in range(2)]
        c_oT = hT

        def ca_proj_pe(pe):
            def bank_free(n):
                if n < 8:
                    ready_T(pe, "c", n)
                else:
                    pe.wait_ge(sem("c_rows"), n - 7)
            for p in range(6):
                rows_pe(pe, "ca", f"ca{p}", hT, TT, 4 * (p % 2),
                        ready=(lambda k: ready_T(pe, "c", k)) if p == 0 else None,
                        bank_free=lambda i: bank_free(4 * p + i))

        def ca_proj_act(a):
            for n in range(16):
                if n % 4 == 0:
                    pieces_hi(a, f"ca{n // 4}_1", 2)
                rows_wait(a, "ca", f"ca{n // 4}", TT, n // 4, n % 4)
                if n >= 2:
                    a.wait_ge(sem("c_rows"), n - 1)
                a.activation(c_tmp[:, n % 2].rearrange("p a b -> p (a b)"), ps[:, n % 8, :], ACT.Square).then_inc(sem("c_sqs"), 1)
                a.wait_ge(sem("c_ss"), n + 1)
                a.activation(c_rt[:, n % 2, :], c_ss[:, n % 2, :], ACT.Sqrt, bias=pcol("eps"), scale=1.0 / CD).then_inc(sem("ca_root"), 1)
            for n in range(16, 24):
                if n % 4 == 0:
                    pieces_hi(a, "ca5_1", n // 4 - 4)
                rows_wait(a, "ca", f"ca{n // 4}", TT, n // 4, n % 4)
                c0 = (n // 4 - 4) * 512
                a.activation(v_rows[:, n % 4, c0:c0 + 512], ps[:, n % 8, :], ACT.Copy).then_inc(sem("c_v"), 1)

        def ca_proj_dve(v):
            link(v, v.tensor_scalar(cq_scaled, pcol("cq_g"), CD ** -0.5, None, ALU.mult), "c_scale")
            for n in range(16):
                if n % 4 == 0:
                    pieces_lo(v, f"ca{n // 4}_1", 2)
                v.wait_ge(sem("c_sqs"), n + 1)
                v.tensor_reduce(c_ss[:, n % 2, :], c_tmp[:, n % 2], AX, ALU.add).then_inc(sem("c_ss"), 1)
                v.wait_ge(sem("ca_root"), n + 1)
                link(v, v.reciprocal(c_r[:, n % 2, :], c_rt[:, n % 2, :]), "dve_step")
                dst = (q_rows if n < 8 else ck_rows)[:, n % 4, (n // 4 % 2) * 512:(n // 4 % 2 + 1) * 512]
                v.tensor_tensor(dst.rearrange("p (h n) -> p h n", n=CD), ps[:, n % 8, :].rearrange("p (h n) -> p h n", n=CD),
                                     bc(c_r[:, n % 2, :], 2, CD), ALU.mult).then_inc(sem("c_rows"), 1)

        def ca_turn_pe(pe):
            for m in range(16):
                if m < 8:
                    pe.wait_ge(sem("c_v"), m + 1)
                    if m == 0:
                        pe.wait_ge(sem("c_rows"), 16)
                else:
                    pe.wait_ge(sem(f"c_T{'av'[m % 2]}"), after(f"c_T{'av'[m % 2]}", (m - 8) // 2 + 1))
                for i in range(TT):
                    ins = pe.transpose(ps[:, m % 8, i * P:(i + 1) * P], (q_rows if m < 8 else ck_rows)[:, i, (m % 8) * P:(m % 8 + 1) * P], ident)
                ins.then_inc(sem("ca_turned"), 1)

        def ca_turn_evac(eng, act):
            for m in range(0 if act else 1, 16, 2):
                eng.wait_ge(sem("ca_turned"), m + 1)
                dst, src = (cqT if m < 8 else ckT)[:, m % 8, :], ps[:, m % 8, :]
                if m < 8:
                    dst, src = dst.rearrange("p (i n) -> p i n", i=TT), src.rearrange("p (i n) -> p i n", i=TT)[:, :, ::-1]
                scale = cq_scaled if m < 8 else pcol("ck_g")
                if act:
                    if m == 0:
                        eng.wait_ge(sem("c_scale"), 1)
                    eng.activation(dst, src, ACT.Copy, scale=scale).then_inc(sem("c_Ta"), 1)
                else:
                    eng.tensor_scalar(dst, src, scale, None, ALU.mult).then_inc(sem("c_Tv"), 1)

        def ca_scores_pe(pe, h):
            r = slice(64 * (h % 2), 64 * (h % 2) + 64)
            if h == 0:
                pe.wait_ge(sem("c_Ta"), 8)
                pe.wait_ge(sem("c_Tv"), 8)
            for i in range(TT):
                if h > 0:
                    pe.wait_ge(sem("c_s2"), 4 * (h - 1) + i + 1)
                n = (i + 1) * P
                pe.matmul(ps[:, i, 0:n], cqT[r, h // 2, i * P:(i + 1) * P], ckT[r, h // 2, 0:n], start=True, stop=True).then_inc(sem("c_s"), 1)

        def ca_turn_p_pe(pe, h):
            for s in range(TT):
                m = 4 * h + s
                if m >= 3:
                    pe.wait_ge(sem(COPY[(m - 3) % 4][0]), 2 * ((m - 3) // 4) + COPY[(m - 3) % 4][1])
                for i in range(s, TT):
                    if s == 0:
                        pe.wait_ge(sem("c_p"), 4 * h + i + 1)
                    ins = pe.transpose(ps[:, 4 + m % 3, i * P:(i + 1) * P], p_c[h % 2][:, i, s * P:(s + 1) * P], ident)
                ins.then_inc(sem("c_tr"), 1)

        def ca_values_pe(pe, h):
            r = slice(64 * (h % 2), 64 * (h % 2) + 64)
            if h > 0:
                pe.wait_ge(sem("c_ol"), h)
            for s in range(TT):
                pe.wait_ge(sem(COPY[s][0]), 2 * h + COPY[s][1])
                ins = pe.matmul(ps[r, 7, s * P:SEQ], v_rows[:, s, h * CD:(h + 1) * CD], pT_c[h % 2][:, s, s * P:SEQ],
                                start=(s == 0), stop=(s == TT - 1), skip_group_check=True)
            ins.then_inc(sem("c_o"), 1)

        COPY = [("c_pa", 1), ("c_pv", 1), ("c_pv", 2), ("c_pa", 2)]

        def ca_copy(eng, h, s):
            eng.wait_ge(sem("c_tr"), 4 * h + s + 1)
            if h >= 2:
                eng.wait_ge(sem("c_o"), h - 1)
            dst, src = pT_c[h % 2][:, s, s * P:SEQ], ps[:, 4 + (4 * h + s) % 3, s * P:SEQ]
            if COPY[s][0] == "c_pa":
                eng.activation(dst, src, ACT.Copy).then_inc(sem("c_pa"), 1)
            else:
                eng.tensor_copy(dst, src).then_inc(sem("c_pv"), 1)

        def ca_pe(pe):
            ca_scores_pe(pe, 0)
            ca_scores_pe(pe, 1)
            for h in range(CH):
                ca_turn_p_pe(pe, h)
                if h + 2 < CH:
                    ca_scores_pe(pe, h + 2)
                ca_values_pe(pe, h)

        def ca_sp(sp, h):
            if h == 0:
                sp.wait_ge(sem("c_rows"), 1)
            if h >= 4:
                sp.wait_ge(sem("c_s2"), 4 * (h - 3))
            e = A["rel_rows"]
            src = bass.AP(e.tensor, h * BAND_E, [[1, P], [1, BAND_W]])
            sp.dma_start(bias_ring[:, h % 4, :], src).then_inc(sem(f"bias_in{h % 4}"), 16)

        def ca_act(a):
            def exps(h):
                a.wait_ge(sem("c_max"), h + 1)
                for i in range(TT):
                    n = (i + 1) * P
                    a.activation(p_c[h % 2][:, i, 0:n], p_c[h % 2][:, i, 0:n], ACT.Exp, bias=c_neg[:, h % 2, i:i + 1],
                                      accum_out=c_sum[:, h % 2, i:i + 1]).then_inc(sem("c_exp"), 1)
            exps(0)
            for h in range(CH):
                ca_copy(a, h, 0)
                ca_copy(a, h, 3)
                if h + 1 < CH:
                    exps(h + 1)
                a.wait_ge(sem("c_o"), h + 1)
                r = slice(64 * (h % 2), 64 * (h % 2) + 64)
                a.activation(c_oT[0][r, h // 2, :].rearrange("p (i n) -> p i n", i=TT),
                                  ps[r, 7, :].rearrange("p (i n) -> p i n", i=TT)[:, :, ::-1], ACT.Copy).then_inc(sem("c_oc"), 1)

        def ca_dve(v):
            def sums(h):
                v.wait_ge(sem(f"bias_in{h % 4}"), after(f"bias_in{h % 4}", 16 * (h // 4 + 1)))
                link(v, v.memset(bias_ring[64:P, h % 4, BAND_W - 64:BAND_W], -1e30), "dve_step")
                if h >= 2:
                    v.wait_ge(sem("c_tr"), 4 * (h - 1))
                for i in range(TT):
                    n = (i + 1) * P
                    v.wait_ge(sem("c_s"), 4 * h + i + 1)
                    v.tensor_tensor_reduce(out=p_c[h % 2][:, i, 0:n], in0=ps[:, i, 0:n],
                                                in1=bias_ring[:, h % 4, BAND_W - n:BAND_W], scale=1.0, scalar=-3.0e38,
                                                op0=ALU.add, op1=ALU.max, accum_out=c_max[:, h % 2, i:i + 1]).then_inc(sem("c_s2"), 1)
                v.wait_ge(sem("c_s2"), 4 * h + 4)
                v.tensor_scalar(c_neg[:, h % 2, :], c_max[:, h % 2, :], -1.0, None, ALU.mult).then_inc(sem("c_max"), 1)

            def out_lo(h):
                r = slice(64 * (h % 2), 64 * (h % 2) + 64)
                v.wait_ge(sem("c_oc"), h + 1)
                v.tensor_tensor(c_oT[1][r, h // 2, :].rearrange("p (i n) -> p i n", i=TT),
                                ps[r, 7, :].rearrange("p (i n) -> p i n", i=TT)[:, :, ::-1],
                                c_oT[0][r, h // 2, :].bitcast(F32).rearrange("p (i n) -> p i n", i=TT), ALU.subtract).then_inc(sem("c_ol"), 1)

            def rescale(h):
                v.wait_ge(sem("c_exp"), 4 * h + 4)
                link(v, v.reciprocal(c_rec[:, h % 2, :], c_sum[:, h % 2, :]), "dve_step")
                for i in range(TT):
                    n = (i + 1) * P
                    v.tensor_scalar(p_c[h % 2][:, i, 0:n], p_c[h % 2][:, i, 0:n], c_rec[:, h % 2, i:i + 1], None, ALU.mult).then_inc(sem("c_p"), 1)

            sums(0)
            sums(1)
            rescale(0)
            for h in range(CH):
                if h > 0:
                    out_lo(h - 1)
                ca_copy(v, h, 1)
                ca_copy(v, h, 2)
                if h + 1 < CH:
                    rescale(h + 1)
                if h + 2 < CH:
                    sums(h + 2)
            out_lo(CH - 1)

        def load_panel(sp, name):
            n = where[name]
            if n >= PIECE0 + 2:
                sp.wait_ge(sem("w_lo"), n - 1 - PIECE0)
            elif n >= 2:
                sp.wait_ge(panel_used, n - 1)
            slot = raw[n % 2] if n >= PIECE0 else slots[n % 2]
            for dst, src in panels[n][1]:
                sp.dma_start(dst(slot), src).then_inc(slot_landed[n % 2], 16)

        def load_pieces(sp, first, last):
            for n in range(where[first], where[last] + 1):
                load_panel(sp, panels[n][0])

        block = ctx.enter_context(nc.Block())
        abo, cao = ["abo0", "abo1"], ["cao0", "cao1"]
        xo = [[f"xo{l}0", f"xo{l}1"] for l in range(DEPTH)]

        @block.sync
        def _(sp):
            sp.dma_start(par, A["par"]).then_inc(sem("par_in"), 16)
            sp.dma_start(x0, A["x"].rearrange("(i p) n -> p i n", p=P)).then_inc(sem("x_in"), 16)
            sp.dma_start(con, A["con"]).then_inc(sem("con_in"), 16)
            load_panel(sp, "ab0")
            load_panel(sp, "ab1")
            sp.dma_start(w_ab, A["ab_w_in"][:, 2560:2568].rearrange("(k p) n -> p k n", p=P)).then_inc(sem("wab_in"), 16)
            sp.dma_start(s5_bc, A["s5_bc"]).then_inc(sem("bc_in"), 16)
            for name in ("ab2", "ab3", "ab4", "glu", "abo0"):
                load_panel(sp, name)
                if name == "glu":
                    s5_u_sp(sp)
            load_panel(sp, "abo1")
            xres_sp(sp)
            mem_sp(sp)
            load_pieces(sp, "kv00_0", "ca5_1")
            for h in range(4):
                ca_sp(sp, h)
            load_pieces(sp, "cao0_0", "cao0_1")
            for h in range(4, CH):
                ca_sp(sp, h)
            load_pieces(sp, "cao1_0", f"dn1_{FT // 2 - 1}")
            for i in range(TT):
                sp.wait_ge(sem("d1_x"), after("d1_x", TT + i + 1))
                sp.dma_start(A["out"][i * P:(i + 1) * P, :], x[:, i, :]).then_inc(sem("stored"), 16)
            sp.wait_ge(sem("stored"), 16 * TT)

        @block.tensor
        def _(pe):
            pe.wait_ge(sem("con_in"), 16)
            norm_pe(pe, "n0", x0, h0)
            for p in range(4):
                ab_groups_pe(pe, p)
            ab_groups_pe(pe, 4)
            logits_pe(pe)
            s5_tables_pe(pe)
            s5_states_pe(pe)
            s5_tm_pe(pe)
            s5_out_pe(pe)
            s5_back_pe(pe)
            s5_glu_pe(pe)
            gates_pe(pe)
            gdn_turn_pe(pe, 0)
            gdn_back_pe(pe, 0)
            for i in range(TT):
                if i + 1 < TT:
                    gdn_turn_pe(pe, i + 1)
                gdn_prod_pe(pe, i)
                if i + 1 < TT:
                    gdn_back_pe(pe, i + 1)
            solve_pe(pe)
            uw_pe(pe)
            rec_pe(pe)
            gout_pe(pe)

            def cat_ready(k):
                if k == 0:
                    pe.wait_ge(sem("gdn_done"), GH)
            outproj_pe(pe, "mo", abo, catT, cat_ready)
            pe.wait_ge(sem("mo_x"), after("mo_x", 8))
            norm_pe(pe, "m", mem_x, mem_x)
            for l in range(DEPTH):
                if l == 0:
                    pe.wait_ge(sem("mem_lo"), 1)
                else:
                    pe.wait_ge(sem("mem_lo"), 2)
                kv_pe(pe, l)
                kv_turn_pe(pe, l)
                pe.wait_ge(sem(f"kv{l}_v"), after(f"kv{l}_v", 4))
                pe.wait_ge(sem(f"kv{l}_kTa"), after(f"kv{l}_kTa", 4))
                pe.wait_ge(sem(f"kv{l}_kTv"), after(f"kv{l}_kTv", 4))
                norm_pe(pe, f"x{l}", x, h_rows)
                xq_pe(pe, l)
                xa_pe(pe, l)

                pe.wait_ge(sem(f"xa{l}_ov"), after(f"xa{l}_ov", KT))
                split_outproj_pe(pe, f"xo{l}", xo[l], oT)
                pe.wait_ge(sem(f"xo{l}_x"), after(f"xo{l}_x", 8))
                norm_pe(pe, f"f{l}", x, h_rows)
                for k in range(KT):
                    ready_T(pe, f"f{l}", k)
                ffn_up_pe(pe, l)
                ffn_down_pe(pe, l)
                if l == 0:
                    pe.wait_ge(sem("d0_x"), after("d0_x", 8))
                    norm_pe(pe, "c", x, h_rows)
                    ca_proj_pe(pe)
                    ca_turn_pe(pe)
                    ca_pe(pe)
                    pe.wait_ge(sem("c_ol"), CH)
                    split_outproj_pe(pe, "co", cao, c_oT)
                    pe.wait_ge(sem("co_x"), after("co_x", 8))

        @block.scalar
        def _(a):
            a.wait_ge(sem("x_in"), 16)
            squares_act(a, "n0", x0, sq_junk0, ss2)
            a.wait_ge(sem("par_in"), 16)
            norm_act(a, "n0", x0, h0, ss2, hT0, "ab_g")
            s5_params_act(a)
            for n in range(12):
                silu_act(a, n)
            for n in range(12, 16):
                gate_act(a, n)
            for n in range(16, 20):
                u_act(a, n)
            s5_tables_act(a)
            s5_tm_act(a)
            s5_out_act(a)
            s5_glu_act(a)
            gates_act(a)
            gdn_tok_act(a, 0)
            gdn_back_act(a, 0)
            for i in range(TT):
                if i + 1 < TT:
                    gdn_tok_act(a, i + 1)
                gdn_dec_act(a, i)
                if i + 1 < TT:
                    gdn_back_act(a, i + 1)
            solve_act(a)
            uw_act(a)
            rec_act(a)
            gout_act(a)
            a.wait_ge(sem("mem_in"), 16)
            squares_act(a, "m", mem_x, sq_junk, rms_m)
            norm_act(a, "m", mem_x, mem_x, rms_m, memT, "mem_g", ("kv00_1",))
            a.wait_ge(sem("m_outa"), after("m_outa", KT // 2))
            a.wait_ge(sem("m_outv"), after("m_outv", KT // 2))
            mem_split_act(a)
            squares_act(a, "x0", x, sq_junk, ss2, "mo_x")
            for l in range(DEPTH):
                if l == 1:
                    squares_act(a, "x1", x, sq_junk, ss2, "co_x", "cao1_1")
                pieces_hi(a, f"kv{l}0_1")
                kv_act(a, l)
                norm_act(a, f"x{l}", x, h_rows, ss2, hT, f"xa_g{l}", (f"kv{l}3_1", 2))
                xq_act(a, l)
                xa_act(a, l)
                squares_act(a, f"f{l}", x, sq_junk, ss2, f"xo{l}_x", f"xo{l}1_1")
                norm_act(a, f"f{l}", x, h_rows, ss2, hT, f"f_g{l}", (f"xo{l}1_1", 2))
                ffn_up_act(a, l)
                pieces_hi(a, f"dn{l}_{FT // 2 - 1}", 1)
                if l == 0:
                    squares_act(a, "c", x, gs_junk, ss2, "d0_x")
                    norm_act(a, "c", x, h_rows, ss2, hT, "c_g", (f"dn0_{FT // 2 - 1}", 2))
                    ca_proj_act(a)
                    ca_turn_evac(a, True)
                    pieces_hi(a, "ca5_1", 2)
                    ca_act(a)
                    mem_split_act(a)

        @block.vector
        def _(v):
            v.wait_ge(sem("x_in"), 16)
            v.wait_ge(sem("par_in"), 16)
            norm_dve(v, "n0", x0, h0, ss2, hT0, "ab_g")
            v.wait_ge(sem("con_in"), 16)
            for n in range(4):
                conv_dve(v, n)
            s5_g_dve(v)
            for n in range(4, 12):
                conv_dve(v, n)
            logits_dve(v)
            s5_v_dve(v)
            s5_states_dve(v)
            s5_out_dve(v)
            s5_glu_dve(v)
            gates_dve(v)
            gdn_tok_dve(v, 0)
            for i in range(TT):
                if i + 1 < TT:
                    gdn_tok_dve(v, i + 1)
                gdn_prod_dve(v, i)
            solve_dve(v)
            uw_dve(v)
            rec_dve(v)
            gout_dve(v)
            v.wait_ge(sem("x_in"), 32)
            outproj_dve(v, "mo", abo, x)
            norm_dve(v, "m", mem_x, mem_x, rms_m, memT, "mem_g", ("kv00_1",))
            mem_split_dve(v, 0)
            for l in range(DEPTH):
                kv_dve(v, l)
                norm_dve(v, f"x{l}", x, h_rows, ss2, hT, f"xa_g{l}", (f"kv{l}3_1", 2))
                xq_dve(v, l)
                xa_dve(v, l)
                outproj_dve(v, f"xo{l}", xo[l], x)
                norm_dve(v, f"f{l}", x, h_rows, ss2, hT, f"f_g{l}", (f"xo{l}1_1", 2))
                ffn_up_dve(v, l)
                down_dve(v, l)
                if l == 0:
                    norm_dve(v, "c", x, h_rows, ss2, hT, "c_g", (f"dn0_{FT // 2 - 1}", 2))
                    ca_proj_dve(v)
                    pieces_lo(v, "ca5_1", 1)
                    ca_turn_evac(v, False)
                    pieces_lo(v, "ca5_1", 2)
                    ca_dve(v)
                    mem_split_dve(v, 1)
                    outproj_dve(v, "co", cao, x)

        @block.gpsimd
        def _(g):
            g.wait_ge(sem("par_in"), 16)
            s5_params_pool(g)
            g.wait_ge(sem("con_in"), 16)
            solve_masks_pool(g)
            ffn_up_pool(g, 0)
            ffn_up_pool(g, 1)


def _layout(inputs):
    import numpy as np

    f = {k: np.ascontiguousarray(np.asarray(v)) for k, v in inputs.items()}

    def cols(v):
        return v.reshape(-1, P).T

    gp = lambda a: a.reshape(S5_GP, 2, S5_P).transpose(1, 2, 0).reshape(P, S5_GP)
    ri = lambda a: np.concatenate([a.T, a.T], 0)
    rep = lambda row: np.broadcast_to(row[None, :], (P, row.size))
    both = lambda a: np.concatenate([ri(a), gp(a)], 1)
    ones = np.ones((P, 1), np.float32)
    sgn = np.concatenate([-ones[:64], ones[64:]], 0)
    parts = {
        "ab_g": cols(f["ab_norm_g"][0]), "c_g": cols(f["c_norm_g"][0]), "mem_g": cols(f["mem_norm_g"]),
        "xa_g0": cols(f["xa_norm_g"][0]), "xa_g1": cols(f["xa_norm_g"][1]), "f_g0": cols(f["f_norm_g"][0]), "f_g1": cols(f["f_norm_g"][1]),
        "s5_d": cols(f["s5_d"][0].reshape(-1)), "b_glu": cols(f["s5_b_glu"][0]),
        "conv": f["gdn_conv_w"][0].reshape(4, 12, P).transpose(2, 0, 1).reshape(P, 48),
        "gdn_g": cols(f["gdn_out_norm_g"][0]),
        "xq_g0": cols(f["xa_q_norm_g"][0]), "xq_g1": cols(f["xa_q_norm_g"][1]),
        "xk_g0": cols(f["xa_k_norm_g"][0]), "xk_g1": cols(f["xa_k_norm_g"][1]),
        "cq_g": np.concatenate([f["c_q_norm_g"][0]] * 2)[:, None], "ck_g": np.concatenate([f["c_k_norm_g"][0]] * 2)[:, None],
        "dt_bias": rep(f["gdn_dt_bias"][0]), "a_log": rep(f["gdn_a_log"][0]),
        "a_re": both(f["s5_a_re"][0]), "a_im": both(f["s5_a_im"][0]),
        "log_dt": both(np.broadcast_to(f["s5_log_dt"][0][:, None], (S5_G, S5_P))),
        "eps": ones * EPS, "half_pi": ones * (TWO_PI / 4), "sgn": sgn, "one": ones, "nsgn": -sgn,
    }
    par = np.empty((P, N_PAR), np.float32)
    for name, (at, n) in PAR.items():
        par[:, at:at + n] = parts[name]
    j, t = np.meshgrid(np.arange(P), np.arange(P), indexing="ij")
    same = (j // CHUNK) == (t // CHUNK)
    con = {"ident": j == t, "inc": same & (j <= t), "neg": np.where(same & (j <= t), 0.0, -1e30),
           "same": same, "first": j < CHUNK, "second": j >= CHUNK}
    for l in range(1, 7):
        s = 2 ** (l - 1)
        con[f"m{l}"] = (j // (2 * s) == t // (2 * s)) & (t % (2 * s) >= s) & (j % (2 * s) < s)
    con = np.concatenate([np.asarray(con[n], np.float32) for n in CON], 1)
    bt = [f[n][0].transpose(1, 0, 2) for n in ("s5_b_re", "s5_b_im")]
    ct = [f[n][0].transpose(2, 0, 1) for n in ("s5_c_re", "s5_c_im")]
    cg = [f[n][0].reshape(S5_GP, 2, S5_CH, S5_P).transpose(1, 3, 0, 2).reshape(P, -1) for n in ("s5_c_re", "s5_c_im")]
    s5_bc = np.concatenate([np.concatenate([bt[0], bt[1]], 0).reshape(P, -1), np.concatenate([bt[1], bt[0]], 0).reshape(P, -1),
                            np.concatenate([ct[0], ct[1]], 0).reshape(P, -1), cg[0], cg[1]], 1)
    rel = f["c_rel_bias"][0][:, np.clip(BAND_W - 1 - np.arange(BAND_E), -REL, REL) + REL]
    return {
        "x": f["x"][0], "mem": f["mem"][0], "par": par, "con": con, "s5_bc": s5_bc, "rel_rows": rel,
        "ab_w_in": f["ab_w_in"][0], "ab_w_out": f["ab_w_out"][0], "s5_w_glu": f["s5_w_glu"][0],
        "c_w_qkv": f["c_w_qkv"][0], "c_w_out": f["c_w_out"][0],
        "xa_w_q": f["xa_w_q"], "xa_w_kv": f["xa_w_kv"], "xa_w_out": f["xa_w_out"],
        "f_w_gate": f["f_w_gate"], "f_w_up": f["f_w_up"], "f_w_down": f["f_w_down"],
    }


def kernel(**inputs):
    import numpy as np
    import concourse.bacc as bacc
    from concourse.bass_utils import run_bass_kernel_spmd

    nc = bacc.Bacc("TRN2", target_bir_lowering=False, num_devices=1)
    arrays = {f"in_{k}": np.ascontiguousarray(v) for k, v in _layout(inputs).items()}
    A = {k[3:]: nc.dram_tensor(k, v.shape, mybir.dt.from_np(v.dtype), kind="ExternalInput").ap() for k, v in arrays.items()}
    A["out"] = nc.dram_tensor("out_0", (SEQ, D), F32, kind="ExternalOutput").ap()
    build_program(nc, A)
    r = run_bass_kernel_spmd(nc, [arrays], core_ids=[0])
    return r.results[0]["out_0"].reshape(1, SEQ, D)
```

```python
from contextlib import ExitStack

import concourse.bass as bass
from concourse import mybir

F32 = mybir.dt.float32
F32R = mybir.dt.float32r
ALU = mybir.AluOpType
ACT = mybir.ActivationFunctionType
AX = mybir.AxisListType.X

P = 128
D = 1024
SEQ = 512
N_MEM = 256
DEPTH = 2
KT = D // P
TT = SEQ // P
MT = N_MEM // P
CHUNK = 64
EPS = 1e-6
S5_W = D // 2
S5_CH = 16
S5_G = S5_W // S5_CH
S5_P = 64
S5_L = 8
S5_C = SEQ // S5_L
S5_GP = S5_G // 2
S5_COLS = S5_G + S5_GP
GH = 4
GD = 128
NCH = SEQ // CHUNK
CH = 16
CD = D // CH
XH = 4
XD = D // XH
FH = -(-8 * D // (3 * 256)) * 256
FT = FH // P
REL = 128
BAND_W = SEQ
BAND_E = BAND_W + P - 1

PAR = {}
_at = 0
for _name, _n in (
    ("ab_g", KT), ("c_g", KT), ("mem_g", KT), ("xa_g0", KT), ("xa_g1", KT), ("f_g0", KT), ("f_g1", KT),
    ("s5_d", 4), ("b_glu", 4), ("conv", 48), ("gdn_g", 1), ("xq_g0", 2), ("xq_g1", 2), ("xk_g0", 2), ("xk_g1", 2),
    ("cq_g", 1), ("ck_g", 1), ("dt_bias", GH), ("a_log", GH), ("a_re", S5_COLS), ("a_im", S5_COLS), ("log_dt", S5_COLS),
    ("eps", 1), ("half_pi", 1), ("sgn", 1), ("one", 1), ("nsgn", 1),
):
    PAR[_name] = (_at, _n)
    _at += _n
N_PAR = _at
CON = {n: i * P for i, n in enumerate(["ident", "inc", "neg", "m1", "m2", "m3", "m4", "m5", "m6", "same", "first", "second"])}
N_CON = len(CON) * P
TOP = 53120

TWO_PI = 6.283185307179586
PI_PARTS = (6.28125, 0.0019353071693331003, 1.0253114e-11)
ROUND = 12582912.0


def build_program(nc, A):
    ctx = ExitStack()
    with ctx:
        def tensor_at(name, at, dtype, *shape):
            assert at % 8 == 0
            with nc.sbuf_tensor(f"below_{name}", [P, at], F32), nc.sbuf_tensor(name, [P, *shape], dtype) as v:
                return v[(slice(None),) * (1 + len(shape))]

        def rounded(name, at, *shape):
            return tensor_at(name, at, F32R, *shape)

        with nc.sbuf_tensor("params", [P, N_PAR], F32) as par:
            par = par[:, :]
        memT = tensor_at("memT", N_PAR, F32, KT, N_MEM)
        SB0 = N_PAR + KT * N_MEM
        sb = tensor_at("sb", SB0, F32, TOP - SB0)
        ps = ctx.enter_context(nc.psum_tensor("ps", [P, 8, 512], F32))
        sems = {}

        PER_LAYER = {
            "kv_sq": 8, "kv_rt": 1, "kv_v": 4, "kv_kTa": 4, "kv_k": 4, "kv_kTv": 4, "kv_turned": 8,
            "xq_sq": 16, "xq_rt": 2, "xq_qTa": 4, "xq_q": 8, "xq_qTv": 4, "xq_turned": 8,
            "xa_s": 4, "xa_exp": 16, "xa_max": 4, "xa_p": 4, "xa_tr": 8, "xa_pTa": 4, "xa_pTv": 4,
            "xa_o": 8, "xa_oa": 8, "xa_ov": 8,
            "f_mm": FT, "f_silu": FT, "f_free": FT + 2, "f_ahi": FT, "f_alo": FT + 2,
        }
        SERIES = {"norm": ("n0", "m", "x0", "f0", "c", "x1", "f1"), "back": ("mo", "kv0", "xq0", "xo0", "d0", "ca", "co", "kv1", "xq1", "xo1", "d1")}

        GOES_ON = {**{f"bias_in{i}": (f"x_tile{i}", 16) for i in range(TT)},
                   "glu_landed": ("wab_in", 16), "g_v": ("u_s", 8),
                   "cat_hi": ("go_sq", TT), "cat_lo": ("go_n", TT), "mem_kept": ("cat_s5", 1),
                   "s5_pad": ("conv", 12), "y_v": ("conv", 20), "y_a": ("u_s", 4)}

        def in_series(what, tail, tag):
            if what == "back":
                if tail == "mm":
                    return {"kv": 4 * (MT - 1), "ca": 6 * (TT - 1), "d": 2 * TT - 1}.get(tag.rstrip("01"), 2 * (TT - 1))
                return 2 * TT if tail == "x" and tag.rstrip("01") in ("mo", "xo", "d", "co") else None
            n = MT if tag == "m" else TT
            return {"sq": 2 * n, "sum": 1, "root": 1, "rinv": 1, "hv": n,
                    "turned": KT, "outa": KT, "outv": KT}.get(tail)

        def named(name):
            if name in GOES_ON:
                return GOES_ON[name]
            head, _, tail = name.partition("_")
            for what, tags in SERIES.items():
                if head in tags and in_series(what, tail, head) is not None:
                    return f"{what}_{tail}", sum(in_series(what, tail, t) or 0 for t in tags[:tags.index(head)])
            if head[-1].isdigit() and f"{head[:-1]}_{tail}" in PER_LAYER:
                base_name = f"{head[:-1]}_{tail}"
                return base_name, int(head[-1]) * PER_LAYER[base_name]
            return name, 0

        def sem(name):
            name = named(name)[0]
            if name not in sems:
                sems[name] = ctx.enter_context(nc.semaphore(name))
            return sems[name]

        def reg(at, *shape):
            n = 1
            for s in shape:
                n *= s
            v = sb[:, at - SB0:at - SB0 + n]
            if len(shape) == 2:
                v = v.rearrange("p (a b) -> p a b", a=shape[0])
            if len(shape) == 3:
                v = v.rearrange("p (a b c) -> p a b c", a=shape[0], b=shape[1])
            if len(shape) == 4:
                v = v.rearrange("p (a b c d) -> p a b c d", a=shape[0], b=shape[1], c=shape[2])
            return v

        class Space:
            def __init__(self, at, end):
                self.at, self.end = at, end

            def __call__(self, *shape):
                n = 1
                for s in shape:
                    n *= s
                v = reg(self.at, *shape)
                self.at += n
                assert self.at <= self.end, (self.at, self.end)
                return v

        fixed = Space(SB0, 14900)
        con = fixed(N_CON)
        slots_at = fixed.at
        slots = [fixed(4096), fixed(4096)]
        ss2 = fixed(2, TT)
        nrm = fixed(2, TT)
        rinv = fixed(TT)
        spare = fixed(2)
        warm = fixed(1)
        rms_m = fixed(3, MT)
        top = TOP
        base = -(-fixed.at // 8) * 8

        def pcol(name, i=0):
            return par[:, PAR[name][0] + i:PAR[name][0] + i + 1]

        def pcols(name):
            return par[:, PAR[name][0]:PAR[name][0] + PAR[name][1]]

        def ccol(name):
            return con[:, CON[name]:CON[name] + P]

        ident = ccol("ident")

        panels = []

        def kview(w, c0, n, k0=0, nk=KT):
            return w[k0 * P:(k0 + nk) * P, c0:c0 + n].rearrange("(k p) n -> p k n", p=P)

        def full(slot, nk=KT, n=512):
            return slot[:, 0:nk * n].rearrange("p (k n) -> p k n", k=nk)

        def add_panel(name, parts):
            panels.append((name, parts))

        for i, c0 in enumerate((512, 1024, 1536, 2048, 0)):
            for half in range(2):
                add_panel(f"ab{i}_{half}", [(lambda s: full(s, KT, 256), kview(A["ab_w_in"], c0 + 256 * half, 256))])
        AB_PIECES = len(panels)
        add_panel("glu", [(lambda s: full(s, 4), kview(A["s5_w_glu"], 0, 512, 0, 4))])

        def add_pieces(name, w, c0):
            for kh in range(2):
                add_panel(f"{name}_{kh}", [(lambda s: full(s, 4), kview(w, c0, 512, 4 * kh, 4))])

        def add_xa_ffn(l):
            for i in range(4):
                add_pieces(f"kv{l}{i}", A["xa_w_kv"][l], 512 * i)
            for i in range(2):
                add_pieces(f"xq{l}{i}", A["xa_w_q"][l], 512 * i)
            for i in range(2):
                add_pieces(f"xo{l}{i}", A["xa_w_out"][l], 512 * i)
            for i in range(FT):
                add_panel(f"gu{l}_{i}", [
                    (lambda s: full(s, KT, 2 * P)[:, :, 0:P], kview(A["f_w_gate"][l], P * i, P)),
                    (lambda s: full(s, KT, 2 * P)[:, :, P:2 * P], kview(A["f_w_up"][l], P * i, P))])
            for i in range(FT // 2):
                add_panel(f"dn{l}_{i}", [
                    (lambda s: full(s, 2, D)[:, 0, :], A["f_w_down"][l][2 * i * P:(2 * i + 1) * P, :]),
                    (lambda s: full(s, 2, D)[:, 1, :], A["f_w_down"][l][(2 * i + 1) * P:(2 * i + 2) * P, :])])

        PIECE0 = len(panels)
        for i in range(2):
            add_pieces(f"abo{i}", A["ab_w_out"], 512 * i)
        add_xa_ffn(0)
        for i in range(6):
            add_pieces(f"ca{i}", A["c_w_qkv"], 512 * i)
        for i in range(2):
            add_pieces(f"cao{i}", A["c_w_out"], 512 * i)
        add_xa_ffn(1)
        where = {name: n for n, (name, _) in enumerate(panels)}
        landed = []
        tally = [0, 0]
        for n, (_, parts) in enumerate(panels):
            if not AB_PIECES <= n < PIECE0:
                tally[n % 2] += 16 * len(parts)
            landed.append(tally[n % 2])
        slot_landed = [sem("slot0_landed"), sem("slot1_landed")]
        panel_used = sem("panel_used")

        def take(pe, name):
            pe.wait_ge(sem(f"{name}_landed"), after(f"{name}_landed", 16))
            return slots[whole_slot[name]]

        PIECE = 2048
        arena = base + (KT + 3 * GH + GH + KT) * SEQ
        raw_all = tensor_at("raw", slots_at, F32, 2, PIECE)
        raw = [raw_all[:, s, :] for s in range(2)]
        w_hi = rounded("w_hi", slots_at + 2 * PIECE, 2, PIECE)
        w_lo_late = rounded("w_lo", base + 8192, 2, PIECE)
        w_lo_ab = rounded("w_lo_ab", arena + 7680, 2, PIECE)

        w_lo_abo = rounded("w_lo_abo", arena + 12288, 2, PIECE)

        def w_lo(n):
            return w_lo_ab if n < PIECE0 else w_lo_abo if n <= where["abo1_1"] else w_lo_late

        def nth(n):
            return n if n < AB_PIECES else n - (PIECE0 - AB_PIECES)

        whole_slot = {"glu": 1}

        def piece_hi(a, n):
            a.wait_ge(slot_landed[n % 2], landed[n])
            if n >= 2:
                a.wait_ge(panel_used, n - 1 if n < PIECE0 else max(n - 1, PIECE0))
            a.activation(w_hi[:, n % 2, :], raw[n % 2], ACT.Copy).then_inc(sem("w_hi"), 1)

        def piece_lo(v, n):
            v.wait_ge(sem("w_hi"), nth(n) + 1)
            v.tensor_tensor(w_lo(n)[:, n % 2, :], raw[n % 2], w_hi[:, n % 2, :].bitcast(F32), ALU.subtract).then_inc(sem("w_lo"), 1)

        split = {"a": 0, "v": 0}

        def upto(name, ahead=0):
            return min(where[name] + ahead, len(panels) - 1) + 1

        def pieces_hi(a, name, ahead=0):
            for n in range(split["a"], upto(name, ahead)):
                if not AB_PIECES <= n < PIECE0:
                    piece_hi(a, n)
            split["a"] = upto(name, ahead)

        def pieces_lo(v, name, ahead=0):
            for n in range(split["v"], upto(name, ahead)):
                if not AB_PIECES <= n < PIECE0:
                    piece_lo(v, n)
            split["v"] = upto(name, ahead)

        def take_split(pe, name, nk):
            i = where[name]
            pe.wait_ge(sem("w_lo"), nth(i) + 1)
            return tuple(w[:, i % 2, :].rearrange("p (k n) -> p k n", k=nk) for w in (w_hi, w_lo(i)))

        def product(pe, out, a, b, start, stop):
            pe.matmul(out, a[0], b[0], start=start, stop=False)
            pe.matmul(out, a[0], b[1], start=False, stop=False)
            return pe.matmul(out, a[1], b[0], start=False, stop=stop)

        def of(pair, *at):
            if len(pair) == 4:
                pair, at = pair[2 * (at[0] // 4):2 * (at[0] // 4) + 2], (at[0] % 4, *at[1:])
            return tuple(v[(slice(None), *at)] for v in pair)

        def bc(ap, axis, n):
            v = ap.unsqueeze(axis)
            shape = list(v.shape)
            shape[axis] = n
            return v.broadcast_to(shape)

        count = {}

        def after(name, n):
            return n + named(name)[1]

        def link(eng, ins, name):
            ins.then_inc(sem(name), 1)
            name = named(name)[0]
            count[name] = count.get(name, 0) + 1
            eng.wait_ge(sem(name), count[name])

        def norm_rows_dve(v, t, x, h, r_in):
            n = x.shape[1]
            v.wait_ge(sem(f"{t}_sq"), after(f"{t}_sq", 2 * n))
            link(v, v.tensor_tensor(nrm[:, 0, 0:n], r_in[:, 0, 0:n], r_in[:, 1, 0:n], ALU.add), f"{t}_sum")
            v.wait_ge(sem(f"{t}_root"), after(f"{t}_root", 1))
            link(v, v.reciprocal(rinv[:, 0:n], nrm[:, 1, 0:n]), f"{t}_rinv")
            for i in range(n):
                v.tensor_scalar(h[:, i, :], x[:, i, :], rinv[:, i:i + 1], None, ALU.mult).then_inc(sem(f"{t}_hv"), 1)

        def norm_out_dve(v, t, n, dst, gain, ahead):
            pieces_lo(v, *ahead)
            for k in range(KT):
                v.wait_ge(sem(f"{t}_outa"), after(f"{t}_outa", k + 1))
                v.scalar_tensor_tensor(dst[1][:, k, :], ps[:, k, 0:n * P], pcol(gain, k), dst[0][:, k, :].bitcast(F32),
                                       ALU.mult, ALU.subtract).then_inc(sem(f"{t}_outv"), 1)

        def norm_dve(v, t, x, h, r_in, dst, gain, ahead):
            norm_rows_dve(v, t, x, h, r_in)
            norm_out_dve(v, t, x.shape[1], dst, gain, ahead)

        def norm_root_act(a, t, n):
            a.wait_ge(sem(f"{t}_sum"), after(f"{t}_sum", 1))
            a.activation(nrm[:, 1, 0:n], nrm[:, 0, 0:n], ACT.Sqrt, bias=pcol("eps"), scale=1.0 / D).then_inc(sem(f"{t}_root"), 1)

        def norm_out_act(a, t, n, dst, gain, ahead):
            pieces_hi(a, *ahead)
            for k in range(KT):
                a.wait_ge(sem(f"{t}_turned"), after(f"{t}_turned", k + 1))
                a.activation(dst[0][:, k, :], ps[:, k, 0:n * P], ACT.Copy, scale=pcol(gain, k)).then_inc(sem(f"{t}_outa"), 1)

        def norm_act(a, t, n, dst, gain, ahead):
            norm_root_act(a, t, n)
            norm_out_act(a, t, n, dst, gain, ahead)

        def norm_pe(pe, t, x, h):
            n = x.shape[1]
            for k in range(KT):
                for i in range(n):
                    if k == 0:
                        pe.wait_ge(sem(f"{t}_hv"), after(f"{t}_hv", i + 1))
                    ins = pe.transpose(ps[:, k, i * P:(i + 1) * P], h[:, i, k * P:(k + 1) * P], ident)
                ins.then_inc(sem(f"{t}_turned"), 1)

        def sqrt_table(a):
            a.activation(warm, pcol("one"), ACT.Sqrt).then_inc(sem("act_warm"), 1)
            name = "act_warm"
            count[name] = count.get(name, 0) + 1
            a.wait_ge(sem("act_warm"), count[name])

        def squares_act(a, t, x, junk, dst, ready=None, ahead=None):
            for half in range(2):
                if ahead is not None:
                    pieces_hi(a, ahead, half)
                if half == 1:
                    sqrt_table(a)
                for i in range(x.shape[1]):
                    if t == "n0":
                        a.wait_ge(sem(f"x_tile{i}"), 16)
                    if ready is not None:
                        a.wait_ge(sem(ready), after(ready, half * x.shape[1] + i + 1))
                    n = half * x.shape[1] + i
                    if n >= 2:
                        a.wait_ge(sem(f"{t}_sq"), after(f"{t}_sq", n - 1))
                    a.activation(junk[:, (n % 2) * 512:(n % 2 + 1) * 512], x[:, i, half * 512:(half + 1) * 512], ACT.Square,
                                      accum_out=dst[:, half, i:i + 1]).then_inc(sem(f"{t}_sq"), 1)
            a.wait_ge(sem(f"{t}_sq"), after(f"{t}_sq", 2 * x.shape[1]))

        def ready_T(pe, t, k):
            pe.wait_ge(sem(f"{t}_outv"), after(f"{t}_outv", k + 1))

        def rows_pe(pe, t, name, srcT, tiles, bank, ready=None, bank_free=None, between=None):
            for kh in range(2):
                if kh == 1 and between is not None:
                    between()
                w = take_split(pe, f"{name}_{kh}", 4)
                for i in range(tiles):
                    if kh == 0 and bank_free is not None:
                        bank_free(i)
                    for k in range(4):
                        kk = 4 * kh + k
                        if i == 0 and ready is not None:
                            ready(kk)
                        ins = product(pe, ps[:, bank + i, :], of(srcT, kk, slice(i * P, (i + 1) * P)), of(w, k), kk == 0, kk == KT - 1)
                    if i == tiles - 1:
                        ins.then_inc(panel_used, 1)
                    elif kh == 1:
                        ins.then_inc(sem(f"{t}_mm"), 1)

        def rows_wait(eng, t, name, tiles, j, i):
            if i < tiles - 1:
                eng.wait_ge(sem(f"{t}_mm"), after(f"{t}_mm", j * (tiles - 1) + i + 1))
            else:
                eng.wait_ge(panel_used, where[f"{name}_1"] + 1)

        def split_outproj_pe(pe, t, names, srcT):
            for half, name in enumerate(names):
                rows_pe(pe, t, name, srcT, TT, 4 * half)

        def outproj_dve(v, t, names, x):
            for half in range(2):
                pieces_lo(v, f"{names[1]}_1", half)
                for i in range(TT):
                    rows_wait(v, t, names[half], TT, half, i)
                    v.tensor_tensor(x[:, i, half * 512:(half + 1) * 512], ps[:, 4 * half + i, :],
                                         x[:, i, half * 512:(half + 1) * 512], ALU.add).then_inc(sem(f"{t}_x"), 1)

        mix = Space(base, top)
        catT = mix(KT, SEQ)
        qkvT = mix(3 * GH, SEQ)
        gateT = mix(GH, SEQ)
        hT_at = mix.at
        mix(KT, SEQ)
        hT0 = (rounded("h0_hi", hT_at, KT, SEQ), rounded("h0_lo", arena + 7680 + 4096, KT, SEQ))
        x = reg(hT_at, TT, D)
        assert arena == mix.at
        x0 = reg(base, TT, D)
        h0 = x0
        sq_junk0 = reg(arena + 2 * D, 1024)
        s5 = Space(arena, top)
        G = s5(S5_G, 15, S5_CH)
        WT = s5(S5_G, P)
        TM = s5(S5_G, P)
        E_re, E_im = s5(S5_GP, S5_C), s5(S5_GP, S5_C)
        R8 = s5(S5_GP, S5_C)
        H_re, H_im = s5(8, S5_COLS), s5(8, S5_COLS)
        B1, B2 = s5(S5_G, S5_CH), s5(S5_G, S5_CH)
        Cst = s5(S5_G, S5_CH)
        C_re, C_im = s5(S5_GP, S5_CH), s5(S5_GP, S5_CH)
        sm = {n: s5(S5_COLS) for n in (
            "dt ar th n r t t2 ab sn cs e e8 L_re L_im den rd f_re f_im L2_re L2_im L4_re L4_im u_re u_im w_re w_im").split()}
        Hs = s5(8, S5_G)
        t_pool2 = s5(S5_GP, S5_C // 2)
        logits = s5(TT, 2 * GH)
        late = Space(arena, arena + S5_G * 15 * S5_CH)
        V_re, V_im = late(S5_GP, 8, S5_CH), late(S5_GP, 8, S5_CH)
        z_re, z_im, t_a = late(S5_GP, S5_C), late(S5_GP, S5_C), late(S5_GP, S5_C)
        late2 = Space(hT_at, hT_at + KT * SEQ)
        t_b, t_c = late2(S5_GP, S5_C), late2(S5_GP, S5_C)
        U2 = late2(S5_G, S5_C)
        uP = catT[:, 4:8, :]
        yP = reg(arena + 7680 + 8192, 4, SEQ)
        hg = reg(arena + 7680 + 4096, 4, SEQ)
        sg = reg(arena + 7680 + 4096 + 2048, 4, SEQ)
        s5_bc = reg(arena + 7680 + 8192 + 3072 + 768, 2048)
        s5_top = -(-s5.at // 8) * 8
        w_ab_split = rounded("wab_split", s5_top, KT, 2, 2 * GH)
        w_ab = tensor_at("w_ab", s5_top + 128, F32, KT, 2 * GH)
        t_pool = Space(s5_top + 192, top)(2, 4, S5_COLS)
        C_pad = TM
        K8 = reg(arena + 7680 + 8192 + 3072 + 768, 4, 15 * S5_CH)
        yS = reg(arena + 7680, 8, S5_W)
        u_dram = nc.dram_tensor("u_dram", (S5_G, S5_CH, 8 * S5_C), F32, kind="Internal").ap()

        def ab_wait(eng, n):
            if n % 2 == 0:
                eng.wait_ge(sem("ab_mm"), n // 2 + 1)
            else:
                eng.wait_ge(panel_used, where[f"ab{n // 4}_{n % 4 // 2}"] + 1)

        def ab_groups_pe(pe, pi):
            for n in range(4 * pi, 4 * pi + 4):
                if n % 2 == 0:
                    w = take_split(pe, f"ab{pi}_{n % 4 // 2}", KT)
                if n < 8:
                    ready_T(pe, "n0", n)
                else:
                    pe.wait_ge(sem("conv"), n - 7)
                for k in range(KT):
                    if n == 0:
                        ready_T(pe, "n0", k)
                    ins = product(pe, ps[:, n % 8, :], of(w, k, slice(n % 2 * P, (n % 2 + 1) * P)), of(hT0, k), k == 0, k == KT - 1)
                if n % 2 == 0:
                    ins.then_inc(sem("ab_mm"), 1)
                else:
                    ins.then_inc(panel_used, 1)

        def ab_ahead(n):
            return "ab0_0", min(n // 2 + 2, AB_PIECES - 1)

        conv_y = catT[:, 0:2, :]

        def conv_dve(v, n):
            ab_wait(v, n)
            if n >= 2:
                v.wait_ge(sem("qkv_s"), n - 1)
            y = conv_y[:, n % 2, :]
            b = ps[:, n % 8, :]
            link(v, v.tensor_scalar(y, b, pcol("conv", 3 * 12 + n), None, ALU.mult), "dve_step")
            for s in (1, 2, 3):
                ins = v.scalar_tensor_tensor(y[:, s:SEQ], b[:, 0:SEQ - s], pcol("conv", (3 - s) * 12 + n),
                                             y[:, s:SEQ], ALU.mult, ALU.add)
                if s < 3:
                    link(v, ins, "dve_step")
                else:
                    ins.then_inc(sem("conv"), 1)

        def silu_act(a, n):
            a.wait_ge(sem("conv"), n + 1)
            a.activation(qkvT[:, n, :], conv_y[:, n % 2, :], ACT.Silu).then_inc(sem("qkv_s"), 1)

        def gate_act(a, n):
            ab_wait(a, n)
            a.activation(gateT[:, n - 12, :], ps[:, n % 8, :], ACT.Silu).then_inc(sem("gate_s"), 1)

        def u_act(a, n):
            ab_wait(a, n)
            a.activation(uP[:, n - 16, :].rearrange("p (l c) -> p c l", l=8),
                              ps[:, n % 8, :].rearrange("p (c l) -> p c l", l=8), ACT.Copy).then_inc(sem("u_s"), 1)

        def logits_pe(pe):
            pe.wait_ge(sem("gate_s"), 4)
            pe.wait_ge(sem("wab_lo"), 1)
            for i in range(TT):
                for k in range(KT):
                    for part in range(2):
                        ins = pe.matmul(ps[:, 7, i * 16:(i + 1) * 16], hT0[part][:, k, i * P:(i + 1) * P],
                                        w_ab_split[:, k, :, :].rearrange("p a b -> p (a b)"), start=(k == 0 and part == 0), stop=(k == KT - 1 and part == 1))
            ins.then_inc(sem("logit_mm"), 1)

        def cmul(eng, o_re, o_im, a_re, a_im, b_re, b_im, t1, t2, name):
            link(eng, eng.tensor_tensor(t1, a_re, b_re, ALU.mult), name)
            link(eng, eng.tensor_tensor(t2, a_im, b_im, ALU.mult), name)
            link(eng, eng.tensor_tensor(o_re, t1, t2, ALU.subtract), name)
            link(eng, eng.tensor_tensor(t1, a_re, b_im, ALU.mult), name)
            link(eng, eng.tensor_tensor(t2, a_im, b_re, ALU.mult), name)
            link(eng, eng.tensor_tensor(o_im, t1, t2, ALU.add), name)

        def s5_params_act(a):
            a.wait_ge(sem("par_in"), 16)
            a.activation(sm["dt"], pcols("log_dt"), ACT.Exp).then_inc(sem("s5_dt"), 1)
            a.wait_ge(sem("s5_arg"), 1)
            a.activation(sm["e"], sm["ar"], ACT.Exp).then_inc(sem("s5_fn"), 1)
            a.activation(sm["e8"], sm["ar"], ACT.Exp, scale=8.0).then_inc(sem("s5_fn"), 1)
            a.activation(sm["sn"], sm["r"], ACT.Sin).then_inc(sem("s5_fn"), 1)
            link(a, a.activation(sm["ab"], sm["r"], ACT.Abs), "act_step")
            a.activation(sm["cs"], sm["ab"], ACT.Sin, bias=pcol("half_pi"), scale=-1.0).then_inc(sem("s5_fn"), 1)

        def s5_params_pool(g):
            ch = "s5_pool"
            a_re, a_im = pcols("a_re"), pcols("a_im")
            g.wait_ge(sem("s5_dt"), 1)
            link(g, g.tensor_tensor(sm["ar"], a_re, sm["dt"], ALU.mult), ch)
            link(g, g.tensor_tensor(sm["th"], a_im, sm["dt"], ALU.mult), ch)
            link(g, g.tensor_scalar(sm["n"], sm["th"], 1.0 / TWO_PI, ROUND, ALU.mult, ALU.add), ch)
            link(g, g.tensor_scalar(sm["n"], sm["n"], ROUND, None, ALU.subtract), ch)
            src = sm["th"]
            for c in PI_PARTS:
                link(g, g.tensor_scalar(sm["t"], sm["n"], c, None, ALU.mult), ch)
                link(g, g.tensor_tensor(sm["r"], src, sm["t"], ALU.subtract), ch)
                src = sm["r"]
            link(g, g.tensor_scalar(sm["r"], sm["r"], 3.1415925, -3.1415925, ALU.min, ALU.max), "s5_arg")
            g.wait_ge(sem("s5_fn"), 4)
            link(g, g.tensor_tensor(sm["L_re"], sm["e"], sm["cs"], ALU.mult), ch)
            link(g, g.tensor_tensor(sm["L_im"], sm["e"], sm["sn"], ALU.mult), ch)
            link(g, g.tensor_tensor(sm["t"], a_re, a_re, ALU.mult), ch)
            link(g, g.tensor_tensor(sm["t2"], a_im, a_im, ALU.mult), ch)
            link(g, g.tensor_tensor(sm["den"], sm["t"], sm["t2"], ALU.add), "s5_den")
            link(g, g.tensor_scalar(sm["n"], sm["L_re"], 1.0, None, ALU.subtract), ch)
            link(g, g.tensor_tensor(sm["t"], sm["n"], a_re, ALU.mult), ch)
            link(g, g.tensor_tensor(sm["t2"], sm["L_im"], a_im, ALU.mult), ch)
            link(g, g.tensor_tensor(sm["f_re"], sm["t"], sm["t2"], ALU.add), ch)
            link(g, g.tensor_tensor(sm["t"], sm["L_im"], a_re, ALU.mult), ch)
            link(g, g.tensor_tensor(sm["t2"], sm["n"], a_im, ALU.mult), ch)
            link(g, g.tensor_tensor(sm["f_im"], sm["t"], sm["t2"], ALU.subtract), ch)
            g.wait_ge(sem("s5_rd"), 1)
            for h, f, l in ((H_re, "f_re", "L_re"), (H_im, "f_im", "L_im")):
                link(g, g.tensor_tensor(h[:, 7, 0:S5_G], sm[f][:, 0:S5_G], sm["rd"][:, 0:S5_G], ALU.mult), ch)
                link(g, g.tensor_copy(h[:, 7, S5_G:S5_COLS], sm[l][:, S5_G:S5_COLS]), ch)
            L = lambda n: (sm[n + "_re"], sm[n + "_im"])
            cmul(g, *L("L2"), *L("L"), *L("L"), sm["t"], sm["t2"], ch)
            cmul(g, *L("L4"), *L("L2"), *L("L2"), sm["t"], sm["t2"], ch)
            tmp = t_pool
            for lo, n, p in ((6, 1, "L"), (4, 2, "L2"), (0, 4, "L4")):
                l_re, l_im = L(p)
                cmul(g, H_re[:, lo:lo + n, :], H_im[:, lo:lo + n, :], H_re[:, lo + n:lo + 2 * n, :], H_im[:, lo + n:lo + 2 * n, :],
                     bc(l_re, 1, n), bc(l_im, 1, n), tmp[:, 0, 0:n, :], tmp[:, 1, 0:n, :], ch)
            link(g, g.tensor_copy(E_re[:, :, 1:2], sm["cs"][:, S5_G:S5_COLS].unsqueeze(2)), ch)
            g.wait_ge(sem("bc_in"), 16)
            for m in range(8):
                link(g, g.tensor_scalar(Hs[:, m, :], H_im[:, m, 0:S5_G], pcol("sgn"), None, ALU.mult), ch)
            link(g, g.tensor_scalar(Cst, Cst, pcol("nsgn"), None, ALU.mult), "s5_tables")

            u, w = (sm["u_re"][:, 0:S5_GP], sm["u_im"][:, 0:S5_GP]), (sm["w_re"][:, 0:S5_GP], sm["w_im"][:, 0:S5_GP])
            one = (sm["cs"][:, S5_G:S5_COLS], sm["sn"][:, S5_G:S5_COLS])
            tt1, tt2 = sm["t"][:, 0:S5_GP], sm["t2"][:, 0:S5_GP]
            cmul(g, *u, *one, *one, tt1, tt2, ch)
            cmul(g, *w, *u, *u, tt1, tt2, ch)
            cmul(g, *u, *w, *w, tt1, tt2, ch)
            link(g, g.memset(E_re[:, :, 0:1], 1.0), ch)
            link(g, g.memset(E_im[:, :, 0:1], 0.0), ch)
            n = 1
            while n < S5_C:
                cmul(g, E_re[:, :, n:2 * n], E_im[:, :, n:2 * n], E_re[:, :, 0:n], E_im[:, :, 0:n],
                     bc(u[0], 2, n), bc(u[1], 2, n), R8[:, :, 0:n], t_pool2[:, :, 0:n], ch)
                n *= 2
                if n < S5_C:
                    cmul(g, *w, *u, *u, tt1, tt2, ch)
                    u, w = w, u
            link(g, g.memset(R8, 0.0), ch)
            link(g, g.tensor_tensor(R8[:, :, 1:S5_C], R8[:, :, 1:S5_C], bc(sm["e8"][:, S5_G:S5_COLS], 2, S5_C - 1), ALU.add), "s5_turn")

            g.wait_ge(sem("s5_copied"), 10)
            cr, ci, vr, vi = s5_v_operands()
            t1 = reg(base, S5_GP, 8, S5_CH)
            link(g, g.tensor_tensor(V_im, cr, vi, ALU.mult), ch)
            link(g, g.tensor_tensor(t1, ci, vr, ALU.mult), ch)
            link(g, g.tensor_tensor(V_im, V_im, t1, ALU.add), "s5_v")

        def s5_v_operands():
            vr = H_re[:, :, S5_G:S5_COLS].rearrange("p i g -> p g i")
            vi = H_im[:, :, S5_G:S5_COLS].rearrange("p i g -> p g i")
            return bc(C_re, 2, 8), bc(C_im, 2, 8), bc(vr, 3, S5_CH), bc(vi, 3, S5_CH)

        def s5_v_dve(v):
            v.wait_ge(sem("s5_tables"), 1)
            v.wait_ge(sem("s5_copied"), 10)
            cr, ci, vr, vi = s5_v_operands()
            t1 = reg(arena + 4096, S5_GP, 8, S5_CH)
            link(v, v.tensor_tensor(V_re, cr, vr, ALU.mult), "dve_step")
            link(v, v.tensor_tensor(t1, ci, vi, ALU.mult), "dve_step")
            v.tensor_tensor(V_re, V_re, t1, ALU.subtract).then_inc(sem("s5_vre"), 1)

        def s5_pad_dve(v):
            v.wait_ge(sem("logit_mm"), 1)
            link(v, v.memset(C_pad, 0.0), "dve_step")
            c8 = Cst.rearrange("p (o r) c -> p o r c", o=4)
            pad = C_pad.rearrange("p (o r) n -> p o r n", o=4)
            for r in range(8):
                v.tensor_copy(pad[:, :, r, r * S5_CH:(r + 1) * S5_CH], c8[:, :, r, :]).then_inc(sem("s5_pad"), 1)

        def s5_rd_dve(v):
            v.wait_ge(sem("s5_den"), 1)
            v.reciprocal(sm["rd"], sm["den"]).then_inc(sem("s5_rd"), 1)

        def s5_g_dve(v, n):
            if n == 0:
                v.wait_ge(sem("s5_tables"), 1)
            else:
                v.wait_ge(sem("s5_g"), n)
            gs = slice(8 * n, 8 * n + 8)
            o = G[:, gs, 0:8, :]
            hr = bc(H_re[:, :, gs].rearrange("p m g -> p g m"), 3, S5_CH)
            hi = bc(Hs[:, :, gs].rearrange("p m g -> p g m"), 3, S5_CH)
            t = reg(base + 1024, 8, 8, S5_CH)
            v.tensor_tensor(o, hr, bc(B1[:, gs, :], 2, 8), ALU.mult)
            link(v, v.tensor_tensor(t, hi, bc(B2[:, gs, :], 2, 8), ALU.mult), "dve_step")
            v.tensor_tensor(o, o, t, ALU.add).then_inc(sem("s5_g"), 1)
            if n == 3:
                v.memset(G[:, :, 8:15, :], 0.0).then_inc(sem("s5_g"), 1)

        def s5_tables_pe(pe):
            pe.wait_ge(sem("s5_g"), 5)
            for s in range(10):
                if s == 0:
                    pe.wait_ge(sem("gate_s"), 4)
                if s >= 3:
                    pe.wait_ge(sem("s5_copied"), s - 2)
                bank = ps[:, 4 + s % 3, :]
                if s < 8:
                    for q in range(4):
                        ins = pe.transpose(bank[:, q * P:(q + 1) * P], G[:, 4 * s + q, 0:8, :].rearrange("p m c -> p (m c)"), ident)
                else:
                    pe.wait_ge(sem("s5_pad"), after("s5_pad", 8))
                    for o in range(2):
                        for r in range(8):
                            g = 8 * (2 * (s - 8) + o) + r
                            ins = pe.matmul(bank[:, o * 240:(o + 1) * 240], C_pad[:, g, :], G[:, g, :, :].rearrange("p m c -> p (m c)"),
                                            start=(r == 0), stop=(r == 7))
                ins.then_inc(sem("s5_tab"), 1)

        def s5_tables_act(a):
            for s in range(10):
                a.wait_ge(sem("s5_tab"), s + 1)
                if s < 8:
                    a.activation(WT[:, 4 * s:4 * s + 4, :].rearrange("p g n -> p (g n)"), ps[:, 4 + s % 3, :], ACT.Copy).then_inc(sem("s5_copied"), 1)
                else:
                    a.activation(K8[:, 2 * (s - 8):2 * (s - 8) + 2, :].rearrange("p o n -> p (o n)"), ps[:, 4 + s % 3, 0:480],
                                 ACT.Copy).then_inc(sem("s5_copied"), 1)

        def s5_tm_pe(pe):
            pe.wait_ge(sem("u_s"), 4)
            pe.wait_ge(sem("s5_copied"), 10)
            for s in range(8):
                if s >= 4:
                    pe.wait_ge(sem("s5_copied"), 10 + s - 3)
                for q in range(4):
                    i = 4 * (s % 2) + q
                    ins = pe.transpose(ps[:, s % 4, q * P:(q + 1) * P], K8[:, s // 2, i * S5_CH:i * S5_CH + P], ident)
                ins.then_inc(sem("s5_tab"), 1)

        def s5_tm_act(a):
            for s in range(8):
                o, ih = s // 2, s % 2
                a.wait_ge(sem("s5_tab"), 10 + s + 1)
                a.activation(TM[:, 8 * o:8 * o + 8, ih * 64:(ih + 1) * 64].rearrange("p r (i c) -> p i r c", i=4),
                             ps[:, s % 4, :].rearrange("p (i r c) -> p i r c", i=4, r=8), ACT.Copy).then_inc(sem("s5_copied"), 1)

        def s5_u_sp(sp):
            sp.wait_ge(sem("u_s"), 4)
            sp.dma_start(u_dram.rearrange("(f g) c n -> (g c) f n", f=4), uP).then_inc(sem("u_out"), 16)
            sp.wait_ge(sem("u_out"), 16)
            sp.wait_ge(panel_used, where["ab4_1"] + 1)
            sp.wait_ge(sem("logit_mm"), 1)
            for l in range(8):
                sp.dma_start(U2[l * S5_CH:(l + 1) * S5_CH, :, :],
                             u_dram[:, :, l * S5_C:(l + 1) * S5_C].rearrange("g c n -> c g n")).then_inc(sem("u_in"), 16)

        def s5_states_pe(pe):
            pe.wait_ge(sem("s5_copied"), 10)
            pe.wait_ge(sem("gcum"), 1)
            pe.wait_ge(sem("decays"), 3)
            pe.wait_ge(sem("u_in"), 16 * 8)
            for ri in range(2):
                for g in range(S5_G):
                    gp, g2 = g // 2, g % 2
                    ins = pe.matmul(ps[g2 * 64:g2 * 64 + 64, 4 + 2 * ri + gp // 8, (gp % 8) * S5_C:(gp % 8 + 1) * S5_C],
                                    WT[:, g, ri * 64:ri * 64 + 64], U2[:, g, :], start=True, stop=True)
                ins.then_inc(sem("s5_x"), 1)

        def s5_states_dve(v):
            X_re = ps[:, 4:6, :].rearrange("p b (g c) -> p (b g) c", c=S5_C)
            X_im = ps[:, 6:8, :].rearrange("p b (g c) -> p (b g) c", c=S5_C)
            ch = "dve_step"
            flat = lambda a: a.rearrange("p g c -> p (g c)")
            v.wait_ge(sem("s5_turn"), 1)
            v.wait_ge(sem("s5_vre"), 1)
            v.wait_ge(sem("s5_x"), 2)
            link(v, v.tensor_tensor(t_a, X_re, E_re, ALU.mult), ch)
            link(v, v.tensor_tensor(t_b, X_im, E_im, ALU.mult), ch)
            link(v, v.tensor_tensor(t_a, t_a, t_b, ALU.add), ch)
            link(v, v.tensor_tensor_scan(flat(z_re), flat(R8), flat(t_a), 0.0, ALU.mult, ALU.add), ch)
            link(v, v.tensor_tensor(t_c, X_im, E_re, ALU.mult), ch)
            link(v, v.tensor_tensor(t_b, X_re, E_im, ALU.mult), "s5_xread")
            link(v, v.tensor_tensor(t_c, t_c, t_b, ALU.subtract), ch)
            link(v, v.tensor_tensor_scan(flat(z_im), flat(R8), flat(t_c), 0.0, ALU.mult, ALU.add), ch)
            n = S5_C - 1
            link(v, v.tensor_tensor(t_a, z_re, E_re, ALU.mult), ch)
            link(v, v.tensor_tensor(t_b, z_im, E_im, ALU.mult), ch)
            link(v, v.tensor_tensor(t_c[:, :, 1:], t_a[:, :, 0:n], t_b[:, :, 0:n], ALU.subtract), ch)
            link(v, v.memset(t_c[:, :, 0:1], 0.0), ch)
            link(v, v.tensor_tensor(t_a, z_re, E_im, ALU.mult), ch)
            link(v, v.tensor_tensor(t_b, z_im, E_re, ALU.mult), ch)
            link(v, v.scalar_tensor_tensor(z_re[:, :, 1:], t_a[:, :, 0:n], -1.0, t_b[:, :, 0:n], ALU.mult, ALU.subtract), ch)
            v.memset(z_re[:, :, 0:1], 0.0).then_inc(sem("s5_carry"), 1)

        def s5_out_pe(pe):
            def place(n):
                gp, g2 = n % S5_GP, n // S5_GP
                return gp, g2, ps[0:S5_C, 4 * g2 + gp // 4, (gp % 4) * P:(gp % 4 + 1) * P]
            pe.wait_ge(sem("s5_copied"), 10 + 8)
            for n in range(S5_G):
                gp, g2, o = place(n)
                if n == S5_GP:
                    pe.wait_ge(sem("s5_xread"), 1)
                pe.matmul(o, U2[:, 2 * gp + g2, :], TM[:, 2 * gp + g2, :], start=(gp % 4 == 0), stop=False, skip_group_check=True)
            pe.wait_ge(sem("s5_carry"), 1)
            pe.wait_ge(sem("s5_v"), 1)
            for n in range(S5_G):
                gp, g2, o = place(n)
                r = slice(g2 * 64, g2 * 64 + 64)
                pe.matmul(o, t_c[r, gp, :], V_re[r, gp, :, :].rearrange("p i c -> p (i c)"), start=False, stop=False, skip_group_check=True)
                ins = pe.matmul(o, z_re[r, gp, :], V_im[r, gp, :, :].rearrange("p i c -> p (i c)"), start=False, stop=True, skip_group_check=True)
                if gp % 4 == 3:
                    ins.then_inc(sem("s5_y"), 1)

        def s5_y_evac(eng, b):
            dst = yS[0:S5_C].rearrange("p i (g two c) -> p i g two c", two=2, c=S5_CH)[:, :, 4 * (b % 4):4 * (b % 4) + 4, b // 4, :]
            return dst, ps[0:S5_C, b, :].rearrange("p (g i c) -> p i g c", g=4, i=8)

        def s5_out_act(a):
            for b in range(0, 8, 2):
                a.wait_ge(sem("s5_y"), b + 1)
                a.activation(*s5_y_evac(a, b), ACT.Copy).then_inc(sem("y_a"), 1)

        def s5_out_dve(v):
            for b in range(1, 8, 2):
                v.wait_ge(sem("s5_y"), b + 1)
                v.tensor_copy(*s5_y_evac(v, b)).then_inc(sem("y_v"), 1)

        def s5_back_pe(pe):
            for f in range(4):
                pe.wait_ge(sem(("y_a", "y_v")[f % 2]), after(("y_a", "y_v")[f % 2], 3 + f // 2))
                for i in range(8):
                    ins = pe.transpose(ps[:, f, (7 - i) * S5_C:(8 - i) * S5_C], yS[0:S5_C, i, f * P:(f + 1) * P], ident[0:S5_C, 0:S5_C])
                ins.then_inc(sem("s5_yt"), 1)

        def s5_glu_dve(v):
            for f in range(4):
                v.wait_ge(sem("s5_yt"), f + 1)
                v.scalar_tensor_tensor(yP[:, f, :], uP[:, f, :], pcol("s5_d", f), ps[:, f, :], ALU.mult, ALU.add).then_inc(sem("y_d"), 1)

        def s5_gated_dve(v):
            for f in range(4):
                v.wait_ge(sem("glu_s"), f + 1)
                v.tensor_tensor(catT[:, f, :].rearrange("p (c l) -> p l c", l=8),
                                     sg[:, f, :].rearrange("p (l c) -> p l c", l=8),
                                     hg[:, f, :].rearrange("p (l c) -> p l c", l=8), ALU.mult)

        def s5_glu_act(a):
            for f in range(4):
                a.wait_ge(sem("y_d"), f + 1)
                a.activation(hg[:, f, :], yP[:, f, :], ACT.Gelu_apprx_tanh).then_inc(sem("gelu_s"), 1)

        def s5_gated_act(a):
            for f in range(4):
                if f < 3:
                    a.wait_ge(sem("glu_mm"), f + 1)
                else:
                    a.wait_ge(panel_used, where["glu"] + 1)
                a.activation(sg[:, f, :], ps[:, 4 + f, :], ACT.Sigmoid, bias=pcol("b_glu", f)).then_inc(sem("glu_s"), 1)

        def s5_glu_pe(pe):
            w = full(take(pe, "glu"), 4)
            for f in range(4):
                for k in range(4):
                    if f == 0:
                        pe.wait_ge(sem("gelu_s"), k + 1)
                    ins = pe.matmul(ps[:, 4 + f, :], w[:, k, f * P:(f + 1) * P], hg[:, k, :], start=(k == 0), stop=(k == 3))
                if f < 3:
                    ins.then_inc(sem("glu_mm"), 1)
                else:
                    ins.then_inc(panel_used, 1)

        gd = Space(hT_at, top)
        q_n, k_n, k_b, q_g = gd(GH, GD), gd(GH, GD), gd(GH, GD), gd(GH, GD)
        q_nT, k_nT, k_bT = gd(GH, P), gd(GH, P), gd(GH, P)
        dec_m = gd(GH, P)
        k_bg, v_b, k_t = gd(TT, GH, GD), gd(TT, GH, GD), gd(TT, GH, GD)
        q_gT = gd(TT, GH, P)
        A_T, QK_T = gd(TT, GH, P), gd(TT, GH, P)
        U_m, T_m, Y_m, A_l = gd(TT, GH, P), gd(TT, GH, P), gd(TT, GH, P), gd(TT, GH, P)
        g_bc = gd(GH, P)
        state = gd(GH, GD)
        w_c = gd(2, GH * GD)
        small_at = [0]

        def small(*shape):
            n = 1
            for c in shape:
                n *= c
            v = memT.rearrange("p k n -> p (k n)")[:, small_at[0]:small_at[0] + n]
            small_at[0] += n
            return v.rearrange("p (a b) -> p a b", a=shape[0]) if len(shape) == 2 else v

        gs = {n: small(TT, GH) for n in "z az e1 l1 sp g eb beta gc tail gamma ss_o r_o".split()}
        ea = small(GH)
        dec = small(2, TT * GH)
        ssq = gd(2, GH)
        rq = gd(2, GH)
        co = {n: gd(GH) for n in "q qg k kb kbg kt".split()}
        lg = small(TT, 2 * GH)
        qkv0 = base + KT * SEQ
        u_n, wk_T, o_t = reg(qkv0, TT, GH, GD), reg(qkv0 + 2048, TT, GH, P), reg(qkv0 + 4096, TT, GH, GD)
        flat3 = lambda a: a.rearrange("p a b -> p (a b)")

        def logits_dve(v):
            v.wait_ge(sem("logit_mm"), 1)
            b = ps[:, 7, 0:TT * 16].rearrange("p (i a n) -> p i a n", i=TT, a=2)
            link(v, v.tensor_copy(logits, b[:, :, 0, :]), "dve_step")
            v.tensor_tensor(logits, logits, b[:, :, 1, :], ALU.add).then_inc(sem("logit"), 1)

        def gates_dve(v):
            ch = "dve_step"
            link(v, v.tensor_copy(lg, logits), ch)
            link(v, v.tensor_tensor(gs["z"], lg[:, :, 0:GH], bc(pcols("dt_bias"), 1, TT), ALU.add), ch)
            link(v, v.tensor_scalar(gs["az"], gs["z"], -1.0, None, ALU.mult), ch)
            link(v, v.tensor_tensor(gs["az"], gs["az"], gs["z"], ALU.max), "gate_in")
            v.wait_ge(sem("gate_fn"), 3)
            link(v, v.scalar_tensor_tensor(gs["sp"], gs["z"], 0.0, gs["l1"], ALU.max, ALU.add), ch)
            link(v, v.tensor_tensor(gs["sp"], gs["sp"], bc(ea, 1, TT), ALU.mult), ch)
            link(v, v.tensor_scalar(gs["g"], gs["sp"], -1.0, None, ALU.mult), "g_ready")
            link(v, v.tensor_scalar(gs["eb"], gs["eb"], 1.0, None, ALU.add), ch)
            link(v, v.reciprocal(gs["beta"], gs["eb"]), ch)

        def gates_sums_dve(v):
            ch = "dve_step"
            v.wait_ge(sem("gcum_mm"), 1)
            link(v, v.tensor_copy(gs["gc"].rearrange("p a b -> p (a b)"), ps[:, 7, 0:16]), ch)
            link(v, v.tensor_tensor(gs["tail"].rearrange("p a b -> p (a b)"), ps[:, 7, 16:32],
                                    gs["gc"].rearrange("p a b -> p (a b)"), ALU.subtract), "gcum")

        def gates_act(a):
            a.wait_ge(sem("gate_in"), 1)
            link(a, a.activation(gs["e1"], gs["az"], ACT.Exp, scale=-1.0), "act_step")
            a.activation(gs["l1"], gs["e1"], ACT.Ln, bias=pcol("one")).then_inc(sem("gate_fn"), 1)
            a.activation(gs["eb"], lg[:, :, GH:2 * GH], ACT.Exp, scale=-1.0).then_inc(sem("gate_fn"), 1)
            a.activation(ea, pcols("a_log"), ACT.Exp).then_inc(sem("gate_fn"), 1)

        def gates_decays_act(a):
            a.wait_ge(sem("gcum"), 1)
            a.activation(gs["gamma"], gs["gc"], ACT.Exp).then_inc(sem("decays"), 1)
            a.activation(gs["tail"], gs["tail"], ACT.Exp).then_inc(sem("decays"), 1)
            a.activation(dec.rearrange("p a b -> p (a b)"), ps[:, 7, 32:64], ACT.Exp).then_inc(sem("decays"), 1)

        def gates_pe(pe):
            pe.wait_ge(sem("g_ready"), 1)
            g = gs["g"].rearrange("p a b -> p (a b)")
            for n, m in enumerate(("inc", "same", "first", "second")):
                ins = pe.matmul(ps[:, 7, 16 * n:16 * n + 16], ccol(m), g, start=True, stop=True)
            ins.then_inc(sem("gcum_mm"), 1)

        def gdn_turn_pe(pe, i):
            if i == 0:
                pe.wait_ge(sem("qkv_s"), 12)
                pe.wait_ge(sem("y_d"), 4)
            else:
                pe.wait_ge(sem("g_tok"), 6 * i)
                pe.wait_ge(sem("g_v"), after("g_v", 4 * i))
            for n in range(3):
                for h in range(GH):
                    ins = pe.transpose(ps[:, n, h * P:(h + 1) * P], qkvT[:, n * GH + h, i * P:(i + 1) * P], ident)
                ins.then_inc(sem("g_tr"), 1)

        def gdn_back_pe(pe, i):
            pe.wait_ge(sem("g_tok"), 6 * i + 4)
            if i == 0:
                pe.wait_ge(sem("glu_s"), 4)
            else:
                pe.wait_ge(sem("g_at"), 2 * i)
            for n, src in enumerate((q_n, k_n, k_b, q_g)):
                for h in range(GH):
                    ins = pe.transpose(ps[:, 3 + n, h * P:(h + 1) * P], src[:, h, :], ident)
                ins.then_inc(sem("g_back"), 1)

        def gdn_prod_pe(pe, i):
            pe.wait_ge(sem("g_ft"), 4 * i + 4)
            if i == 0:
                pe.wait_ge(sem("decays"), 3)
            for bank, l, r in ((7, k_nT, k_bT), (3, k_nT, q_nT)):
                for h in range(GH):
                    ins = pe.matmul(ps[:, bank, h * P:(h + 1) * P], l[:, h, :], r[:, h, :], start=True, stop=True)
                ins.then_inc(sem("g_prod"), 1)
            pe.wait_ge(sem("g_bc"), i + 1)
            for h in range(GH):
                ins = pe.matmul(ps[:, 4, h * P:(h + 1) * P], g_bc[:, h, :], ccol("inc"), start=True, stop=True)
            ins.then_inc(sem("g_row"), 1)

        def gdn_tok_act(a, i):
            for n in range(2):
                a.wait_ge(sem("g_tr"), 3 * i + n + 1)
                if i > 0:
                    a.wait_ge(sem("g_ss"), 2 * i - 1 + n)
                a.activation(A_l[:, n, :, :].rearrange("p a b -> p (a b)"), ps[:, n, :], ACT.Square).then_inc(sem("g_sq"), 1)
            a.wait_ge(sem("g_ss"), 2 * i + 2)
            a.activation(rq, ssq, ACT.Sqrt, bias=pcol("eps")).then_inc(sem("g_rt"), 1)
            a.wait_ge(sem("g_tr"), 3 * i + 3)
            for h in range(GH):
                a.activation(v_b[:, i, h, :], ps[:, 2, h * P:(h + 1) * P], ACT.Copy, scale=gs["beta"][:, i, h:h + 1]).then_inc(sem("g_v"), 1)
            if i > 0:
                a.wait_ge(sem("g_row"), i)
            a.activation(g_bc, bc(gs["g"][:, i, :], 2, P), ACT.Copy).then_inc(sem("g_bc"), 1)

        def gdn_back_act(a, i):
            if i > 0:
                a.wait_ge(sem("g_row"), i)
            for n, dst in enumerate((q_nT, k_nT, k_bT, q_gT[:, i, :, :])):
                a.wait_ge(sem("g_back"), 4 * i + n + 1)
                a.activation(dst, ps[:, 3 + n, :].rearrange("p (a b) -> p a b", a=GH), ACT.Copy).then_inc(sem("g_ft"), 1)

        def gdn_dec_act(a, i):
            a.wait_ge(sem("g_diff"), 4 * i + 4)
            a.activation(dec_m, dec_m, ACT.Exp).then_inc(sem("g_dec"), 1)

        def gdn_tok_dve(v, i):
            for n in range(2):
                v.wait_ge(sem("g_sq"), 2 * i + n + 1)
                link(v, v.tensor_reduce(ssq[:, n, :], A_l[:, n, :, :], AX, ALU.add), "g_ss")
            if i == 0:
                v.wait_ge(sem("decays"), 3)
            v.wait_ge(sem("g_rt"), i + 1)
            ch = "dve_step"
            link(v, v.reciprocal(rq, rq), ch)
            link(v, v.tensor_scalar(co["q"], rq[:, 0, :], GD ** -0.5, None, ALU.mult), ch)
            link(v, v.tensor_tensor(co["qg"], co["q"], gs["gamma"][:, i, :], ALU.mult), ch)
            link(v, v.tensor_tensor(co["kb"], rq[:, 1, :], gs["beta"][:, i, :], ALU.mult), ch)
            link(v, v.tensor_tensor(co["kbg"], co["kb"], gs["gamma"][:, i, :], ALU.mult), ch)
            link(v, v.tensor_tensor(co["kt"], rq[:, 1, :], gs["tail"][:, i, :], ALU.mult), ch)
            if i > 0:
                v.wait_ge(sem("g_back"), 4 * i)
                v.wait_ge(sem("g_row"), i)
            v.wait_ge(sem("g_tr"), 3 * i + 2)
            if i > 0:
                gdn_diff_dve(v, i - 1)
            for dst, bank, c in ((q_n, 0, co["q"]), (k_n, 1, rq[:, 1, :]), (k_b, 1, co["kb"]), (q_g, 0, co["qg"]),
                                 (k_bg[:, i], 1, co["kbg"]), (k_t[:, i], 1, co["kt"])):
                v.tensor_tensor(dst, ps[:, bank, :].rearrange("p (a b) -> p a b", a=GH), bc(c, 2, GD), ALU.mult).then_inc(sem("g_tok"), 1)

        def gdn_diff_dve(v, i):
            v.wait_ge(sem("g_row"), i + 1)
            for h in range(GH):
                v.scalar_tensor_tensor(dec_m[:, h, :], ps[:, 4, h * P:(h + 1) * P], gs["gc"][:, i, h:h + 1],
                                            ccol("neg"), ALU.subtract, ALU.add).then_inc(sem("g_diff"), 1)

        def gdn_prod_dve(v, i):
            if i == TT - 1:
                gdn_diff_dve(v, i)
            v.wait_ge(sem("g_dec"), i + 1)
            for dst, bank in ((A_T, 7), (QK_T, 3)):
                v.tensor_tensor(dst[:, i], ps[:, bank, :].rearrange("p (a b) -> p a b", a=GH), dec_m, ALU.mult).then_inc(sem("g_at"), 1)

        LEVELS = 5

        def solve_start_pool(g):
            for i in range(TT):
                g.wait_ge(sem("g_at"), 2 * i + 1)
                link(g, g.tensor_tensor(U_m[:, i], A_T[:, i], bc(ccol("m1"), 1, GH), ALU.mult), "s5_pool")
                g.tensor_tensor(U_m[:, i], bc(ident, 1, GH), U_m[:, i], ALU.subtract).then_inc(sem("g_u"), 1)

        def solve_masks_pool(g):
            for l in range(LEVELS):
                for i in range(TT):
                    if l == 0:
                        g.wait_ge(sem("g_u"), TT)
                    else:
                        g.wait_ge(sem("sv_y"), (l - 1) * TT + i + 1)
                    g.tensor_tensor(A_l[:, i], A_T[:, i], bc(ccol(f"m{l + 2}"), 1, GH), ALU.mult).then_inc(sem("sv_mask"), 1)

        def solve_pe(pe):
            pe.wait_ge(sem("g_at"), 2 * TT)
            for i in range(TT):
                pe.wait_ge(sem("g_u"), TT)
                if i >= 2:
                    pe.wait_ge(sem("sv_t0"), i - 1)
                for h in range(GH):
                    ins = pe.transpose(ps[:, i % 2, h * P:(h + 1) * P], U_m[:, i, h, :], ident)
                ins.then_inc(sem("sv_tr"), 1)
            for l in range(LEVELS):
                for i in range(TT):
                    n = l * TT + i
                    pe.wait_ge(sem("sv_mask"), n + 1)
                    if l == 0:
                        pe.wait_ge(sem("sv_t0"), min(i + 3, TT))
                    else:
                        pe.wait_ge(sem("sv_t"), n - TT + 1)
                    if n >= 2:
                        pe.wait_ge(sem("sv_yc"), n - 1)
                    for h in range(GH):
                        ins = pe.matmul(ps[:, n % 2, h * P:(h + 1) * P], A_l[:, i, h, :], T_m[:, i, h, :], start=True, stop=True)
                    ins.then_inc(sem("sv_y"), 1)
                for i in range(TT):
                    n = l * TT + i
                    pe.wait_ge(sem("sv_yc"), n + 1)
                    if l > 0:
                        pe.wait_ge(sem("sv_u"), n - TT + 1)
                    if n >= 3:
                        pe.wait_ge(sem("sv_u"), n - 2)
                    for h in range(GH):
                        ins = pe.matmul(ps[:, 2 + n % 3, h * P:(h + 1) * P], Y_m[:, i, h, :], U_m[:, i, h, :], start=True, stop=True)
                    if l < LEVELS - 1:
                        if n >= 3:
                            pe.wait_ge(sem("sv_t"), n - 2)
                        for h in range(GH):
                            ins = pe.matmul(ps[:, 5 + n % 3, h * P:(h + 1) * P], U_m[:, i, h, :], Y_m[:, i, h, :], start=True, stop=True)
                    ins.then_inc(sem("sv_d"), 1)

        def solve_act(a):
            for i in range(TT):
                a.wait_ge(sem("sv_tr"), i + 1)
                a.activation(flat3(T_m[:, i]), ps[:, i % 2, :], ACT.Copy).then_inc(sem("sv_t0"), 1)
            for n in range(LEVELS * TT):
                a.wait_ge(sem("sv_y"), n + 1)
                if n >= TT:
                    a.wait_ge(sem("sv_d"), n - TT + 1)
                a.activation(flat3(Y_m[:, n % TT]), ps[:, n % 2, :], ACT.Copy).then_inc(sem("sv_yc"), 1)

        def solve_dve(v):
            for n in range(LEVELS * TT):
                i = n % TT
                v.wait_ge(sem("sv_d"), n + 1)
                if n >= TT:
                    v.wait_ge(sem("sv_u"), n - TT + 1)
                v.tensor_tensor(flat3(U_m[:, i]), flat3(U_m[:, i]), ps[:, 2 + n % 3, :], ALU.subtract).then_inc(sem("sv_u"), 1)
                if n < (LEVELS - 1) * TT:
                    v.tensor_tensor(flat3(T_m[:, i]), flat3(T_m[:, i]), ps[:, 5 + n % 3, :], ALU.subtract).then_inc(sem("sv_t"), 1)

        def uw_pe(pe):
            pe.wait_ge(sem("sv_u"), LEVELS * TT)
            pe.wait_ge(sem("g_v"), after("g_v", 4 * TT))
            for i in range(TT):
                for h in range(GH):
                    ins = pe.matmul(ps[:, 2 * i, h * P:(h + 1) * P], U_m[:, i, h, :], v_b[:, i, h, :], start=True, stop=True)
                ins.then_inc(sem("uw"), 1)
                for h in range(GH):
                    ins = pe.matmul(ps[:, 2 * i + 1, h * P:(h + 1) * P], k_bg[:, i, h, :], U_m[:, i, h, :], start=True, stop=True)
                ins.then_inc(sem("uw"), 1)

        def uw_act(a):
            for i in range(TT):
                a.wait_ge(sem("uw"), 2 * i + 1)
                a.activation(flat3(u_n[:, i]), ps[:, 2 * i, :], ACT.Copy).then_inc(sem("u_c"), 1)

        def uw_dve(v):
            v.memset(state, 0.0).then_inc(sem("s_new"), 1)
            for i in range(TT):
                v.wait_ge(sem("uw"), 2 * i + 2)
                v.tensor_copy(flat3(wk_T[:, i]), ps[:, 2 * i + 1, :]).then_inc(sem("wk_c"), 1)

        def rec_pe(pe):
            for c in range(NCH):
                i, r = c // 2, slice(64 * (c % 2), 64 * (c % 2) + 64)
                pe.wait_ge(sem("s_new"), 1 + GH * c)
                if c == 0:
                    pe.wait_ge(sem("u_c"), TT)
                    pe.wait_ge(sem("wk_c"), TT)
                for h in range(GH):
                    ins = pe.matmul(ps[r, c % 2, h * P:(h + 1) * P], wk_T[:, i, h, r], state[:, h, :], start=True, stop=True)
                ins.then_inc(sem("r_ws"), 1)
                if c >= 2:
                    pe.wait_ge(sem("r_o"), c - 1)
                for h in range(GH):
                    pe.matmul(ps[r, 2 + c % 2, h * P:(h + 1) * P], q_gT[:, i, h, r], state[:, h, :], start=(h == 0), stop=False,
                              skip_group_check=True)
                pe.wait_ge(sem("r_w"), c + 1)
                for h in range(GH):
                    ins = pe.matmul(ps[:, 4 + c % 2, h * P:(h + 1) * P], k_t[r, i, h, :], w_c[r, c % 2, h * P:(h + 1) * P], start=True, stop=True)
                ins.then_inc(sem("r_kw"), 1)
                for h in range(GH):
                    ins = pe.matmul(ps[r, 2 + c % 2, h * P:(h + 1) * P], QK_T[r, i, h, r], w_c[r, c % 2, h * P:(h + 1) * P],
                                    start=False, stop=True, skip_group_check=True)
                ins.then_inc(sem("r_om"), 1)

        def rec_dve(v):
            for c in range(NCH):
                i, r = c // 2, slice(64 * (c % 2), 64 * (c % 2) + 64)
                v.wait_ge(sem("r_ws"), c + 1)
                if c == 0:
                    v.wait_ge(sem("u_c"), TT)
                if c >= 2:
                    v.wait_ge(sem("r_om"), c - 1)
                v.tensor_tensor(w_c[r, c % 2, :], flat3(u_n[r, i]), ps[r, c % 2, :], ALU.subtract).then_inc(sem("r_w"), 1)
                v.wait_ge(sem("r_kw"), c + 1)
                v.wait_ge(sem("s_new"), 1 + GH * c)
                for h in range(GH):
                    v.scalar_tensor_tensor(state[:, h, :], state[:, h, :], dec[:, c % 2, i * GH + h:i * GH + h + 1],
                                                ps[:, 4 + c % 2, h * P:(h + 1) * P], ALU.mult, ALU.add).then_inc(sem("s_new"), 1)
                if c % 2 == 1 and c >= 3:
                    gout_sums(v, (c - 3) // 2)

        def rec_act(a):
            for c in range(NCH):
                i, r = c // 2, slice(64 * (c % 2), 64 * (c % 2) + 64)
                a.wait_ge(sem("r_om"), c + 1)
                a.activation(flat3(o_t[r, i]), ps[r, 2 + c % 2, :], ACT.Copy).then_inc(sem("r_o"), 1)
                if c % 2 == 1:
                    a.wait_ge(sem("r_o"), c + 1)
                    a.activation(A_l[:, i], o_t[:, i], ACT.Square).then_inc(sem("go_sq"), 1)

        def gout_act(a):
            sqrt_table(a)
            a.wait_ge(sem("go_ss"), 4)
            a.activation(gs["r_o"], gs["ss_o"], ACT.Sqrt, bias=pcol("eps"), scale=1.0 / GD).then_inc(sem("go_rt"), 1)

        def gout_sums(v, i):
            v.wait_ge(sem("go_sq"), i + 1)
            v.tensor_reduce(gs["ss_o"][:, i, :], A_l[:, i], AX, ALU.add).then_inc(sem("go_ss"), 1)

        def gout_dve(v):
            gout_sums(v, TT - 1)
            v.wait_ge(sem("go_rt"), 1)
            link(v, v.reciprocal(gs["r_o"], gs["r_o"]), "dve_step")
            for i in range(TT):
                v.tensor_tensor(o_t[:, i], o_t[:, i], bc(gs["r_o"][:, i, :], 2, GD), ALU.mult).then_inc(sem("go_n"), 1)
            for h in range(GH):
                v.wait_ge(sem("go_tr"), h + 1)
                v.scalar_tensor_tensor(cat_f[:, h, :], ps[:, 4 + h, :], pcol("gdn_g"), gateT[:, h, :], ALU.mult, ALU.mult).then_inc(sem("gdn_done"), 1)
                if h > 0:
                    gout_lo(v, h - 1)
            gout_lo(v, GH - 1)

        cat = (rounded("s5_hi", arena + 8192, 4, SEQ), rounded("s5_lo", arena + 2048, 4, SEQ),
               rounded("gdn_hi", arena + 16384, 4, SEQ), rounded("gdn_lo", base + 2048, 4, SEQ))
        cat_f = reg(arena + 18432, GH, SEQ)

        def gout_hi_act(a):
            for h in range(GH):
                a.wait_ge(sem("gdn_done"), h + 1)
                a.activation(cat[2][:, h, :], cat_f[:, h, :], ACT.Copy).then_inc(sem("cat_hi"), 1)

        def gout_lo(v, h):
            v.wait_ge(sem("cat_hi"), after("cat_hi", h + 1))
            v.tensor_tensor(cat[3][:, h, :], cat_f[:, h, :], cat[2][:, h, :].bitcast(F32), ALU.subtract).then_inc(sem("cat_lo"), 1)

        def abo_pool(g):
            g.wait_ge(sem("uw"), 2 * TT)
            for name in ("abo0_0", "abo0_1"):
                piece_lo(g, where[name])
            s5_half = catT[:, 0:4, :]
            link(g, g.tensor_copy(cat[0], s5_half), "s5_pool")
            g.tensor_tensor(cat[1], s5_half, cat[0].bitcast(F32), ALU.subtract).then_inc(sem("cat_s5"), 1)

        def gout_pe(pe):
            pe.wait_ge(sem("s_new"), 1 + GH * NCH)
            pe.wait_ge(sem("go_n"), TT)
            for h in range(GH):
                for i in range(TT):
                    ins = pe.transpose(ps[:, 4 + h, i * P:(i + 1) * P], o_t[:, i, h, :], ident)
                ins.then_inc(sem("go_tr"), 1)

        def xres_sp(sp):
            sp.wait_ge(sem("g_at"), 2 * TT)
            sp.wait_ge(sem("g_row"), TT)
            sp.dma_start(x, A["x"].rearrange("(i p) n -> p i n", p=P)).then_inc(sem("x_in"), 16)

        low = Space(base, hT_at)
        high = Space(arena, top)
        hT = (rounded("h_hi", low.at, KT, SEQ), rounded("h_lo", low.at + 4096, KT, SEQ))
        oT = hT
        high_a = high(4096)
        high_b = high(4096)
        high_c = high(4096)
        high_d = high(4096)
        high_e = high(4096)
        at_b, at_c, at_d, at_e, at_f = (arena + 4096 * n for n in range(1, 6))
        rows = lambda v, n=TT: v[:, 0:n * D].rearrange("p (i n) -> p i n", i=n)
        feat = lambda v: v.rearrange("p (k n) -> p k n", k=KT)
        h_rows = rows(high_a)
        q_rows = h_rows
        qT = feat(high_b)
        mem_T = (rounded("mem_hi", at_b, KT, N_MEM), rounded("mem_lo", at_b + 2048, KT, N_MEM))
        xk_rows = rows(reg(at_c, 2048), MT)
        sq_junk = reg(at_c + 2048, 1024)
        xk_T = reg(at_d, KT, N_MEM)
        xv = reg(at_d + 2048, MT, D)
        p_x = [reg(at_e + 1024 * n, TT, N_MEM) for n in range(2)]
        pT_x = [reg(at_e + 2048 + 1024 * n, MT, SEQ) for n in range(2)]
        mem_x = rows(high_a, MT)
        xs = Space(at_f + 2048 + 1200, at_f + 4096)
        kss, kr = xs(MT, XH), xs(MT, XH)
        qss, qr = xs(TT, XH), xs(TT, XH)
        nmax = xs(2, TT)
        psum_x = xs(2, TT)
        prec = xs(2, TT)

        def mem_keep_pool(g):
            g.wait_ge(sem("m_outv"), after("m_outv", KT))
            g.tensor_tensor(memT, mem_T[0].bitcast(F32), mem_T[1].bitcast(F32), ALU.add).then_inc(sem("mem_kept"), 1)

        def mem_split_act(a):
            a.wait_ge(sem("mem_kept"), after("mem_kept", 1))
            a.activation(mem_T[0], memT, ACT.Copy).then_inc(sem("mem_hi"), 1)

        def mem_split_dve(v):
            v.wait_ge(sem("mem_hi"), 1)
            v.tensor_tensor(mem_T[1], memT, mem_T[0].bitcast(F32), ALU.subtract).then_inc(sem("mem_lo"), 1)

        def mem_sp(sp):
            sp.wait_ge(sem("uw"), 2 * TT)
            sp.dma_start(mem_x, A["mem"].rearrange("(i p) n -> p i n", p=P)).then_inc(sem("mem_in"), 16)

        def kv_pe(pe, l):
            t = f"kv{l}"
            for j in range(4):
                rows_pe(pe, t, f"kv{l}{j}", mem_T, MT, 2 * j, ready=(lambda k: ready_T(pe, "m", k)) if l == 0 and j == 0 else None)

        def kv_wait(eng, l, j, i):
            rows_wait(eng, f"kv{l}", f"kv{l}{j}", MT, j, i)

        def kv_act(a, l):
            t = f"kv{l}"
            for j in range(2):
                pieces_hi(a, f"kv{l}{j}_1", 2)
                for i in range(MT):
                    kv_wait(a, l, j, i)
                    b = ps[:, 2 * j + i, :]
                    for h in range(2):
                        n = 4 * j + 2 * i + h
                        if n >= 4:
                            a.wait_ge(sem(f"{t}_sq"), after(f"{t}_sq", n - 3))
                        a.activation(sq_junk[:, (n % 4) * 256:(n % 4 + 1) * 256], b[:, h * 256:(h + 1) * 256], ACT.Square,
                                          accum_out=kss[:, i, 2 * j + h:2 * j + h + 1]).then_inc(sem(f"{t}_sq"), 1)
            a.wait_ge(sem(f"{t}_sq"), after(f"{t}_sq", 8))
            a.activation(kr, kss, ACT.Sqrt, bias=pcol("eps"), scale=1.0 / XD).then_inc(sem(f"{t}_rt"), 1)
            pieces_hi(a, f"kv{l}3_1")
            for i in range(MT):
                kv_wait(a, l, 2, i)
                a.activation(xv[:, i, 0:512], ps[:, 4 + i, :], ACT.Copy).then_inc(sem(f"{t}_v"), 1)
            pieces_hi(a, f"kv{l}3_1", 1)
            for i in range(MT):
                kv_wait(a, l, 3, i)
                a.activation(xv[:, i, 512:1024], ps[:, 6 + i, :], ACT.Copy).then_inc(sem(f"{t}_v"), 1)

        def kv_turned_act(a, l):
            t = f"kv{l}"
            for k in range(4):
                a.wait_ge(sem(f"{t}_turned"), after(f"{t}_turned", k // 2 * 2 + 2))
                a.activation(xk_T[:, k, :], ps[:, k // 2, k % 2 * N_MEM:(k % 2 + 1) * N_MEM], ACT.Copy,
                             scale=pcol(f"xk_g{l}", k % 2)).then_inc(sem(f"{t}_kTa"), 1)

        def kv_dve(v, l):
            t = f"kv{l}"
            pieces_lo(v, f"kv{l}2_1")
            v.wait_ge(sem(f"{t}_rt"), after(f"{t}_rt", 1))
            link(v, v.reciprocal(kr, kr), "dve_step")
            for j in range(2):
                for i in range(MT):
                    v.tensor_tensor(xk_rows[:, i, j * 512:(j + 1) * 512].rearrange("p (h n) -> p h n", h=2),
                                         ps[:, 2 * j + i, :].rearrange("p (h n) -> p h n", h=2),
                                         bc(kr[:, i, 2 * j:2 * j + 2], 2, XD), ALU.mult).then_inc(sem(f"{t}_k"), 1)
            pieces_lo(v, f"kv{l}3_1", 1)

        def kv_turned_dve(v, l):
            t = f"kv{l}"
            for k in range(4, KT):
                v.wait_ge(sem(f"{t}_turned"), after(f"{t}_turned", k // 2 * 2 + 2))
                v.tensor_scalar(xk_T[:, k, :], ps[:, k // 2, k % 2 * N_MEM:(k % 2 + 1) * N_MEM], pcol(f"xk_g{l}", k % 2), None,
                                ALU.mult).then_inc(sem(f"{t}_kTv"), 1)

        def kv_turn_pe(pe, l):
            t = f"kv{l}"
            pe.wait_ge(sem(f"xq{l}_q"), after(f"xq{l}_q", 4))
            for k in range(KT):
                for i in range(MT):
                    ins = pe.transpose(ps[:, k // 2, k % 2 * N_MEM + i * P:k % 2 * N_MEM + (i + 1) * P], xk_rows[:, i, k * P:(k + 1) * P], ident)
                ins.then_inc(sem(f"{t}_turned"), 1)

        def xq_pe(pe, l):
            t = f"xq{l}"
            for j in range(2):
                rows_pe(pe, t, f"xq{l}{j}", hT, TT, 4 * j,
                        ready=(lambda k: ready_T(pe, f"x{l}", k)) if j == 0 else None,
                        bank_free=lambda i: ready_T(pe, f"x{l}", 4 * j + i))
            kv_turn_pe(pe, l)
            for k in range(KT):
                if k == 0:
                    pe.wait_ge(sem(f"{t}_q"), after(f"{t}_q", 8))
                if k == 4:
                    pe.wait_ge(sem(f"kv{l}_kTa"), after(f"kv{l}_kTa", 4))
                    pe.wait_ge(sem(f"kv{l}_kTv"), after(f"kv{l}_kTv", 4))
                for i in range(TT):
                    ins = pe.transpose(ps[:, (k + 4) % 8, i * P:(i + 1) * P], q_rows[:, i, k * P:(k + 1) * P], ident)
                ins.then_inc(sem(f"{t}_turned"), 1)

        def xq_act(a, l):
            t = f"xq{l}"
            for j in range(2):
                pieces_hi(a, f"xq{l}1_1", j)
                sqrt_table(a)
                for i in range(TT):
                    rows_wait(a, t, f"xq{l}{j}", TT, j, i)
                    for h in range(2):
                        n = 8 * j + 2 * i + h
                        if n >= 4:
                            a.wait_ge(sem(f"{t}_sq"), after(f"{t}_sq", n - 3))
                        a.activation(sq_junk[:, (n % 4) * 256:(n % 4 + 1) * 256], ps[:, 4 * j + i, h * 256:(h + 1) * 256], ACT.Square,
                                          accum_out=qss[:, i, 2 * j + h:2 * j + h + 1]).then_inc(sem(f"{t}_sq"), 1)
                a.wait_ge(sem(f"{t}_sq"), after(f"{t}_sq", 8 * (j + 1)))
                a.activation(qr[:, :, 2 * j:2 * j + 2], qss[:, :, 2 * j:2 * j + 2], ACT.Sqrt, bias=pcol("eps"),
                             scale=1.0 / XD).then_inc(sem(f"{t}_rt"), 1)
            kv_turned_act(a, l)
            a.wait_ge(sem("mem_kept"), after("mem_kept", 1))
            for k in range(0, KT, 2):
                a.wait_ge(sem(f"{t}_turned"), after(f"{t}_turned", k + 1))
                a.activation(qT[:, k, :], ps[:, (k + 4) % 8, :], ACT.Copy, scale=pcol(f"xq_g{l}", 0)).then_inc(sem(f"{t}_qTa"), 1)

        def xq_dve(v, l):
            t = f"xq{l}"
            for j in range(2):
                pieces_lo(v, f"xq{l}1_1", j)
                v.wait_ge(sem(f"{t}_rt"), after(f"{t}_rt", j + 1))
                r = qr[:, :, 2 * j:2 * j + 2]
                link(v, v.reciprocal(r, r), "dve_step")
                link(v, v.tensor_scalar(r, r, XD ** -0.5, None, ALU.mult), "dve_step")
                for i in range(TT):
                    v.tensor_tensor(q_rows[:, i, j * 512:(j + 1) * 512].rearrange("p (h n) -> p h n", h=2),
                                         ps[:, 4 * j + i, :].rearrange("p (h n) -> p h n", h=2),
                                         bc(qr[:, i, 2 * j:2 * j + 2], 2, XD), ALU.mult).then_inc(sem(f"{t}_q"), 1)
            kv_turned_dve(v, l)
            v.wait_ge(sem("mem_kept"), after("mem_kept", 1))
            for k in range(1, KT, 2):
                v.wait_ge(sem(f"{t}_turned"), after(f"{t}_turned", k + 1))
                v.tensor_scalar(qT[:, k, :], ps[:, (k + 4) % 8, :], pcol(f"xq_g{l}", 1), None, ALU.mult).then_inc(sem(f"{t}_qTv"), 1)

        def xa_scores_pe(pe, l, h):
            t = f"xa{l}"
            if h == 0:
                for k in range(KT):
                    pe.wait_ge(sem(f"xq{l}_qT{'av'[k % 2]}"), after(f"xq{l}_qT{'av'[k % 2]}", k // 2 + 1))
            if h >= 2:
                pe.wait_ge(sem(f"{t}_exp"), after(f"{t}_exp", TT * (h - 1)))
            for i in range(TT):
                for d in range(2):
                    ins = pe.matmul(ps[:, 2 * (h % 2) + i // 2, (i % 2) * 256:(i % 2) * 256 + 256],
                                    qT[:, 2 * h + d, i * P:(i + 1) * P], xk_T[:, 2 * h + d, :], start=(d == 0), stop=(d == 1))
            ins.then_inc(sem(f"{t}_s"), 1)

        def xa_turn_pe(pe, l, h):
            t = f"xa{l}"
            pe.wait_ge(sem(f"{t}_p"), after(f"{t}_p", h + 1))
            if h > 0:
                pe.wait_ge(sem(f"{t}_pTa"), after(f"{t}_pTa", h))
                pe.wait_ge(sem(f"{t}_pTv"), after(f"{t}_pTv", h))
            for s in range(MT):
                for i in range(TT):
                    ins = pe.transpose(ps[:, 4 + s, i * P:(i + 1) * P], p_x[h % 2][:, i, s * P:(s + 1) * P], ident)
                ins.then_inc(sem(f"{t}_tr"), 1)

        def xa_values_pe(pe, l, h):
            t = f"xa{l}"
            pe.wait_ge(sem(f"{t}_pTa"), after(f"{t}_pTa", h + 1))
            pe.wait_ge(sem(f"{t}_pTv"), after(f"{t}_pTv", h + 1))
            if h > 0:
                pe.wait_ge(sem(f"{t}_ov"), after(f"{t}_ov", 2 * h))
            for d in range(2):
                for s in range(MT):
                    ins = pe.matmul(ps[:, 6 + d, :], xv[:, s, h * XD + d * P:h * XD + (d + 1) * P], pT_x[h % 2][:, s, :], start=(s == 0), stop=(s == 1))
                ins.then_inc(sem(f"{t}_o"), 1)

        def xa_act(a, l):
            t = f"xa{l}"

            def exps(h):
                a.wait_ge(sem(f"{t}_max"), after(f"{t}_max", h + 1))
                if h >= 2:
                    a.wait_ge(sem(f"{t}_tr"), after(f"{t}_tr", 2 * (h - 1)))
                for i in range(TT):
                    a.activation(p_x[h % 2][:, i, :], ps[:, 2 * (h % 2) + i // 2, (i % 2) * 256:(i % 2) * 256 + 256], ACT.Exp,
                                      bias=nmax[:, h % 2, i:i + 1], accum_out=psum_x[:, h % 2, i:i + 1]).then_inc(sem(f"{t}_exp"), 1)
            exps(0)
            for h in range(XH):
                a.wait_ge(sem(f"{t}_tr"), after(f"{t}_tr", 2 * h + 1))
                if h >= 2:
                    a.wait_ge(sem(f"{t}_o"), after(f"{t}_o", 2 * (h - 1)))
                a.activation(pT_x[h % 2][:, 0, :], ps[:, 4, :], ACT.Copy).then_inc(sem(f"{t}_pTa"), 1)
                if h + 1 < XH:
                    exps(h + 1)
                for d in range(2):
                    a.wait_ge(sem(f"{t}_o"), after(f"{t}_o", 2 * h + d + 1))
                    a.activation(oT[0][:, 2 * h + d, :], ps[:, 6 + d, :], ACT.Copy).then_inc(sem(f"{t}_oa"), 1)
                if h == 0:
                    pieces_hi(a, f"xq{l}1_1", 2)

        def xa_dve(v, l):
            t = f"xa{l}"

            def maxes(h):
                v.wait_ge(sem(f"{t}_s"), after(f"{t}_s", h + 1))
                v.tensor_reduce(nmax[:, h % 2, :], ps[:, 2 * (h % 2):2 * (h % 2) + 2, :].rearrange("p b (i n) -> p (b i) n", i=2),
                                     AX, ALU.max, negate=True).then_inc(sem(f"{t}_max"), 1)
            def rescale(h):
                v.wait_ge(sem(f"{t}_exp"), after(f"{t}_exp", TT * (h + 1)))
                link(v, v.reciprocal(prec[:, h % 2, :], psum_x[:, h % 2, :]), "dve_step")
                v.tensor_tensor(p_x[h % 2], p_x[h % 2], bc(prec[:, h % 2, :], 2, N_MEM), ALU.mult).then_inc(sem(f"{t}_p"), 1)

            maxes(0)
            maxes(1)
            rescale(0)
            for h in range(XH):
                v.wait_ge(sem(f"{t}_tr"), after(f"{t}_tr", 2 * h + 2))
                if h >= 2:
                    v.wait_ge(sem(f"{t}_o"), after(f"{t}_o", 2 * (h - 1)))
                v.tensor_copy(pT_x[h % 2][:, 1, :], ps[:, 5, :]).then_inc(sem(f"{t}_pTv"), 1)
                if h + 1 < XH:
                    rescale(h + 1)
                if h + 2 < XH:
                    maxes(h + 2)
                for d in range(2):
                    v.wait_ge(sem(f"{t}_oa"), after(f"{t}_oa", 2 * h + d + 1))
                    v.tensor_tensor(oT[1][:, 2 * h + d, :], ps[:, 6 + d, :], oT[0][:, 2 * h + d, :].bitcast(F32),
                                    ALU.subtract).then_inc(sem(f"{t}_ov"), 1)
                if h == 0:
                    pieces_lo(v, f"xq{l}1_1", 2)

        def xa_pe(pe, l):
            xa_scores_pe(pe, l, 0)
            xa_scores_pe(pe, l, 1)
            for h in range(XH):
                xa_turn_pe(pe, l, h)
                if h + 2 < XH:
                    xa_scores_pe(pe, l, h + 2)
                xa_values_pe(pe, l, h)

        aT = (rounded("a_hi", arena, FT * SEQ), rounded("a_lo", arena + FT * SEQ, FT * SEQ))
        up = tensor_at("up", at_f + 2048, F32, 4, SEQ)
        gsil, prod = up[:, 0:2, :], up[:, 2:4, :]
        gs_junk = reg(at_f + 2048, 2 * SEQ)

        def ffn_up_pe(pe, l):
            n0 = where[f"gu{l}_0"]

            def pair(j, first):
                for s in range(2):
                    pe.wait_ge(sem("w_lo"), j * 2 + (nth(n0) + s + 1))
                    if not (first and s == 0):
                        pe.wait_ge(sem(f"f{l}_free"), j * 2 + after(f"f{l}_free", s + 1))
                    w = tuple(v[:, (n0 + s) % 2, :].rearrange("p (k n) -> p k n", k=KT) for v in (w_hi, w_lo(n0)))
                    for gu in range(2):
                        for k in range(KT):
                            if first and s == 0 and gu == 0:
                                ready_T(pe, f"f{l}", k)
                            ins = product(pe, ps[:, 4 * s + gu, :], of(w, k, slice(gu * P, (gu + 1) * P)), of(hT, k), k == 0, k == KT - 1)
                        if gu == 0:
                            ins.then_inc(sem(f"f{l}_mm"), 1)
                        else:
                            ins.then_inc(panel_used, 1)

            pair(0, True)
            with pe.Fori(1, FT // 2) as j:
                pair(j, False)

        def ffn_up_act(a, l):
            n0 = where[f"gu{l}_0"]
            with a.Fori(0, FT // 2) as j:
                for s in range(2):
                    slot = (n0 + s) % 2
                    a.wait_ge(sem(f"f{l}_mm"), j * 2 + after(f"f{l}_mm", s + 1))
                    a.wait_ge(sem(f"f{l}_free"), j * 2 + after(f"f{l}_free", s + 1))
                    a.activation(gsil[:, s, :], ps[:, 4 * s, :], ACT.Silu).then_inc(sem(f"f{l}_silu"), 1)
                    a.wait_ge(slot_landed[slot], j * 32 + landed[n0 + s + 2])
                    a.wait_ge(panel_used, j * 2 + (n0 + s + 1))
                    a.activation(w_hi[:, slot, :], raw[slot], ACT.Copy).then_inc(sem("w_hi"), 1)
            split["a"] = n0 + FT + 2

        def ffn_up_dve(v, l):
            n0 = where[f"gu{l}_0"]
            v.memset(spare[:, 0:1], 0.0).then_inc(sem(f"f{l}_free"), 2)
            with v.Fori(0, FT // 2) as j:
                for s in range(2):
                    slot = (n0 + s) % 2
                    v.wait_ge(sem(f"f{l}_silu"), j * 2 + after(f"f{l}_silu", s + 1))
                    v.wait_ge(panel_used, j * 2 + (n0 + s + 1))
                    v.wait_ge(sem(f"f{l}_alo"), j * 2 + after(f"f{l}_alo", s + 1))
                    v.tensor_tensor(prod[:, s, :], gsil[:, s, :], ps[:, 4 * s + 1, :], ALU.mult).then_inc(sem(f"f{l}_free"), 1)
                    v.wait_ge(sem("w_hi"), j * 2 + (nth(n0) + s + 3))
                    v.tensor_tensor(w_lo(n0)[:, slot, :], raw[slot], w_hi[:, slot, :].bitcast(F32), ALU.subtract).then_inc(sem("w_lo"), 1)
            split["v"] = n0 + FT + 2

        def ffn_up_pool(g, l):
            g.memset(spare[:, 1:2], 0.0).then_inc(sem(f"f{l}_alo"), 2)
            with g.Fori(0, FT // 2) as j:
                for s in range(2):
                    at = bass.ds(j * (2 * SEQ) + s * SEQ, SEQ)
                    g.wait_ge(sem(f"f{l}_free"), j * 2 + after(f"f{l}_free", s + 3))
                    g.tensor_copy(aT[0][:, at], prod[:, s, :]).then_inc(sem(f"f{l}_ahi"), 1)
                    g.wait_ge(sem(f"f{l}_ahi"), j * 2 + after(f"f{l}_ahi", s + 1))
                    g.tensor_tensor(aT[1][:, at], prod[:, s, :], aT[0][:, at].bitcast(F32), ALU.subtract).then_inc(sem(f"f{l}_alo"), 1)

        def ffn_down_pe(pe, l):
            pe.wait_ge(sem(f"f{l}_free"), after(f"f{l}_free", 2 + FT))
            for j in range(FT // 2):
                w = take_split(pe, f"dn{l}_{j}", 2)
                for kk in range(2):
                    k = 2 * j + kk
                    pe.wait_ge(sem(f"f{l}_alo"), after(f"f{l}_alo", 2 + k + 1))
                    for half in range(2):
                        for i in range(TT):
                            ins = product(pe, ps[:, 4 * half + i, :], of(aT, slice(k * SEQ + i * P, k * SEQ + (i + 1) * P)),
                                          of(w, kk, slice(half * 512, (half + 1) * 512)), k == 0, k == FT - 1)
                            if k == FT - 1 and not (half == 1 and i == TT - 1):
                                ins.then_inc(sem(f"d{l}_mm"), 1)
                ins.then_inc(panel_used, 1)

        def down_dve(v, l):
            pieces_lo(v, f"dn{l}_{FT // 2 - 1}", 1)
            for half in range(2):
                for i in range(TT):
                    if half == 1 and i == TT - 1:
                        v.wait_ge(panel_used, where[f"dn{l}_{FT // 2 - 1}"] + 1)
                    else:
                        v.wait_ge(sem(f"d{l}_mm"), after(f"d{l}_mm", 4 * half + i + 1))
                    v.tensor_tensor(x[:, i, half * 512:(half + 1) * 512], ps[:, 4 * half + i, :],
                                         x[:, i, half * 512:(half + 1) * 512], ALU.add).then_inc(sem(f"d{l}_x"), 1)

        v_rows = rows(high_e)
        bias_ring = reg(at_f, 4, BAND_W)
        cs = Space(at_f + 2048, at_f + 2048 + 1200)
        cq_scaled = cs(1)
        c_tmp = cs(2, CH // 2, CD)
        c_ss, c_rt, c_r = cs(2, CH // 2), cs(2, CH // 2), cs(2, CH // 2)
        c_max, c_neg, c_sum, c_rec = cs(2, TT), cs(2, TT), cs(2, TT), cs(2, TT)
        ck_rows = rows(high_b)
        cqT, ckT = feat(high_c), feat(high_d)
        p_c = [reg(arena + 2048 * n, TT, SEQ) for n in range(2)]
        pT_c = [reg(at_b + 2048 * n, TT, SEQ) for n in range(2)]
        c_oT = hT

        def ca_proj_pe(pe):
            def bank_free(n):
                if n < 8:
                    ready_T(pe, "c", n)
                else:
                    pe.wait_ge(sem("c_rows"), n - 7)
            for p in range(6):
                rows_pe(pe, "ca", f"ca{p}", hT, TT, 4 * (p % 2),
                        ready=(lambda k: ready_T(pe, "c", k)) if p == 0 else None,
                        bank_free=lambda i: bank_free(4 * p + i))

        def ca_proj_act(a):
            for n in range(16):
                if n % 4 == 0:
                    pieces_hi(a, f"ca{n // 4}_1", 2)
                rows_wait(a, "ca", f"ca{n // 4}", TT, n // 4, n % 4)
                if n >= 2:
                    a.wait_ge(sem("c_rows"), n - 1)
                a.activation(c_tmp[:, n % 2].rearrange("p a b -> p (a b)"), ps[:, n % 8, :], ACT.Square).then_inc(sem("c_sqs"), 1)
                a.wait_ge(sem("c_ss"), n + 1)
                a.activation(c_rt[:, n % 2, :], c_ss[:, n % 2, :], ACT.Sqrt, bias=pcol("eps"), scale=1.0 / CD).then_inc(sem("ca_root"), 1)
            for n in range(16, 24):
                if n % 4 == 0:
                    pieces_hi(a, "ca5_1", n // 4 - 4)
                rows_wait(a, "ca", f"ca{n // 4}", TT, n // 4, n % 4)
                c0 = (n // 4 - 4) * 512
                a.activation(v_rows[:, n % 4, c0:c0 + 512], ps[:, n % 8, :], ACT.Copy).then_inc(sem("c_v"), 1)

        def ca_proj_dve(v):
            link(v, v.tensor_scalar(cq_scaled, pcol("cq_g"), CD ** -0.5, None, ALU.mult), "c_scale")
            for n in range(16):
                if n % 4 == 0:
                    pieces_lo(v, f"ca{n // 4}_1", 2)
                v.wait_ge(sem("c_sqs"), n + 1)
                v.tensor_reduce(c_ss[:, n % 2, :], c_tmp[:, n % 2], AX, ALU.add).then_inc(sem("c_ss"), 1)
                v.wait_ge(sem("ca_root"), n + 1)
                link(v, v.reciprocal(c_r[:, n % 2, :], c_rt[:, n % 2, :]), "dve_step")
                dst = (q_rows if n < 8 else ck_rows)[:, n % 4, (n // 4 % 2) * 512:(n // 4 % 2 + 1) * 512]
                v.tensor_tensor(dst.rearrange("p (h n) -> p h n", n=CD), ps[:, n % 8, :].rearrange("p (h n) -> p h n", n=CD),
                                     bc(c_r[:, n % 2, :], 2, CD), ALU.mult).then_inc(sem("c_rows"), 1)

        def ca_turn_pe(pe):
            for m in range(16):
                if m < 8:
                    pe.wait_ge(sem("c_v"), m + 1)
                    if m == 0:
                        pe.wait_ge(sem("c_rows"), 16)
                else:
                    pe.wait_ge(sem(f"c_T{'av'[m % 2]}"), after(f"c_T{'av'[m % 2]}", (m - 8) // 2 + 1))
                for i in range(TT):
                    ins = pe.transpose(ps[:, m % 8, i * P:(i + 1) * P], (q_rows if m < 8 else ck_rows)[:, i, (m % 8) * P:(m % 8 + 1) * P], ident)
                ins.then_inc(sem("ca_turned"), 1)

        def ca_turn_evac(eng, act):
            for m in range(0 if act else 1, 16, 2):
                eng.wait_ge(sem("ca_turned"), m + 1)
                dst, src = (cqT if m < 8 else ckT)[:, m % 8, :], ps[:, m % 8, :]
                if m < 8:
                    dst, src = dst.rearrange("p (i n) -> p i n", i=TT), src.rearrange("p (i n) -> p i n", i=TT)[:, :, ::-1]
                scale = cq_scaled if m < 8 else pcol("ck_g")
                if act:
                    if m == 0:
                        eng.wait_ge(sem("c_scale"), 1)
                    eng.activation(dst, src, ACT.Copy, scale=scale).then_inc(sem("c_Ta"), 1)
                else:
                    eng.tensor_scalar(dst, src, scale, None, ALU.mult).then_inc(sem("c_Tv"), 1)

        def ca_scores_pe(pe, h):
            r = slice(64 * (h % 2), 64 * (h % 2) + 64)
            if h == 0:
                pe.wait_ge(sem("c_Ta"), 8)
                pe.wait_ge(sem("c_Tv"), 8)
            for i in range(TT):
                if h > 0:
                    pe.wait_ge(sem("c_s2"), 4 * (h - 1) + i + 1)
                n = (i + 1) * P
                pe.matmul(ps[:, i, 0:n], cqT[r, h // 2, i * P:(i + 1) * P], ckT[r, h // 2, 0:n], start=True, stop=True).then_inc(sem("c_s"), 1)

        def ca_turn_p_pe(pe, h):
            for s in range(TT):
                m = 4 * h + s
                if m >= 3:
                    pe.wait_ge(sem(COPY[(m - 3) % 4][0]), 2 * ((m - 3) // 4) + COPY[(m - 3) % 4][1])
                for i in range(s, TT):
                    if s == 0:
                        pe.wait_ge(sem("c_p"), 4 * h + i + 1)
                    ins = pe.transpose(ps[:, 4 + m % 3, i * P:(i + 1) * P], p_c[h % 2][:, i, s * P:(s + 1) * P], ident)
                ins.then_inc(sem("c_tr"), 1)

        def ca_values_pe(pe, h):
            r = slice(64 * (h % 2), 64 * (h % 2) + 64)
            if h > 0:
                pe.wait_ge(sem("c_ol"), h)
            for s in range(TT):
                pe.wait_ge(sem(COPY[s][0]), 2 * h + COPY[s][1])
                ins = pe.matmul(ps[r, 7, s * P:SEQ], v_rows[:, s, h * CD:(h + 1) * CD], pT_c[h % 2][:, s, s * P:SEQ],
                                start=(s == 0), stop=(s == TT - 1), skip_group_check=True)
            ins.then_inc(sem("c_o"), 1)

        COPY = [("c_pa", 1), ("c_pv", 1), ("c_pv", 2), ("c_pa", 2)]

        def ca_copy(eng, h, s):
            eng.wait_ge(sem("c_tr"), 4 * h + s + 1)
            if h >= 2:
                eng.wait_ge(sem("c_o"), h - 1)
            dst, src = pT_c[h % 2][:, s, s * P:SEQ], ps[:, 4 + (4 * h + s) % 3, s * P:SEQ]
            if COPY[s][0] == "c_pa":
                eng.activation(dst, src, ACT.Copy).then_inc(sem("c_pa"), 1)
            else:
                eng.tensor_copy(dst, src).then_inc(sem("c_pv"), 1)

        def ca_pe(pe):
            ca_scores_pe(pe, 0)
            ca_scores_pe(pe, 1)
            for h in range(CH):
                ca_turn_p_pe(pe, h)
                if h + 2 < CH:
                    ca_scores_pe(pe, h + 2)
                ca_values_pe(pe, h)

        def ca_sp(sp, h):
            if h == 0:
                sp.wait_ge(sem("c_rows"), 1)
            if h >= 4:
                sp.wait_ge(sem("c_s2"), 4 * (h - 3))
            e = A["rel_rows"]
            src = bass.AP(e.tensor, h * BAND_E, [[1, P], [1, BAND_W]])
            sp.dma_start(bias_ring[:, h % 4, :], src).then_inc(sem(f"bias_in{h % 4}"), 16)

        def ca_act(a):
            def exps(h):
                a.wait_ge(sem("c_max"), h + 1)
                for i in range(TT):
                    n = (i + 1) * P
                    a.activation(p_c[h % 2][:, i, 0:n], p_c[h % 2][:, i, 0:n], ACT.Exp, bias=c_neg[:, h % 2, i:i + 1],
                                      accum_out=c_sum[:, h % 2, i:i + 1]).then_inc(sem("c_exp"), 1)
            exps(0)
            for h in range(CH):
                ca_copy(a, h, 0)
                ca_copy(a, h, 3)
                if h + 1 < CH:
                    exps(h + 1)
                a.wait_ge(sem("c_o"), h + 1)
                r = slice(64 * (h % 2), 64 * (h % 2) + 64)
                a.activation(c_oT[0][r, h // 2, :].rearrange("p (i n) -> p i n", i=TT),
                                  ps[r, 7, :].rearrange("p (i n) -> p i n", i=TT)[:, :, ::-1], ACT.Copy).then_inc(sem("c_oc"), 1)

        def ca_dve(v):
            def sums(h):
                v.wait_ge(sem(f"bias_in{h % 4}"), after(f"bias_in{h % 4}", 16 * (h // 4 + 1)))
                link(v, v.memset(bias_ring[64:P, h % 4, BAND_W - 64:BAND_W], -1e30), "dve_step")
                if h >= 2:
                    v.wait_ge(sem("c_tr"), 4 * (h - 1))
                for i in range(TT):
                    n = (i + 1) * P
                    v.wait_ge(sem("c_s"), 4 * h + i + 1)
                    v.tensor_tensor_reduce(out=p_c[h % 2][:, i, 0:n], in0=ps[:, i, 0:n],
                                                in1=bias_ring[:, h % 4, BAND_W - n:BAND_W], scale=1.0, scalar=-3.0e38,
                                                op0=ALU.add, op1=ALU.max, accum_out=c_max[:, h % 2, i:i + 1]).then_inc(sem("c_s2"), 1)
                v.wait_ge(sem("c_s2"), 4 * h + 4)
                v.tensor_scalar(c_neg[:, h % 2, :], c_max[:, h % 2, :], -1.0, None, ALU.mult).then_inc(sem("c_max"), 1)

            def out_lo(h):
                r = slice(64 * (h % 2), 64 * (h % 2) + 64)
                v.wait_ge(sem("c_oc"), h + 1)
                v.tensor_tensor(c_oT[1][r, h // 2, :].rearrange("p (i n) -> p i n", i=TT),
                                ps[r, 7, :].rearrange("p (i n) -> p i n", i=TT)[:, :, ::-1],
                                c_oT[0][r, h // 2, :].bitcast(F32).rearrange("p (i n) -> p i n", i=TT), ALU.subtract).then_inc(sem("c_ol"), 1)

            def rescale(h):
                v.wait_ge(sem("c_exp"), 4 * h + 4)
                link(v, v.reciprocal(c_rec[:, h % 2, :], c_sum[:, h % 2, :]), "dve_step")
                for i in range(TT):
                    n = (i + 1) * P
                    v.tensor_scalar(p_c[h % 2][:, i, 0:n], p_c[h % 2][:, i, 0:n], c_rec[:, h % 2, i:i + 1], None, ALU.mult).then_inc(sem("c_p"), 1)

            sums(0)
            sums(1)
            rescale(0)
            for h in range(CH):
                if h > 0:
                    out_lo(h - 1)
                ca_copy(v, h, 1)
                ca_copy(v, h, 2)
                if h + 1 < CH:
                    rescale(h + 1)
                if h + 2 < CH:
                    sums(h + 2)
            out_lo(CH - 1)

        def load_panel(sp, name):
            n = where[name]
            if n >= PIECE0 + 2 or 2 <= n < AB_PIECES:
                sp.wait_ge(sem("w_lo"), nth(n - 2) + 1)
            elif n >= PIECE0:
                sp.wait_ge(sem("w_lo"), AB_PIECES)
            elif name == "glu":
                sp.wait_ge(panel_used, AB_PIECES)
            for dst, src in panels[n][1]:
                if name in whole_slot:
                    sp.dma_start(dst(slots[whole_slot[name]]), src).then_inc(sem(f"{name}_landed"), 16)
                else:
                    sp.dma_start(dst(raw[n % 2]), src).then_inc(slot_landed[n % 2], 16)

        def load_pieces(sp, first, last):
            for n in range(where[first], where[last] + 1):
                load_panel(sp, panels[n][0])

        block = ctx.enter_context(nc.Block())
        abo, cao = ["abo0", "abo1"], ["cao0", "cao1"]
        xo = [[f"xo{l}0", f"xo{l}1"] for l in range(DEPTH)]

        @block.sync
        def _(sp):
            for i in range(TT):
                sp.dma_start(x0[:, i, :], A["x"][i * P:(i + 1) * P, :]).then_inc(sem(f"x_tile{i}"), 16)
                if i == 0:
                    sp.dma_start(par, A["par"]).then_inc(sem("par_in"), 16)
            sp.dma_start(con, A["con"]).then_inc(sem("con_in"), 16)
            load_pieces(sp, "ab0_0", "ab0_1")
            sp.dma_start(w_ab, A["ab_w_in"][:, 2560:2568].rearrange("(k p) n -> p k n", p=P)).then_inc(sem("wab_in"), 16)
            sp.dma_start(s5_bc, A["s5_bc"]).then_inc(sem("bc_in"), 16)
            load_pieces(sp, "ab1_0", "ab4_1")
            load_panel(sp, "glu")
            s5_u_sp(sp)
            load_pieces(sp, "abo0_0", "abo0_1")
            xres_sp(sp)
            mem_sp(sp)
            load_pieces(sp, "abo1_0", "abo1_1")
            load_pieces(sp, "kv00_0", "ca5_1")
            for h in range(4):
                ca_sp(sp, h)
            load_pieces(sp, "cao0_0", "cao0_1")
            for h in range(4, CH):
                ca_sp(sp, h)
            load_pieces(sp, "cao1_0", f"dn1_{FT // 2 - 1}")
            for i in range(TT):
                sp.wait_ge(sem("d1_x"), after("d1_x", TT + i + 1))
                sp.dma_start(A["out"][i * P:(i + 1) * P, :], x[:, i, :]).then_inc(sem("stored"), 16)
            sp.wait_ge(sem("stored"), 16 * TT)

        @block.tensor
        def _(pe):
            pe.wait_ge(sem("con_in"), 16)
            norm_pe(pe, "n0", x0, h0)
            for p in range(4):
                ab_groups_pe(pe, p)
            ab_groups_pe(pe, 4)
            logits_pe(pe)
            s5_tables_pe(pe)
            gates_pe(pe)
            s5_states_pe(pe)
            s5_tm_pe(pe)
            s5_out_pe(pe)
            s5_back_pe(pe)
            gdn_turn_pe(pe, 0)
            s5_glu_pe(pe)
            gdn_back_pe(pe, 0)
            for i in range(TT):
                if i + 1 < TT:
                    gdn_turn_pe(pe, i + 1)
                gdn_prod_pe(pe, i)
                if i + 1 < TT:
                    gdn_back_pe(pe, i + 1)
            solve_pe(pe)
            uw_pe(pe)
            rec_pe(pe)


            def cat_ready(k):
                if k == 0:
                    pe.wait_ge(sem("r_o"), NCH)
                    pe.wait_ge(sem("cat_s5"), 1)
                if k >= 4:
                    pe.wait_ge(sem("cat_lo"), after("cat_lo", k - 3))
            rows_pe(pe, "mo", "abo0", cat, TT, 0, ready=cat_ready, between=lambda: gout_pe(pe))
            rows_pe(pe, "mo", "abo1", cat, TT, 4)
            pe.wait_ge(sem("mo_x"), after("mo_x", 8))
            norm_pe(pe, "m", mem_x, mem_x)
            for l in range(DEPTH):
                if l == 1:
                    pe.wait_ge(sem("mem_lo"), 1)
                kv_pe(pe, l)
                pe.wait_ge(sem(f"kv{l}_k"), after(f"kv{l}_k", 4))
                pe.wait_ge(sem(f"kv{l}_v"), after(f"kv{l}_v", 4))
                norm_pe(pe, f"x{l}", x, h_rows)
                xq_pe(pe, l)
                xa_pe(pe, l)

                pe.wait_ge(sem(f"xa{l}_ov"), after(f"xa{l}_ov", KT))
                split_outproj_pe(pe, f"xo{l}", xo[l], oT)
                pe.wait_ge(sem(f"xo{l}_x"), after(f"xo{l}_x", 8))
                norm_pe(pe, f"f{l}", x, h_rows)
                ffn_up_pe(pe, l)
                ffn_down_pe(pe, l)
                if l == 0:
                    pe.wait_ge(sem("d0_x"), after("d0_x", 8))
                    norm_pe(pe, "c", x, h_rows)
                    ca_proj_pe(pe)
                    ca_turn_pe(pe)
                    ca_pe(pe)
                    pe.wait_ge(sem("c_ol"), CH)
                    split_outproj_pe(pe, "co", cao, c_oT)
                    pe.wait_ge(sem("co_x"), after("co_x", 8))

        @block.scalar
        def _(a):
            a.wait_ge(sem("par_in"), 16)
            squares_act(a, "n0", x0, sq_junk0, ss2)
            norm_act(a, "n0", TT, hT0, "ab_g", ("ab0_1",))
            a.wait_ge(sem("wab_in"), 16)
            a.activation(w_ab_split[:, :, 0, :], w_ab, ACT.Copy).then_inc(sem("wab_hi"), 1)
            s5_params_act(a)
            for n in range(12):
                pieces_hi(a, *ab_ahead(n))
                silu_act(a, n)
            for n in range(12, 16):
                pieces_hi(a, *ab_ahead(n))
                gate_act(a, n)
            for n in range(16, 20):
                u_act(a, n)
            gates_act(a)
            s5_tables_act(a)
            gates_decays_act(a)
            s5_tm_act(a)
            s5_out_act(a)
            s5_glu_act(a)
            gdn_tok_act(a, 0)
            s5_gated_act(a)
            gdn_back_act(a, 0)
            for i in range(TT):
                if i + 1 < TT:
                    gdn_tok_act(a, i + 1)
                gdn_dec_act(a, i)
                if i + 1 < TT:
                    gdn_back_act(a, i + 1)
            solve_act(a)
            uw_act(a)
            pieces_hi(a, "abo0_1")
            rec_act(a)
            gout_act(a)
            gout_hi_act(a)
            a.wait_ge(sem("mem_in"), 16)
            squares_act(a, "m", mem_x, sq_junk, rms_m)
            norm_root_act(a, "m", MT)
            pieces_hi(a, "abo1_1", 1)
            norm_out_act(a, "m", MT, mem_T, "mem_g", ("kv00_1",))
            squares_act(a, "x0", x, sq_junk, ss2, "mo_x")
            for l in range(DEPTH):
                if l == 1:
                    squares_act(a, "x1", x, sq_junk, ss2, "co_x", "cao1_1")
                pieces_hi(a, f"kv{l}0_1")
                norm_root_act(a, f"x{l}", TT)
                kv_act(a, l)
                norm_out_act(a, f"x{l}", TT, hT, f"xa_g{l}", (f"kv{l}3_1", 2))
                xq_act(a, l)
                xa_act(a, l)
                squares_act(a, f"f{l}", x, sq_junk, ss2, f"xo{l}_x", f"xo{l}1_1")
                norm_act(a, f"f{l}", TT, hT, f"f_g{l}", (f"xo{l}1_1", 2))
                ffn_up_act(a, l)
                pieces_hi(a, f"dn{l}_{FT // 2 - 1}", 1)
                if l == 0:
                    squares_act(a, "c", x, gs_junk, ss2, "d0_x")
                    norm_act(a, "c", TT, hT, "c_g", (f"dn0_{FT // 2 - 1}", 2))
                    ca_proj_act(a)
                    ca_turn_evac(a, True)
                    pieces_hi(a, "ca5_1", 2)
                    ca_act(a)
                    mem_split_act(a)

        @block.vector
        def _(v):
            for i in range(TT):
                v.wait_ge(sem(f"x_tile{i}"), 16)
            v.wait_ge(sem("par_in"), 16)
            norm_dve(v, "n0", x0, h0, ss2, hT0, "ab_g", ("ab0_1",))
            v.wait_ge(sem("wab_hi"), 1)
            v.tensor_tensor(w_ab_split[:, :, 1, :], w_ab, w_ab_split[:, :, 0, :].bitcast(F32), ALU.subtract).then_inc(sem("wab_lo"), 1)
            v.wait_ge(sem("con_in"), 16)
            for n in range(12):
                conv_dve(v, n)
                pieces_lo(v, *ab_ahead(n))
                if n == 3:
                    s5_rd_dve(v)
                if n >= 8:
                    s5_g_dve(v, n - 8)
            pieces_lo(v, *ab_ahead(15))
            logits_dve(v)
            s5_pad_dve(v)
            gates_dve(v)
            gates_sums_dve(v)
            s5_v_dve(v)
            s5_states_dve(v)
            s5_out_dve(v)
            s5_glu_dve(v)
            gdn_tok_dve(v, 0)
            s5_gated_dve(v)
            for i in range(TT):
                if i + 1 < TT:
                    gdn_tok_dve(v, i + 1)
                gdn_prod_dve(v, i)
            solve_dve(v)
            uw_dve(v)
            rec_dve(v)
            gout_dve(v)
            split["v"] = where["abo1_0"]
            norm_rows_dve(v, "m", mem_x, mem_x, rms_m)
            v.wait_ge(sem("x_in"), 16)
            outproj_dve(v, "mo", abo, x)
            norm_out_dve(v, "m", MT, mem_T, "mem_g", ("kv00_1",))
            for l in range(DEPTH):
                pieces_lo(v, f"kv{l}0_1")
                norm_rows_dve(v, f"x{l}", x, h_rows, ss2)
                kv_dve(v, l)
                norm_out_dve(v, f"x{l}", TT, hT, f"xa_g{l}", (f"kv{l}3_1", 2))
                xq_dve(v, l)
                xa_dve(v, l)
                outproj_dve(v, f"xo{l}", xo[l], x)
                norm_dve(v, f"f{l}", x, h_rows, ss2, hT, f"f_g{l}", (f"xo{l}1_1", 2))
                ffn_up_dve(v, l)
                down_dve(v, l)
                if l == 0:
                    norm_dve(v, "c", x, h_rows, ss2, hT, "c_g", (f"dn0_{FT // 2 - 1}", 2))
                    ca_proj_dve(v)
                    pieces_lo(v, "ca5_1", 1)
                    ca_turn_evac(v, False)
                    pieces_lo(v, "ca5_1", 2)
                    ca_dve(v)
                    mem_split_dve(v)
                    outproj_dve(v, "co", cao, x)

        @block.gpsimd
        def _(g):
            g.wait_ge(sem("par_in"), 16)
            s5_params_pool(g)
            g.wait_ge(sem("con_in"), 16)
            solve_start_pool(g)
            solve_masks_pool(g)
            abo_pool(g)
            mem_keep_pool(g)
            ffn_up_pool(g, 0)
            ffn_up_pool(g, 1)


def _layout(inputs):
    import numpy as np

    f = {k: np.ascontiguousarray(np.asarray(v)) for k, v in inputs.items()}

    def cols(v):
        return v.reshape(-1, P).T

    gp = lambda a: a.reshape(S5_GP, 2, S5_P).transpose(1, 2, 0).reshape(P, S5_GP)
    ri = lambda a: np.concatenate([a.T, a.T], 0)
    rep = lambda row: np.broadcast_to(row[None, :], (P, row.size))
    both = lambda a: np.concatenate([ri(a), gp(a)], 1)
    ones = np.ones((P, 1), np.float32)
    sgn = np.concatenate([-ones[:64], ones[64:]], 0)
    parts = {
        "ab_g": cols(f["ab_norm_g"][0]), "c_g": cols(f["c_norm_g"][0]), "mem_g": cols(f["mem_norm_g"]),
        "xa_g0": cols(f["xa_norm_g"][0]), "xa_g1": cols(f["xa_norm_g"][1]), "f_g0": cols(f["f_norm_g"][0]), "f_g1": cols(f["f_norm_g"][1]),
        "s5_d": cols(f["s5_d"][0].reshape(-1)), "b_glu": cols(f["s5_b_glu"][0]),
        "conv": f["gdn_conv_w"][0].reshape(4, 12, P).transpose(2, 0, 1).reshape(P, 48),
        "gdn_g": cols(f["gdn_out_norm_g"][0]),
        "xq_g0": cols(f["xa_q_norm_g"][0]), "xq_g1": cols(f["xa_q_norm_g"][1]),
        "xk_g0": cols(f["xa_k_norm_g"][0]), "xk_g1": cols(f["xa_k_norm_g"][1]),
        "cq_g": np.concatenate([f["c_q_norm_g"][0]] * 2)[:, None], "ck_g": np.concatenate([f["c_k_norm_g"][0]] * 2)[:, None],
        "dt_bias": rep(f["gdn_dt_bias"][0]), "a_log": rep(f["gdn_a_log"][0]),
        "a_re": both(f["s5_a_re"][0]), "a_im": both(f["s5_a_im"][0]),
        "log_dt": both(np.broadcast_to(f["s5_log_dt"][0][:, None], (S5_G, S5_P))),
        "eps": ones * EPS, "half_pi": ones * (TWO_PI / 4), "sgn": sgn, "one": ones, "nsgn": -sgn,
    }
    par = np.empty((P, N_PAR), np.float32)
    for name, (at, n) in PAR.items():
        par[:, at:at + n] = parts[name]
    j, t = np.meshgrid(np.arange(P), np.arange(P), indexing="ij")
    same = (j // CHUNK) == (t // CHUNK)
    con = {"ident": j == t, "inc": same & (j <= t), "neg": np.where(same & (j <= t), 0.0, -1e30),
           "same": same, "first": j < CHUNK, "second": j >= CHUNK}
    for l in range(1, 7):
        s = 2 ** (l - 1)
        con[f"m{l}"] = (j // (2 * s) == t // (2 * s)) & (t % (2 * s) >= s) & (j % (2 * s) < s)
    con = np.concatenate([np.asarray(con[n], np.float32) for n in CON], 1)
    bt = [f[n][0].transpose(1, 0, 2) for n in ("s5_b_re", "s5_b_im")]
    ct = [f[n][0].transpose(2, 0, 1) for n in ("s5_c_re", "s5_c_im")]
    cg = [f[n][0].reshape(S5_GP, 2, S5_CH, S5_P).transpose(1, 3, 0, 2).reshape(P, -1) for n in ("s5_c_re", "s5_c_im")]
    s5_bc = np.concatenate([np.concatenate([bt[0], bt[1]], 0).reshape(P, -1), np.concatenate([bt[1], bt[0]], 0).reshape(P, -1),
                            np.concatenate([ct[0], ct[1]], 0).reshape(P, -1), cg[0], cg[1]], 1)
    rel = f["c_rel_bias"][0][:, np.clip(BAND_W - 1 - np.arange(BAND_E), -REL, REL) + REL]
    return {
        "x": f["x"][0], "mem": f["mem"][0], "par": par, "con": con, "s5_bc": s5_bc, "rel_rows": rel,
        "ab_w_in": f["ab_w_in"][0], "ab_w_out": f["ab_w_out"][0], "s5_w_glu": f["s5_w_glu"][0],
        "c_w_qkv": f["c_w_qkv"][0], "c_w_out": f["c_w_out"][0],
        "xa_w_q": f["xa_w_q"], "xa_w_kv": f["xa_w_kv"], "xa_w_out": f["xa_w_out"],
        "f_w_gate": f["f_w_gate"], "f_w_up": f["f_w_up"], "f_w_down": f["f_w_down"],
    }


def kernel(**inputs):
    import numpy as np
    import concourse.bacc as bacc
    from concourse.bass_utils import run_bass_kernel_spmd

    nc = bacc.Bacc("TRN2", target_bir_lowering=False, num_devices=1)
    arrays = {f"in_{k}": np.ascontiguousarray(v) for k, v in _layout(inputs).items()}
    A = {k[3:]: nc.dram_tensor(k, v.shape, mybir.dt.from_np(v.dtype), kind="ExternalInput").ap() for k, v in arrays.items()}
    A["out"] = nc.dram_tensor("out_0", (SEQ, D), F32, kind="ExternalOutput").ap()
    build_program(nc, A)
    r = run_bass_kernel_spmd(nc, [arrays], core_ids=[0])
    return r.results[0]["out_0"].reshape(1, SEQ, D)
```
